# Optimizing a Trainium2 kernel written in Bass

```python
import jax, jax.numpy as jnp
from jax import lax
import numpy as np

D_MODEL = 1024
BATCH = 1
SEQ = 512
DEPTH = 2

N_MIXERS = 2
S5_GROUP = 16
S5_GROUPS = D_MODEL // S5_GROUP
S5_STATE = 64
S5_CHUNK = 128
DT_MIN = 1e-3
DT_MAX = 1e-1
FOX_HEADS = 16
FOX_HEAD_DIM = D_MODEL // FOX_HEADS
Q_BLOCK = 128
FGATE_B_LO = 2.0
FGATE_B_HI = 6.0
D_FF = 2816
CONV_W = 3
EPS = 1e-6
N_S5 = (DEPTH + 1) // 2
N_FOX = DEPTH // 2


def rmsnorm(x, g):
    x32 = x.astype(jnp.float32)
    y = x32 * lax.rsqrt(jnp.mean(x32 * x32, axis=-1, keepdims=True) + EPS)
    return (y * g.astype(jnp.float32)).astype(x.dtype)

def adaln_params(c, w, b):
    mod = jax.nn.silu(c) @ w + b
    shift, scale, gate = jnp.split(mod, 3, axis=-1)
    return shift[:, None, :], scale[:, None, :], gate[:, None, :]

def modulate(x, g, shift, scale):
    return rmsnorm(x, g) * (1.0 + scale) + shift

def s5_mixer(h, w_in, lam_re, lam_im, log_dt, b_re, b_im, c_re, c_im, d_skip, w_glu, w_out):
    f32 = jnp.float32
    Bsz, S, _ = h.shape
    u = h @ w_in
    ug = u.reshape(Bsz, S, S5_GROUPS, S5_GROUP)
    lre = lam_re.astype(f32)
    lim = lam_im.astype(f32)
    dt = jnp.exp(log_dt.astype(f32))[:, None]
    mag = jnp.exp(lre * dt)
    lb_re = mag * jnp.cos(lim * dt)
    lb_im = mag * jnp.sin(lim * dt)
    num_re = lb_re - 1.0
    den = lre * lre + lim * lim
    k_re = (num_re * lre + lb_im * lim) / den
    k_im = (lb_im * lre - num_re * lim) / den
    br = b_re.astype(f32)
    bi = b_im.astype(f32)
    bb_re = k_re[..., None] * br - k_im[..., None] * bi
    bb_im = k_re[..., None] * bi + k_im[..., None] * br
    cr = c_re.astype(f32)
    ci = c_im.astype(f32)

    def combine(left, right):
        a1r, a1i, b1r, b1i = left
        a2r, a2i, b2r, b2i = right
        ar = a2r * a1r - a2i * a1i
        ai = a2r * a1i + a2i * a1r
        b_r = a2r * b1r - a2i * b1i + b2r
        b_i = a2r * b1i + a2i * b1r + b2i
        return ar, ai, b_r, b_i

    def chunk_step(carry, u_c):
        h_re, h_im = carry
        bu_re = jnp.einsum('blgc,gpc->blgp', u_c, bb_re)
        bu_im = jnp.einsum('blgc,gpc->blgp', u_c, bb_im)
        bu_re = bu_re.at[:, 0].add(lb_re * h_re - lb_im * h_im)
        bu_im = bu_im.at[:, 0].add(lb_re * h_im + lb_im * h_re)
        a_re = jnp.broadcast_to(lb_re, bu_re.shape)
        a_im = jnp.broadcast_to(lb_im, bu_im.shape)
        _, _, hs_re, hs_im = lax.associative_scan(combine, (a_re, a_im, bu_re, bu_im), axis=1)
        y = jnp.einsum('blgp,gcp->blgc', hs_re, cr) - jnp.einsum('blgp,gcp->blgc', hs_im, ci)
        return (hs_re[:, -1], hs_im[:, -1]), y

    n_chunks = S // S5_CHUNK
    u_chunks = ug.reshape(Bsz, n_chunks, S5_CHUNK, S5_GROUPS, S5_GROUP).transpose(1, 0, 2, 3, 4)
    h0 = (jnp.zeros((Bsz, S5_GROUPS, S5_STATE), f32), jnp.zeros((Bsz, S5_GROUPS, S5_STATE), f32))
    _, ys = lax.scan(chunk_step, h0, u_chunks)
    y = ys.transpose(1, 0, 2, 3, 4).reshape(Bsz, S, D_MODEL)
    y = y + d_skip.astype(f32) * u.astype(f32)
    y = jax.nn.gelu(y)
    y = y * jax.nn.sigmoid(y @ w_glu.astype(f32))
    return (y @ w_out.astype(f32)).astype(h.dtype)

def fox_mixer(h, w_in, b_f, w_out):
    f32 = jnp.float32
    Bsz, S, _ = h.shape
    proj = h @ w_in
    q = proj[..., :D_MODEL].reshape(Bsz, S, FOX_HEADS, FOX_HEAD_DIM) * (FOX_HEAD_DIM ** -0.5)
    k = proj[..., D_MODEL:2 * D_MODEL].reshape(Bsz, S, FOX_HEADS, FOX_HEAD_DIM)
    v = proj[..., 2 * D_MODEL:3 * D_MODEL].reshape(Bsz, S, FOX_HEADS, FOX_HEAD_DIM)
    f_logit = proj[..., 3 * D_MODEL:]
    log_f = jax.nn.log_sigmoid((f_logit + b_f).astype(f32))
    F = lax.cumsum(log_f, axis=1).transpose(0, 2, 1)
    n_q = S // Q_BLOCK
    q_blocks = q.reshape(Bsz, n_q, Q_BLOCK, FOX_HEADS, FOX_HEAD_DIM).transpose(1, 0, 3, 2, 4)
    F_blocks = F.reshape(Bsz, FOX_HEADS, n_q, Q_BLOCK).transpose(2, 0, 1, 3)
    k_pos = jnp.arange(S)

    def attend_block(args):
        qi, q_blk, Fq = args
        s = jnp.einsum('bhqd,bshd->bhqs', q_blk, k).astype(f32)
        s = s + Fq[..., None] - F[:, :, None, :]
        q_pos = qi * Q_BLOCK + jnp.arange(Q_BLOCK)
        causal = k_pos[None, :] <= q_pos[:, None]
        s = jnp.where(causal, s, -jnp.inf)
        p = jax.nn.softmax(s, axis=-1)
        return jnp.einsum('bhqs,bshd->bqhd', p.astype(v.dtype), v)

    o = lax.map(attend_block, (jnp.arange(n_q), q_blocks, F_blocks))
    o = o.transpose(1, 0, 2, 3, 4).reshape(Bsz, S, D_MODEL)
    return o @ w_out

def conv_ffn(h, w_up, conv_w, conv_b, w_down):
    up = h @ w_up
    a, b = jnp.split(up, 2, axis=-1)
    S = a.shape[1]
    ap = jnp.pad(a, ((0, 0), (CONV_W - 1, 0), (0, 0)))
    a_conv = conv_b
    for i in range(CONV_W):
        a_conv = a_conv + ap[:, i:i + S] * conv_w[i]
    return (jax.nn.silu(a_conv) * b) @ w_down

def first_inputs(seed: int = 0) -> dict:
    key = jax.random.key(seed)
    ks = jax.random.split(key, 32)
    f32 = jnp.float32
    D, G, P, Cg, H, F = D_MODEL, S5_GROUPS, S5_STATE, S5_GROUP, FOX_HEADS, D_FF
    nrm = lambda k, shape, s: jax.random.normal(k, shape, f32) * s
    x = nrm(ks[0], (BATCH, SEQ, D), 1.0)
    c = nrm(ks[1], (BATCH, D), 1.0)
    norm_g = 1.0 + nrm(ks[2], (DEPTH, 2, D), 0.01)
    ada_w = nrm(ks[3], (DEPTH, 2, D, 3 * D), 0.5 * D ** -0.5)
    ada_b = nrm(ks[4], (DEPTH, 2, 3 * D), 0.01)
    s5_w_in = nrm(ks[5], (N_S5, D, D), D ** -0.5)
    s5_lam_re = -0.5 + nrm(ks[6], (N_S5, G, P), 0.01)
    s5_lam_im = jnp.pi * jnp.arange(P, dtype=f32) + nrm(ks[7], (N_S5, G, P), 0.01)
    s5_log_dt = jax.random.uniform(ks[8], (N_S5, G), f32, np.log(DT_MIN), np.log(DT_MAX))
    s5_b_re = nrm(ks[9], (N_S5, G, P, Cg), (2.0 * Cg) ** -0.5)
    s5_b_im = nrm(ks[10], (N_S5, G, P, Cg), (2.0 * Cg) ** -0.5)
    s5_c_re = nrm(ks[11], (N_S5, G, Cg, P), (2.0 * P) ** -0.5)
    s5_c_im = nrm(ks[12], (N_S5, G, Cg, P), (2.0 * P) ** -0.5)
    s5_d = nrm(ks[13], (N_S5, D), 1.0)
    s5_w_glu = nrm(ks[14], (N_S5, D, D), D ** -0.5)
    s5_w_out = nrm(ks[15], (N_S5, D, D), D ** -0.5)
    fox_w_in = nrm(ks[16], (N_FOX, D, 3 * D + H), D ** -0.5)
    fox_b_f = jax.random.uniform(ks[17], (N_FOX, H), f32, FGATE_B_LO, FGATE_B_HI)
    fox_w_out = nrm(ks[18], (N_FOX, D, D), D ** -0.5)
    ffn_w_up = nrm(ks[19], (DEPTH, D, 2 * F), D ** -0.5)
    ffn_conv_w = nrm(ks[20], (DEPTH, CONV_W, F), CONV_W ** -0.5)
    ffn_conv_b = nrm(ks[21], (DEPTH, F), 0.01)
    ffn_w_down = nrm(ks[22], (DEPTH, F, D), F ** -0.5)
    final_g = 1.0 + nrm(ks[23], (D,), 0.01)
    return {"x": x, "c": c, "norm_g": norm_g, "ada_w": ada_w, "ada_b": ada_b,
            "s5_w_in": s5_w_in, "s5_lam_re": s5_lam_re, "s5_lam_im": s5_lam_im,
            "s5_log_dt": s5_log_dt, "s5_b_re": s5_b_re, "s5_b_im": s5_b_im,
            "s5_c_re": s5_c_re, "s5_c_im": s5_c_im, "s5_d": s5_d,
            "s5_w_glu": s5_w_glu, "s5_w_out": s5_w_out,
            "fox_w_in": fox_w_in, "fox_b_f": fox_b_f, "fox_w_out": fox_w_out,
            "ffn_w_up": ffn_w_up, "ffn_conv_w": ffn_conv_w, "ffn_conv_b": ffn_conv_b,
            "ffn_w_down": ffn_w_down, "final_g": final_g}

def first_block(x, c, norm_g, ada_w, ada_b,
              s5_w_in, s5_lam_re, s5_lam_im, s5_log_dt, s5_b_re, s5_b_im,
              s5_c_re, s5_c_im, s5_d, s5_w_glu, s5_w_out,
              fox_w_in, fox_b_f, fox_w_out,
              ffn_w_up, ffn_conv_w, ffn_conv_b, ffn_w_down, final_g):
    h = x
    for i in range(DEPTH):
        j = i // N_MIXERS
        shift, scale, gate = adaln_params(c, ada_w[i, 0], ada_b[i, 0])
        hn = modulate(h, norm_g[i, 0], shift, scale)
        if i % N_MIXERS == 0:
            m = s5_mixer(hn, s5_w_in[j], s5_lam_re[j], s5_lam_im[j], s5_log_dt[j],
                         s5_b_re[j], s5_b_im[j], s5_c_re[j], s5_c_im[j], s5_d[j],
                         s5_w_glu[j], s5_w_out[j])
        else:
            m = fox_mixer(hn, fox_w_in[j], fox_b_f[j], fox_w_out[j])
        h = (h + gate * m).astype(x.dtype)
        shift, scale, gate = adaln_params(c, ada_w[i, 1], ada_b[i, 1])
        hn = modulate(h, norm_g[i, 1], shift, scale)
        f = conv_ffn(hn, ffn_w_up[i], ffn_conv_w[i], ffn_conv_b[i], ffn_w_down[i])
        h = (h + gate * f).astype(x.dtype)
    return rmsnorm(h, final_g)


DEPTH_2 = 1

CHUNK = 64

SB_HEADS = 8
SB_HEAD_DIM = 64
SB_WIDTH = SB_HEADS * SB_HEAD_DIM

MLA_HEADS = 8
MLA_NOPE_DIM = 64
MLA_ROPE_DIM = 32
MLA_V_DIM = 64
MLA_Q_LORA = 384
MLA_KV_LORA = 256
MLA_QK_DIM = MLA_NOPE_DIM + MLA_ROPE_DIM
MLA_WIDTH = MLA_HEADS * MLA_V_DIM
ROPE_THETA = 10000.0

N_BRANCH = 2
IN_SPLIT_SIZES = (SB_WIDTH, SB_WIDTH, SB_WIDTH, SB_WIDTH,
                  MLA_Q_LORA, MLA_KV_LORA, MLA_ROPE_DIM, MLA_WIDTH,
                  N_BRANCH * D_MODEL)
IN_COLS = sum(IN_SPLIT_SIZES)


def rmsnorm_2(x, g):
    x32 = x.astype(jnp.float32)
    inv = lax.rsqrt(jnp.mean(x32 * x32, axis=-1, keepdims=True) + EPS)
    return (x32 * inv).astype(x.dtype) * g

def rope_tables(seq_len):
    half = MLA_ROPE_DIM // 2
    inv_freq = ROPE_THETA ** (-jnp.arange(half, dtype=jnp.float32) / half)
    ang = jnp.arange(seq_len, dtype=jnp.float32)[:, None] * inv_freq[None, :]
    return jnp.cos(ang), jnp.sin(ang)

def apply_rope(x, cos, sin):
    half = x.shape[-1] // 2
    x32 = x.astype(jnp.float32)
    x1, x2 = x32[..., :half], x32[..., half:]
    c, s = cos[None, :, None, :], sin[None, :, None, :]
    return jnp.concatenate([x1 * c - x2 * s, x1 * s + x2 * c], axis=-1).astype(x.dtype)

def to_query_blocks(q):
    b, s, h, d = q.shape
    return q.reshape(b, s // Q_BLOCK, Q_BLOCK, h, d).transpose(1, 0, 3, 2, 4)

def from_query_blocks(o):
    nb, b, h, qb, d = o.shape
    return o.transpose(1, 0, 3, 2, 4).reshape(b, nb * qb, h, d)

def stick_breaking_attention(q, k, v):
    seq_len = q.shape[1]
    scale = q.shape[-1] ** -0.5
    key_pos = jnp.arange(seq_len)
    qb = to_query_blocks(q)

    def block(args):
        q_blk, i = args
        q_pos = i * Q_BLOCK + jnp.arange(Q_BLOCK)
        z = jnp.einsum("bhqd,bshd->bhqs", q_blk, k).astype(jnp.float32) * scale
        strict = key_pos[None, :] < q_pos[:, None]
        log_beta = jax.nn.log_sigmoid(z)
        log_1m = jnp.where(strict, jax.nn.log_sigmoid(-z), 0.0)
        later = lax.cumsum(log_1m, axis=3, reverse=True) - log_1m
        w = jnp.where(strict, jnp.exp(log_beta + later), 0.0)
        return jnp.einsum("bhqs,bshd->bhqd", w.astype(v.dtype), v)

    o = lax.map(block, (qb, jnp.arange(qb.shape[0])))
    return from_query_blocks(o)

def chunk_causal_softmax_attention(q, k, v):
    seq_len = q.shape[1]
    scale = q.shape[-1] ** -0.5
    key_chunk = jnp.arange(seq_len) // CHUNK
    qb = to_query_blocks(q)

    def block(args):
        q_blk, i = args
        q_chunk = (i * Q_BLOCK + jnp.arange(Q_BLOCK)) // CHUNK
        allowed = key_chunk[None, :] <= q_chunk[:, None]
        z = jnp.einsum("bhqd,bshd->bhqs", q_blk, k).astype(jnp.float32) * scale
        p = jax.nn.softmax(jnp.where(allowed, z, -jnp.inf), axis=-1)
        return jnp.einsum("bhqs,bshd->bhqd", p.astype(v.dtype), v)

    o = lax.map(block, (qb, jnp.arange(qb.shape[0])))
    return from_query_blocks(o)

def second_inputs(seed: int = 0) -> dict:
    key = jax.random.key(seed)
    ks = jax.random.split(key, 16)
    f32 = jnp.float32

    def nrm(k, shape, fan_in):
        return jax.random.normal(k, shape, f32) * (fan_in ** -0.5)

    def gain(k, n):
        return 1.0 + 0.01 * jax.random.normal(k, (DEPTH_2, n), f32)

    return {
        "x": jax.random.normal(ks[0], (BATCH, SEQ, D_MODEL), f32),
        "norm_in_g": gain(ks[1], D_MODEL),
        "w_in": nrm(ks[2], (DEPTH_2, D_MODEL, IN_COLS), D_MODEL),
        "b_gate": 0.1 * jax.random.normal(ks[3], (DEPTH_2, N_BRANCH * D_MODEL), f32),
        "q_norm_g": gain(ks[4], MLA_Q_LORA),
        "w_q_up": nrm(ks[5], (DEPTH_2, MLA_Q_LORA, MLA_HEADS * MLA_QK_DIM), MLA_Q_LORA),
        "kv_norm_g": gain(ks[6], MLA_KV_LORA),
        "w_kv_up": nrm(ks[7], (DEPTH_2, MLA_KV_LORA, MLA_HEADS * (MLA_NOPE_DIM + MLA_V_DIM)), MLA_KV_LORA),
        "w_o_sb": nrm(ks[8], (DEPTH_2, SB_WIDTH, D_MODEL), SB_WIDTH),
        "w_o_mla": nrm(ks[9], (DEPTH_2, MLA_WIDTH, D_MODEL), MLA_WIDTH),
        "w_out": nrm(ks[10], (DEPTH_2, D_MODEL, D_MODEL), D_MODEL),
        "norm_f_g": 1.0 + 0.01 * jax.random.normal(ks[11], (D_MODEL,), f32),
    }

def second_block(x, norm_in_g, w_in, b_gate, q_norm_g, w_q_up, kv_norm_g, w_kv_up,
              w_o_sb, w_o_mla, w_out, norm_f_g):
    b, s, _ = x.shape
    cos, sin = rope_tables(s)
    offsets = [int(o) for o in np.cumsum(IN_SPLIT_SIZES)[:-1]]

    for l in range(DEPTH_2):
        h = rmsnorm_2(x, norm_in_g[l])
        proj = jnp.einsum("bsd,de->bse", h, w_in[l])
        (q_sb, k_sb, v_sb, gate_sb, c_q, c_kv, k_rope,
         gate_mla, gate_logits) = jnp.split(proj, offsets, axis=-1)

        o_sb = stick_breaking_attention(
            q_sb.reshape(b, s, SB_HEADS, SB_HEAD_DIM),
            k_sb.reshape(b, s, SB_HEADS, SB_HEAD_DIM),
            v_sb.reshape(b, s, SB_HEADS, SB_HEAD_DIM)).reshape(b, s, SB_WIDTH)
        y_sb = jnp.einsum("bsc,cd->bsd", o_sb * jax.nn.silu(gate_sb), w_o_sb[l])

        q = jnp.einsum("bsr,re->bse", rmsnorm_2(c_q, q_norm_g[l]), w_q_up[l])
        q = q.reshape(b, s, MLA_HEADS, MLA_QK_DIM)
        q_nope, q_rope = q[..., :MLA_NOPE_DIM], q[..., MLA_NOPE_DIM:]
        q_rope = apply_rope(q_rope, cos, sin)
        kv = jnp.einsum("bsr,re->bse", rmsnorm_2(c_kv, kv_norm_g[l]), w_kv_up[l])
        kv = kv.reshape(b, s, MLA_HEADS, MLA_NOPE_DIM + MLA_V_DIM)
        k_nope, v_mla = kv[..., :MLA_NOPE_DIM], kv[..., MLA_NOPE_DIM:]
        k_rope = apply_rope(k_rope[:, :, None, :], cos, sin)
        q_full = jnp.concatenate([q_nope, q_rope], axis=-1)
        k_full = jnp.concatenate(
            [k_nope, jnp.broadcast_to(k_rope, (b, s, MLA_HEADS, MLA_ROPE_DIM))], axis=-1)
        o_mla = chunk_causal_softmax_attention(q_full, k_full, v_mla).reshape(b, s, MLA_WIDTH)
        y_mla = jnp.einsum("bsc,cd->bsd", o_mla * jax.nn.silu(gate_mla), w_o_mla[l])

        g = jax.nn.sigmoid(gate_logits + b_gate[l]).reshape(b, s, N_BRANCH, D_MODEL)
        merged = g[:, :, 0, :] * y_sb + g[:, :, 1, :] * y_mla
        x = x + jnp.einsum("bsd,de->bse", merged, w_out[l])

    return rmsnorm_2(x, norm_f_g)


def setup_inputs(seed=0):
    out = dict(first_inputs(seed))
    for name, value in second_inputs(seed + 1).items():
        if name != "x":
            out[name + "_2"] = value
    return out


def reference(
    x, c, norm_g, ada_w, ada_b, s5_w_in, s5_lam_re, s5_lam_im, s5_log_dt, s5_b_re, s5_b_im,
    s5_c_re, s5_c_im, s5_d, s5_w_glu, s5_w_out, fox_w_in, fox_b_f, fox_w_out, ffn_w_up,
    ffn_conv_w, ffn_conv_b, ffn_w_down, final_g, norm_in_g_2, w_in_2, b_gate_2, q_norm_g_2,
    w_q_up_2, kv_norm_g_2, w_kv_up_2, w_o_sb_2, w_o_mla_2, w_out_2, norm_f_g_2,
):
    x = first_block(
        x, c, norm_g, ada_w, ada_b, s5_w_in, s5_lam_re, s5_lam_im, s5_log_dt, s5_b_re, s5_b_im,
        s5_c_re, s5_c_im, s5_d, s5_w_glu, s5_w_out, fox_w_in, fox_b_f, fox_w_out, ffn_w_up,
        ffn_conv_w, ffn_conv_b, ffn_w_down, final_g,
    )
    return second_block(
        x, norm_in_g_2, w_in_2, b_gate_2, q_norm_g_2, w_q_up_2, kv_norm_g_2, w_kv_up_2,
        w_o_sb_2, w_o_mla_2, w_out_2, norm_f_g_2,
    )


_drawn_inputs = setup_inputs


def setup_inputs(seed=0):
    import zlib

    import numpy as np

    out = dict(_drawn_inputs(seed))
    spreads = {}
    factors = {'norm_g': 8.0,
     'ada_b': 3.921,
     's5_lam_re': 64.0,
     's5_lam_im': 49.04,
     's5_log_dt': 57.496,
     's5_b_re': 64.0,
     's5_b_im': 64.0,
     's5_c_re': 64.0,
     's5_c_im': 64.0,
     'ffn_conv_b': 8.0,
     'final_g': 5.625,
     'norm_in_g_2': 8.0,
     'b_gate_2': 6.868,
     'q_norm_g_2': 8.0,
     'kv_norm_g_2': 8.0,
     'norm_f_g_2': 28.286}
    for name, (base, spread) in spreads.items():
        noise = np.random.default_rng([zlib.crc32(name.encode()), seed]).standard_normal(out[name].shape)
        drawn = base * np.exp(spread * noise) if base else spread * noise
        out[name] = __import__('jax').numpy.asarray(drawn.astype(out[name].dtype))
    for name, factor in factors.items():
        out[name] = (out[name] * factor).astype(out[name].dtype)
    return out
```

```python
from contextlib import ExitStack

import numpy as np
import concourse.bass as bass
from concourse import mybir

F32 = mybir.dt.float32
F32R = mybir.dt.float32r
ALU = mybir.AluOpType
ACT = mybir.ActivationFunctionType
AX = mybir.AxisListType

P = 128
S = 512
D = 1024
DT = D // P
EPS = 1e-6
NEG = -1e30

FT = 2816 // P
HALVES = (12, 10)
GRP, CG, ST = 64, 16, 64
GP = GRP // 2
TC = 4
NCK = S // TC
HEADS, HD = 16, 64
H2 = 8
ROPE, QK = 32, 96
QL, KVL = 384, 256
QBLK = S // P

LAYERS = [("s5_in", 8, 256, 4), ("s5_glu", 8, 256, 4), ("s5_out", 8, 256, 4)]
for _l in (0, 1):
    if _l == 1:
        LAYERS += [("fox_q", 8, 256, 4), ("fox_k", 8, 256, 4), ("fox_v", 8, 256, 4), ("fox_out", 8, 256, 4)]
    for _h, _n in enumerate(HALVES):
        LAYERS += [(f"up{_l}{_h}", 8, 256, _n), (f"down{_l}{_h}", _n, 128, 8)]
LAYERS += [("sb_q", 8, 256, 2), ("sb_k", 8, 256, 2), ("sb_v", 8, 256, 2), ("mla_c", 8, 256, 3),
           ("mla_q", 3, 256, 4), ("mla_k", 2, 256, 2), ("mla_v", 2, 256, 2),
           ("gate_sb", 8, 256, 2), ("gate_mla", 8, 256, 2)]
for _m in range(4):
    LAYERS += [(f"g0_{_m}", 8, 256, 1), (f"osb_{_m}", 4, 256, 1), (f"g1_{_m}", 8, 256, 1), (f"omla_{_m}", 4, 256, 1)]
LAYERS += [("mix_out", 8, 256, 4)]
FIRST, OFFSET, KT, COLS, COUNT = {}, {}, {}, {}, {}
_n = _o = 0
for _name, _kt, _c, _cnt in LAYERS:
    FIRST[_name], OFFSET[_name], KT[_name], COLS[_name], COUNT[_name] = _n, _o, _kt, _c, _cnt
    _n += _cnt
    _o += _cnt * P * _kt * _c
N_CHUNKS, W_WORDS = _n, _o
CREDIT = 2

PCOL = {}
_n = 0
for _name, _w in (("norm_g", 32), ("ada_b", 96), ("s5_d", 8), ("final_g", 8), ("norm_in_g", 8), ("b_gate", 16),
                  ("q_norm_g", 3), ("kv_norm_g", 2), ("norm_f_g", 8), ("conv_w", 6 * FT), ("conv_b", 2 * FT), ("fox_b", 1)):
    PCOL[_name] = _n
    _n += _w
N_PCOL = _n

NORMS = [("mix0", 8), ("ffn0", 8), ("mix1", 8), ("ffn1", 8), ("final", 8), ("in2", 8), ("cq", 3), ("ckv", 2), ("out", 8)]
NIDX = {n: i for i, (n, _) in enumerate(NORMS)}
NTILE = {n: sum(t for _, t in NORMS[:i]) for i, (n, _) in enumerate(NORMS)}
SSQ = {n: sum(t + 1 for _, t in NORMS[:i]) + 1 for i, (n, _) in enumerate(NORMS)}
SQ = {n: sum(t for _, t in NORMS[:i]) for i, (n, _) in enumerate(NORMS)}


def done_value(j, r):
    return j * 2 + (CREDIT + r + 1)


def row(t, m):
    return t[:, m] if isinstance(m, int) else t[:, bass.ds(m, 1)].rearrange("p o n -> p (o n)")


def col(t, m):
    return t[:, m:m + 1] if isinstance(m, int) else t[:, bass.ds(m, 1)]


def build(nc, weights, ada_w, xT, c, params, consts, rope, s5p, s5bc, fox_f, out):
    with ExitStack() as ctx:
        build_in(ctx, nc, weights, ada_w, xT, c, params, consts, rope, s5p, s5bc, fox_f, out)



XTILE = {n: sum(t for m, t in NORMS[:i] if m not in ("final", "out")) for i, (n, _) in enumerate(NORMS)}
UNIT = {"fox": 0, "sb": 4 * HEADS, "mla": 4 * HEADS + 4 * H2}
GATED = {"s5_glu": 0, "gate_sb": 8, "gate_mla": 12}


def build_in(ctx, nc, weights, ada_w, xT, c, params, consts, rope, s5p, s5bc, fox_f, out):
    place = [16512]

    def sb(name, shape, dt=F32):
        t = nc.alloc_sbuf_tensor_at(name, shape, dt, offset=place[0])
        place[0] += (int(np.prod(shape[1:])) * 4 + 31) // 32 * 32
        return t

    def sem(name):
        return ctx.enter_context(nc.semaphore(name))

    h = sb("h", [P, DT, S])
    xn_at = place[0]
    xn_hi, xn_lo = sb("xn_hi", [P, DT, S], F32R), sb("xn_lo", [P, DT, S], F32R)
    raw, w_hi, w_lo = sb("raw", [P, 2, 2048]), sb("w_hi", [P, 2, 2048], F32R), sb("w_lo", [P, 2, 2048], F32R)
    ada_at = place[0]
    adaw = sb("adaw", [P, 2, D])
    cvec = sb("cvec", [P, D])
    cst = sb("cst", [P, 4, P])
    par = sb("par", [P, N_PCOL])
    mod = sb("mod", [P, 4, 24])
    gain = sb("gain", [P, 4, DT])
    ones = sb("ones", [P, P])
    rstd, ssq = sb("rstd", [P, S]), sb("ssq", [P, S])
    sq, nt, hn = sb("sq", [P, 2, S]), sb("nt", [P, 2, S]), sb("hn", [P, 2, S])
    stat = sb("stat", [P, 4, 4])
    coef = sb("coef", [P, 2, 2, GP])
    epsc, adat = sb("epsc", [P, 1]), sb("adat", [P, 2])
    arena = place[0]
    causal, strict, chunkm = (cst[:, i, :] for i in (1, 2, 3))
    ident = cst[:, 0, :]

    def put(name, address, shape, dt=F32):
        assert address + int(np.prod(shape[1:])) * 4 <= 229344, (name, arena)
        return nc.alloc_sbuf_tensor_at(name, shape, dt, offset=address)

    def at(name, kib, shape, dt=F32):
        return put(name, arena + int(kib * 1024), shape, dt)

    BW, Bz, Kt = at("BW", 0, [P, 2, GP, TC, CG]), at("Bz", 16, [P, 2, GP, 2, CG]), at("Kt", 24, [P, GP, TC, CG])
    lam = put("lam", xn_at, [P, 3, GP])
    bc = put("bc", xn_at + 384, [P, 4, GP, CG])
    t5a, t5b = put("t5a", xn_at + 9 * 1024, [P, 2, GP, CG]), put("t5b", xn_at + 13 * 1024, [P, 2, GP, CG])
    q5 = put("q5", xn_at + 17 * 1024, [P, 32, GP])
    U, uT = at("U", 0, [P, GP, NCK]), at("uT", 16, [P, DT, TC, NCK])
    Mt, Bm, CL = at("Mt", 32, [P, GP, 64]), at("Bm", 40, [P, 2, GP, ST]), at("CL", 56, [P, 2, GP, 5, CG])
    X = put("X", xn_at, [P, NCK, 2, GP])
    Y, yT = at("Y", 0, [P, GP, NCK]), at("yT", 32, [P, DT, S])
    g32 = at("g32", 0, [P, DT, S])
    zg_hi, zg_lo = at("zg_hi", 16, [P, DT, S], F32R), at("zg_lo", 48, [P, DT, S], F32R)
    act_hi, act_lo = at("act_hi", 0, [P, 12, S], F32R), at("act_lo", 24, [P, 12, S], F32R)
    apad = [at(f"apad{r}", 48 + r * 2.0625, [P, S + 2]) for r in range(2)]
    cv, sil, prod = at("cv", 53, [P, 2, S]), at("sil", 57, [P, 2, S]), at("prod", 61, [P, 2, S])
    fq, fk, fv = at("fq", 0, [P, DT, S]), at("fk", 16, [P, DT, S]), at("fv", 32, [P, QBLK, D])
    fbias, fg, fwf = at("fbias", 48, [P, 2, S]), at("fg", 52, [HEADS, 4, S]), at("fwf", 60, [P, DT, HEADS])
    b_q, b_k, b_v = at("b_q", 0, [P, 4, S]), at("b_k", 8, [P, 4, S]), at("b_v", 16, [P, QBLK, S])
    o_sb, o_mla = at("o_sb", 24, [P, 4, S]), at("o_mla", 48, [P, 4, S])
    cc = at("cc", 32, [P, 5, S])
    cq_hi, cq_lo = at("cq_hi", 42, [P, 3, S], F32R), at("cq_lo", 48, [P, 3, S], F32R)
    ck_hi, ck_lo = at("ck_hi", 54, [P, 2, S], F32R), at("ck_lo", 58, [P, 2, S], F32R)
    kr, rt = at("kr", 62, [P, S]), at("rt", 66, [P, S])
    m_q, m_v, m_k = at("m_q", 0, [P, H2, S]), at("m_v", 16, [P, QBLK, S]), at("m_k", 32, [P, H2, S])
    ropt = put("ropt", ada_at, [P, S])
    osb_hi, osb_lo = at("osb_hi", 0, [P, 4, S], F32R), at("osb_lo", 8, [P, 4, S], F32R)
    omla_hi, omla_lo = at("omla_hi", 32, [P, 4, S], F32R), at("omla_lo", 40, [P, 4, S], F32R)
    mg_hi, mg_lo = at("mg_hi", 16, [P, DT, S], F32R), at("mg_lo", 56, [P, DT, S], F32R)
    fin = at("fin", 0, [P, DT, S])
    pw = at("pw", 68, [P, 3, S])
    pt = sq

    ps = ctx.enter_context(nc.psum_tensor("ps", [P, 8, S], F32))
    u_dram = nc.dram_tensor("u_dram", [D, S], F32).ap()
    y_dram = nc.dram_tensor("y_dram", [D, S], F32).ap()
    f_dram = nc.dram_tensor("f_dram", [HEADS, S], F32).ap()

    in_c, in_const, in_x, in_s5, in_fw = sem("in_c"), sem("in_const"), sem("in_x"), sem("in_s5"), sem("in_fw")
    in_rope = sem("in_rope")
    raw_in = [sem("raw_in0"), sem("raw_in1")]
    split_hi, split_lo = sem("split_hi"), sem("split_lo")
    done = [sem("done0"), sem("done1")]
    evac = [sem("evac0"), sem("evac1")]
    ada_in, ada_used, c_ready = [sem("ada_in0"), sem("ada_in1")], sem("ada_used"), sem("c_ready")
    mod_step, mod_copy = sem("mod_step"), sem("mod_copy")
    init = sem("init")
    sq_ready, ssq_ready, stat_done, std_ready = sem("sq_ready"), sem("ssq_ready"), sem("stat_done"), sem("std_ready")
    rstd_ready, norm_t, norm_h, xh, xl = sem("rstd_ready"), sem("norm_t"), sem("norm_h"), sem("xh"), sem("xl")
    s5_act, s5_arg, s5_step, bw_ready, cl_ready = sem("s5_act"), sem("s5_arg"), sem("s5_step"), sem("bw_ready"), sem("cl_ready")
    turned, turned_out, kt_done, kt_out, mt_in = sem("turned"), sem("turned_out"), sem("kt_done"), sem("kt_out"), sem("mt_in")
    u_saved, u_in, x_done, x_out, scan = sem("u_saved"), sem("u_in"), sem("x_done"), sem("x_out"), sem("scan")
    y_done, y_out, y_saved, y_in = sem("y_done"), sem("y_out"), sem("y_saved"), sem("y_in")
    z_done, g_done, gh_done, gl_done = sem("z_done"), sem("g_done"), sem("gh_done"), sem("gl_done")
    gm_prod, gm_hi, gm_lo = sem("gm_prod"), sem("gm_hi"), sem("gm_lo")
    pad_ready, cv_step, conv_done, silu_done = sem("pad_ready"), sem("cv_step"), sem("conv_done"), sem("silu_done")
    acth, actl = sem("acth"), sem("actl")
    f_done, f_dve, f_act, f_saved, bias_in = sem("f_done"), sem("f_dve"), sem("f_act"), sem("f_saved"), [sem("bias_in0"), sem("bias_in1")]
    s_done, s_free, mx_done, nm_done, exp_done, rc_done = (sem(n) for n in ("s_done", "s_free", "mx_done", "nm_done", "exp_done", "rc_done"))
    w_ready, tr_done, pt_done, pv_done, o_hi, o_done = (sem(n) for n in ("w_ready", "tr_done", "pt_done", "pv_done", "o_hi", "o_done"))
    a_step, ln_done, sp_done, sc_done = sem("a_step"), sem("ln_done"), sem("sp_done"), sem("sc_done")
    rope_t, kr_ready, mq_nope, mk_rope = sem("rope_t"), sem("kr_ready"), sem("mq_nope"), sem("mk_rope")
    mq_ready = sem("mq_ready")
    m_sum, m_hi, m_lo, out_saved = sem("m_sum"), sem("m_hi"), sem("m_lo"), sem("out_saved")

    def f32(ap):
        return ap.bitcast(F32)

    def pcol(name, i, p=slice(0, P)):
        return par[p, PCOL[name] + i:PCOL[name] + i + 1]

    def last_of(name):
        n = FIRST[name] + COUNT[name] - 1
        return n // 2, n % 2

    def size(n):
        for name, *_ in LAYERS:
            if FIRST[name] <= n < FIRST[name] + COUNT[name]:
                return KT[name] * COLS[name]

    def after_layer(eng, name, sems=evac):
        n = FIRST[name] + COUNT[name] - 1
        for m in (n, n - 1):
            eng.wait_ge(sems[m % 2], done_value(m // 2, 1))

    def s5_io(t):
        return t.rearrange("(g q c) (j k) -> q j c g k", q=2, c=CG, j=TC)

    def conv_par(l, tap, f):
        return PCOL["conv_w"] + (l * 3 + tap) * FT + f

    block = ctx.enter_context(nc.Block())

    @block.sync
    def _(sp):
        sp.dma_start(cst[:], consts).then_inc(in_const, 16)
        sp.dma_start(par[:], params).then_inc(in_const, 16)
        sp.dma_start(h[:], xT.rearrange("(m p) t -> p m t", p=P)).then_inc(in_x, 16)
        sp.dma_start(lam[:], s5p).then_inc(in_s5, 16)
        sp.dma_start(bc[:], s5bc).then_inc(in_s5, 16)
        at_chunk = [0]

        def chunk_source(name, i):
            words = KT[name] * COLS[name]
            all_of = weights[OFFSET[name]:OFFSET[name] + COUNT[name] * P * words]
            all_of = all_of.rearrange("(n p f) -> p n f", p=P, f=words)
            return row(all_of, i)

        def load(j, b, name, i):
            if not (isinstance(j, int) and j == 0):
                sp.wait_ge(split_lo, j * 2 + (b - 1))
            sp.dma_start(raw[:, b, 0:KT[name] * COLS[name]], chunk_source(name, i)).then_inc(raw_in[b], 16)

        def upto(name, count=None):
            stop = FIRST[name] + (COUNT[name] if count is None else count)
            for layer, *_ in LAYERS:
                n0, n1 = FIRST[layer], FIRST[layer] + COUNT[layer]
                if n1 <= at_chunk[0] or n0 >= stop:
                    continue
                if layer[:2] in ("up", "do") and n0 == at_chunk[0]:
                    with sp.Fori(0, COUNT[layer] // 2) as i:
                        for b in range(2):
                            load(i + n0 // 2, b, layer, i * 2 + b)
                    at_chunk[0] = n1
                    continue
                for n in range(max(n0, at_chunk[0]), min(n1, stop)):
                    load(n // 2, n % 2, layer, n - n0)
                    at_chunk[0] = n + 1

        upto("s5_in", 2)
        sp.wait_ge(kt_out, 4)
        sp.wait_ge(init, 2)
        for q in range(2):
            for i in range(TC):
                sp.dma_start(Mt[q * 64 + i * CG:q * 64 + (i + 1) * CG, :, i * CG:64],
                             Kt[q * CG:(q + 1) * CG, :, 0:TC - i, :].rearrange("p g d c -> p g (d c)")).then_inc(mt_in, 16)
        upto("s5_in")
        for n in range(4):
            sp.wait_ge(evac[n % 2], done_value(n // 2, 1))
            sp.dma_start(u_dram[n * 256:(n + 1) * 256, :].rearrange("(m p) t -> p m t", p=P),
                         uT[:, 2 * n:2 * n + 2].rearrange("p m j k -> p m (j k)")).then_inc(u_saved, 16)
            if n:
                upto("s5_glu", n)
        sp.wait_ge(u_saved, 64)
        for q in range(2):
            for j in range(TC):
                sp.dma_start(U[q * 64 + j * CG:q * 64 + (j + 1) * CG], s5_io(u_dram)[q, j]).then_inc(u_in, 16)
        sp.wait_ge(y_out, 8)
        for q in range(2):
            for j in range(TC):
                sp.dma_start(s5_io(y_dram)[q, j], Y[q * 64 + j * CG:q * 64 + (j + 1) * CG]).then_inc(y_saved, 16)
        sp.wait_ge(y_saved, 128)
        sp.dma_start(yT[:], y_dram.rearrange("(m p) t -> p m t", p=P)).then_inc(y_in, 16)
        upto("down01")
        upto("fox_q", 2)
        after_layer(sp, "down01")
        sp.dma_start(fwf[:], fox_f).then_inc(in_fw, 16)
        sp.wait_ge(f_dve, 3)
        sp.dma_start(f_dram, fg[:, 3]).then_inc(f_saved, 16)
        upto("fox_out", 3)
        sp.wait_ge(f_saved, 16)
        for hd in range(HEADS):
            if hd >= 2:
                sp.wait_ge(s_free, 4 * (hd - 1))
            sp.dma_start(fbias[:, hd % 2], f_dram[hd:hd + 1, :].to_broadcast([P, S])).then_inc(bias_in[hd % 2], 16)
        upto("mix_out")
        sp.wait_ge(norm_h, NTILE["out"] + 8)
        sp.dma_start(out.rearrange("(m p) t -> p m t", p=P), fin[:]).then_inc(out_saved, 16)
        sp.wait_ge(out_saved, 16)

    @block.gpsimd
    def _(pool):
        pool.dma_start(cvec[:], c.to_broadcast([P, D])).then_inc(in_c, 16)
        for b in range(2):
            pool.dma_start(adaw[:, b], ada_w[b]).then_inc(ada_in[b], 16)
        with pool.Fori(1, 48) as i:
            for b in range(2):
                pool.wait_ge(ada_used, i * 2 + (b - 1))
                pool.dma_start(adaw[:, b], row(ada_w.rearrange("n p k -> p n k"), i * 2 + b)).then_inc(ada_in[b], 16)
        pool.wait_ge(ada_used, 96)
        pool.dma_start(ropt[64:P, :], rope).then_inc(in_rope, 16)
        pool.wait_ge(kr_ready, 1)
        after_layer(pool, "mla_q")
        for hd in range(H2):
            nc.gpsimd.tensor_copy(m_k[64:QK, hd], kr[64:QK, :]).then_inc(mk_rope, 1)

    @block.tensor
    def _(pe):
        def three(bank, hi_w, lo_w, hi_x, lo_x, start, stop):
            pe.matmul(bank, lo_w, hi_x, start=start, stop=False)
            pe.matmul(bank, hi_w, lo_x, start=False, stop=False)
            return pe.matmul(bank, hi_w, hi_x, start=False, stop=stop)

        def chunk_ready(j, b):
            pe.wait_ge(split_lo, j * 2 + (b + 1))
            pe.wait_ge(evac[b], done_value(j, -1))

        def product(name, j, b, x_hi, x_lo, x_ready=None):
            chunk_ready(j, b)
            kt, cols = KT[name], COLS[name]
            for k in range(kt):
                if x_ready:
                    pe.wait_ge(x_ready[0], x_ready[1] + k + 1)
                for r in range(cols // P):
                    w = slice(k * cols + r * P, k * cols + (r + 1) * P)
                    mm = three(ps[:, 2 * b + r], w_hi[:, b, w], w_lo[:, b, w], x_hi[:, k], x_lo[:, k], k == 0, k == kt - 1)
                    if k == kt - 1:
                        mm.then_inc(done[b], 2 * P // cols)

        def product_rows(name, j, b, x_hi, x_lo):
            chunk_ready(j, b)
            kt = KT[name]
            for t in range(QBLK):
                for k in range(kt):
                    x = slice(t * P, (t + 1) * P)
                    w = slice(k * 256, (k + 1) * 256)
                    mm = three(ps[:, 2 * b + t // 2, (t % 2) * 256:(t % 2 + 1) * 256], x_hi[:, k, x], x_lo[:, k, x],
                               w_hi[:, b, w], w_lo[:, b, w], k == 0, k == kt - 1)
                if t % 2:
                    mm.then_inc(done[b], 1)

        def layer(name, x_hi, x_lo, x_ready=None, rows=False):
            for i in range(COUNT[name]):
                n = FIRST[name] + i
                if rows:
                    product_rows(name, n // 2, n % 2, x_hi, x_lo)
                else:
                    product(name, n // 2, n % 2, x_hi, x_lo, x_ready if i == 0 else None)

        def layer_loop(name, x_hi, x_lo):
            with pe.Fori(0, COUNT[name] // 2) as i:
                for b in range(2):
                    product(name, i + FIRST[name] // 2, b, x_hi, x_lo)

        def norm_stat(name):
            pe.wait_ge(ssq_ready, SSQ[name] + dict(NORMS)[name])
            if NIDX[name]:
                pe.wait_ge(std_ready, NIDX[name])
            pe.matmul(ps[:, 7], ones[:], ssq[:], start=True, stop=True).then_inc(stat_done, 1)

        def attention(kind, heads, q, k, v, rows, diag_mask):
            n = 4 * heads
            S_BANK, T_BANK, O_BANK = (4, 5, 6), (0, 3), (1, 2)

            def scores(u):
                g, hd, i = UNIT[kind] + u, u // 4, u % 4
                if g >= 3:
                    pe.wait_ge(s_free, g - 2)
                bank = ps[:, S_BANK[g % 3]]
                pe.matmul(bank[:, 0:(i + 1) * P], q(hd)[:, i * P:(i + 1) * P], k(hd)[:, 0:(i + 1) * P], start=True, stop=False)
                pe.matmul(bank[:, i * P:(i + 1) * P], ident, diag_mask, start=False, stop=True).then_inc(s_done, 1)

            def turn(u):
                g, i = UNIT[kind] + u, u % 4
                pe.wait_ge(w_ready, g + 1)
                if g >= 2:
                    pe.wait_ge(pt_done, g - 1)
                for t in range(i + 1):
                    mm = pe.transpose(ps[:, T_BANK[g % 2], t * P:(t + 1) * P], pw[:, g % 3, t * P:(t + 1) * P], ident)
                mm.then_inc(tr_done, 1)

            def weigh(u):
                g, hd, i = UNIT[kind] + u, u // 4, u % 4
                pe.wait_ge(pt_done, g + 1)
                if u % 8 == 0 and g // 8 >= 2:
                    pe.wait_ge(o_done, g // 8 - 1)
                half = hd % 2 * 64
                for t in range(i + 1):
                    mm = pe.matmul(ps[half:half + 64, O_BANK[g // 8 % 2], i * P:(i + 1) * P], v[:, t, hd * 64:(hd + 1) * 64],
                                   pt[:, g % 2, t * P:(t + 1) * P], start=t == 0, stop=t == i)
                mm.then_inc(pv_done, 1)

            for s in range(n + 3):
                if s < n:
                    scores(s)
                if 2 <= s < n + 2:
                    turn(s - 2)
                if s >= 3:
                    weigh(s - 3)

        for b in range(2):
            nc.tensor.sem_inc(done[b], CREDIT)
        pe.wait_ge(in_const, 32)
        pe.wait_ge(bw_ready, 1)
        for n in range(16):
            q, ri = n // 2, n % 2
            if n >= 4:
                pe.wait_ge(turned_out, n - 3)
            for g in range(4):
                mm = pe.transpose(ps[0:64, n % 4, g * P:(g + 1) * P], BW[:, ri, 4 * q + g].rearrange("p j c -> p (j c)"), ident)
            mm.then_inc(turned, 1)
        pe.wait_ge(cl_ready, 1)
        for q in range(4):
            if q == 3:
                pe.wait_ge(kt_out, 1)
            for g in range(8 * q, 8 * q + 8):
                for ri in range(2):
                    mm = pe.matmul(ps[0:32, 4 + q % 3, (g % 8) * 64:(g % 8 + 1) * 64], Bz[:, ri, g].rearrange("p q c -> p (q c)"),
                                   CL[:, ri, g, 0:TC].rearrange("p d c -> p (d c)"), start=ri == 0, stop=ri == 1)
            mm.then_inc(kt_done, 1)

        pe.wait_ge(init, 1)
        norm_stat("mix0")
        layer("s5_in", xn_hi, xn_lo, (xl, XTILE["mix0"]))

        after_layer(pe, "s5_in")
        pe.wait_ge(u_in, 128)
        pe.wait_ge(turned_out, 16)
        for n in range(16):
            q, ri = n // 2, n % 2
            if n >= 4:
                pe.wait_ge(x_out, n - 3)
            for g in range(4):
                for p in (slice(0, 64), slice(64, P)):
                    mm = pe.matmul(ps[p, n % 4, g * P:(g + 1) * P], Bm[p, ri, 4 * q + g], U[p, 4 * q + g], start=True, stop=True)
            mm.then_inc(x_done, 1)
        pe.wait_ge(x_out, 16)
        pe.wait_ge(mt_in, 128)
        pe.wait_ge(kt_out, 4)
        pe.wait_ge(std_ready, 1)
        for g in range(GP):
            for p in (slice(0, 64), slice(64, P)):
                pe.matmul(ps[p, g // 4, (g % 4) * P:(g % 4 + 1) * P], Mt[p, g], U[p, g], start=g % 4 == 0, stop=False,
                          skip_group_check=True)
        pe.wait_ge(scan, 4 * (NCK - 2) + 1)
        for g in range(GP):
            for p in (slice(0, 64), slice(64, P)):
                for ri in range(2):
                    mm = pe.matmul(ps[p, g // 4, (g % 4) * P + 1:(g % 4 + 1) * P], CL[p, ri, g, 1:5].rearrange("p d c -> p (d c)"),
                                   X[p, 0:NCK - 1, ri, g], start=False, stop=ri == 1, skip_group_check=True)
            if g % 4 == 3:
                mm.then_inc(y_done, 1)
        pe.wait_ge(y_out, 8)
        layer("s5_glu", xn_hi, xn_lo, (gl_done, 0))
        layer("s5_out", zg_hi, zg_lo, (gm_lo, 0))

        for l in (0, 1):
            if l:
                norm_stat("mix1")
                pe.wait_ge(xl, XTILE["mix1"] + 8)
                pe.wait_ge(in_fw, 16)
                for k in range(2 * DT):
                    x = (xn_hi, xn_lo)[k // DT]
                    mm = pe.matmul(ps[0:HEADS, 6], fwf[:, k % DT], f32(x[:, k % DT]), start=k == 0, stop=k == 2 * DT - 1)
                mm.then_inc(f_done, 1)
                layer("fox_q", xn_hi, xn_lo)
                layer("fox_k", xn_hi, xn_lo)
                layer("fox_v", xn_hi, xn_lo, rows=True)
                after_layer(pe, "fox_v")
                pe.wait_ge(f_dve, 1)
                attention("fox", HEADS, lambda hd: fq[hd % 2 * 64:hd % 2 * 64 + 64, hd // 2],
                          lambda hd: fk[hd % 2 * 64:hd % 2 * 64 + 64, hd // 2], fv, 64, causal)
                layer("fox_out", xn_hi, xn_lo, (o_done, 0))
            norm_stat(f"ffn{l}")
            tiles = sum(HALVES) * l
            pe.wait_ge(xl, XTILE[f"ffn{l}"] + 8)
            for hf, nf in enumerate(HALVES):
                layer_loop(f"up{l}{hf}", xn_hi, xn_lo)
                tiles += nf
                pe.wait_ge(actl, tiles)
                layer_loop(f"down{l}{hf}", act_hi, act_lo)

        norm_stat("final")
        norm_stat("in2")
        layer("sb_q", xn_hi, xn_lo, (xl, XTILE["in2"]))
        layer("sb_k", xn_hi, xn_lo)
        layer("sb_v", xn_hi, xn_lo, rows=True)
        after_layer(pe, "sb_v")
        attention("sb", H2, lambda hd: b_q[hd % 2 * 64:hd % 2 * 64 + 64, hd // 2],
                  lambda hd: b_k[hd % 2 * 64:hd % 2 * 64 + 64, hd // 2], b_v, 64, strict)
        pe.wait_ge(o_done, 12)
        layer("mla_c", xn_hi, xn_lo)
        norm_stat("cq")
        norm_stat("ckv")
        layer("mla_q", cq_hi, cq_lo, (xl, XTILE["cq"]))
        layer("mla_k", ck_hi, ck_lo, (xl, XTILE["ckv"]))
        layer("mla_v", ck_hi, ck_lo, rows=True)
        after_layer(pe, "mla_v")
        pe.wait_ge(mk_rope, H2)
        attention("mla", H2, lambda hd: m_q[0:QK, hd], lambda hd: m_k[0:QK, hd], m_v, QK, chunkm)
        pe.wait_ge(o_done, 16)
        layer("gate_sb", xn_hi, xn_lo)
        layer("gate_mla", xn_hi, xn_lo)
        for m in range(4):
            layer(f"g0_{m}", xn_hi, xn_lo)
            layer(f"osb_{m}", osb_hi, osb_lo, (gm_lo, GATED["gate_sb"]) if m == 0 else None)
            layer(f"g1_{m}", xn_hi, xn_lo)
            layer(f"omla_{m}", omla_hi, omla_lo, (gm_lo, GATED["gate_mla"]) if m == 0 else None)
        layer("mix_out", mg_hi, mg_lo, (m_lo, 0))
        norm_stat("out")

    @block.scalar
    def _(act):
        A = nc.scalar.activation

        def split(j, b, words=2048):
            act.wait_ge(raw_in[b], j * 16 + 16)
            act.wait_ge(done[b], done_value(j, -1))
            A(w_hi[:, b, 0:words], raw[:, b, 0:words], ACT.Copy).then_inc(split_hi, 1)

        def split_next(n):
            if n + 1 < N_CHUNKS:
                split((n + 1) // 2, (n + 1) % 2, size(n + 1))

        def layer(name, evacuate):
            for i in range(COUNT[name]):
                n = FIRST[name] + i
                split_next(n)
                evacuate(n // 2, n % 2, i)

        def copy_out(dst, scale=1.0):
            def evacuate(j, b, i):
                for r in range(2):
                    act.wait_ge(done[b], done_value(j, r))
                    A(dst[:, 2 * i + r], ps[:, 2 * b + r], ACT.Copy, scale=scale).then_inc(evac[b], 1)
            return evacuate

        def rows_out(dst):
            def evacuate(j, b, i):
                for r in range(2):
                    act.wait_ge(done[b], done_value(j, r))
                    A(dst[:, 2 * r:2 * r + 2, i * 256:(i + 1) * 256], ps[:, 2 * b + r].rearrange("p (t n) -> p t n", t=2),
                      ACT.Copy).then_inc(evac[b], 1)
            return evacuate

        def square(name, m, r, src):
            act.wait_ge(ssq_ready, m + (SSQ[name] - 1))
            A(sq[:, r], src, ACT.Square).then_inc(sq_ready, 1)

        def residual(squares, tiles=2):
            def evacuate(j, b, i):
                if squares:
                    for r in range(tiles):
                        act.wait_ge(evac[b], done_value(j, r if tiles == 2 else 1))
                        square(squares, i * tiles + r, r if tiles == 2 else b, row(h, i * tiles + r))
            return evacuate

        def norm(name, dst_hi=None, width=D):
            i = NIDX[name]
            act.wait_ge(stat_done, i + 1)
            A(rstd[:], ps[:, 7], ACT.Sqrt, bias=epsc[:, 0:1], scale=1.0 / width).then_inc(std_ready, 1)
            if dst_hi is not None:
                for m in range(dict(NORMS)[name]):
                    act.wait_ge(norm_h, NTILE[name] + m + 1)
                    A(dst_hi[:, m], hn[:, m % 2], ACT.Copy).then_inc(xh, 1)

        def gated(name, func, dst_hi):
            base = GATED[name]

            def evacuate(j, b, i):
                for r in range(2):
                    act.wait_ge(done[b], done_value(j, r))
                    A(nt[:, r], ps[:, 2 * b + r], func).then_inc(evac[b], 1)
                for r in range(2):
                    act.wait_ge(gm_prod, base + 2 * i + r + 1)
                    A(dst_hi[:, 2 * i + r], hn[:, r], ACT.Copy).then_inc(gm_hi, 1)
            return evacuate

        def turned_copy(u):
            act.wait_ge(tr_done, u + 1)
            if u >= 2:
                act.wait_ge(pv_done, u - 1)
            w = (u % 4 + 1) * P
            A(pt[:, u % 2, 0:w], ps[:, (0, 3)[u % 2], 0:w], ACT.Copy).then_inc(pt_done, 1)

        def attention(kind, heads, dst, scale=1.0):
            n, base = 4 * heads, UNIT[kind]

            def weights_of(u):
                g, w = base + u, (u % 4 + 1) * P
                p, st = pw[:, g % 3, 0:w], stat[:, g % 4]
                if kind == "fox":
                    act.wait_ge(nm_done, g + 1)
                    A(p, p, ACT.Exp, bias=st[:, 1:2], accum_out=st[:, 2:3]).then_inc(exp_done, 1)
                elif kind == "mla":
                    act.wait_ge(nm_done, g - 4 * H2 + 1)
                    act.wait_ge(tr_done, g - 2)
                    A(p, ps[:, 4 + g % 3, 0:w], ACT.Exp, bias=st[:, 1:2], scale=scale, accum_out=st[:, 2:3]).then_inc(s_free, 1)
                else:
                    t = nt[:, g % 2, 0:w]
                    act.wait_ge(s_done, g + 1)
                    if u >= 2:
                        act.wait_ge(sp_done, u - 1)
                    A(t, ps[:, 4 + g % 3, 0:w], ACT.Abs).then_inc(a_step, 1)
                    act.wait_ge(a_step, 2 * u + 1)
                    A(t, t, ACT.Exp, scale=-1.0).then_inc(a_step, 1)
                    act.wait_ge(a_step, 2 * u + 2)
                    A(t, t, ACT.Ln, bias=1.0).then_inc(ln_done, 1)

            def stick_weights(u):
                g, w = base + u, (u % 4 + 1) * P
                act.wait_ge(s_free, g + 1)
                A(pw[:, g % 3, 0:w], pw[:, g % 3, 0:w], ACT.Exp).then_inc(w_ready, 1)

            for s in range(n + 5):
                if s < n:
                    weights_of(s)
                if kind == "sb" and 1 <= s < n + 1:
                    stick_weights(s - 1)
                if 2 <= s < n + 2:
                    turned_copy(base + s - 2)
                if s >= 12 and s % 8 == 4 or s == n + 4:
                    pair = (s - 5) // 8 if s < n + 4 else heads // 2 - 1
                    act.wait_ge(pv_done, base + 8 * pair + 8)
                    g = base // 8 + pair
                    A(dst[:, pair], ps[:, (1, 2)[g % 2]], ACT.Copy).then_inc(o_hi if kind == "fox" else o_done, 1)

        for b in range(2):
            nc.scalar.sem_inc(evac[b], CREDIT)
        act.wait_ge(in_c, 16)
        A(cvec[:], cvec[:], ACT.Silu).then_inc(c_ready, 1)
        split(0, 0)
        act.wait_ge(in_x, 16)
        for m in range(DT):
            square("mix0", m, m % 2, h[:, m])
        act.wait_ge(in_s5, 32)
        A(q5[:, 0], lam[:, 2], ACT.Exp).then_inc(s5_act, 1)
        act.wait_ge(s5_arg, 1)
        A(q5[:, 5], q5[:, 1], ACT.Exp).then_inc(s5_act, 1)
        A(q5[:, 6], q5[:, 4], ACT.Sin).then_inc(s5_act, 1)
        A(q5[:, 7], q5[:, 4], ACT.Sin, scale=0.5).then_inc(s5_act, 1)
        for n in range(16):
            q, ri = n // 2, n % 2
            act.wait_ge(turned, n + 1)
            v = ps[0:64, n % 4].rearrange("p (g q s) -> p g q s", g=4, q=2)
            A(Bm[0:64, ri, 4 * q:4 * q + 4], v[:, :, 0], ACT.Copy)
            A(Bm[64:P, ri, 4 * q:4 * q + 4], v[:, :, 1], ACT.Copy).then_inc(turned_out, 1)
        for q in range(4):
            act.wait_ge(kt_done, q + 1)
            A(Kt[0:32, 8 * q:8 * q + 8].rearrange("p g d c -> p (g d c)"), ps[0:32, 4 + q % 3], ACT.Copy).then_inc(kt_out, 1)
        norm("mix0", xn_hi)

        def input_out(j, b, i):
            for r in range(2):
                act.wait_ge(done[b], done_value(j, r))
                A(uT[:, 2 * i + r], ps[:, 2 * b + r].rearrange("p (k j) -> p j k", j=TC), ACT.Copy).then_inc(evac[b], 1)

        act.wait_ge(mt_in, 128)
        layer("s5_in", input_out)
        for n in range(16):
            q, ri = n // 2, n % 2
            act.wait_ge(x_done, n + 1)
            A(X[:, :, ri, 4 * q:4 * q + 4], ps[:, n % 4].rearrange("p (g k) -> p k g", g=4), ACT.Copy).then_inc(x_out, 1)
        for q in range(8):
            act.wait_ge(y_done, q + 1)
            A(Y[:, 4 * q:4 * q + 4].rearrange("p g k -> p (g k)"), ps[:, q], ACT.Copy).then_inc(y_out, 1)
        for m in range(DT):
            act.wait_ge(z_done, m + 1)
            A(g32[:, m], nt[:, m % 2], ACT.Gelu_apprx_tanh).then_inc(g_done, 1)
            act.wait_ge(g_done, m + 1)
            A(xn_hi[:, m], g32[:, m], ACT.Copy).then_inc(gh_done, 1)
        layer("s5_glu", gated("s5_glu", ACT.Sigmoid, zg_hi))
        layer("s5_out", residual("ffn0"))

        for l in (0, 1):
            if l:
                norm("mix1", xn_hi)
                act.wait_ge(f_dve, 1)
                A(fg[:, 1], fg[:, 0], ACT.Abs).then_inc(f_act, 1)
                act.wait_ge(f_act, 1)
                A(fg[:, 1], fg[:, 1], ACT.Exp, scale=-1.0).then_inc(f_act, 1)
                act.wait_ge(f_act, 2)
                A(fg[:, 2], fg[:, 1], ACT.Ln, bias=1.0).then_inc(f_act, 1)
                layer("fox_q", copy_out(fq, HD ** -0.5))
                layer("fox_k", copy_out(fk))
                layer("fox_v", rows_out(fv))
                attention("fox", HEADS, xn_hi)
                layer("fox_out", residual("ffn1"))
            norm(f"ffn{l}", xn_hi)
            tiles = sum(HALVES) * l
            for hf, nf in enumerate(HALVES):
                with act.Fori(0, nf // 2) as i:
                    j = i + FIRST[f"up{l}{hf}"] // 2
                    f = i * 2 + tiles
                    split(j, 1)
                    for r in range(2):
                        act.wait_ge(done[0], done_value(j, r))
                        A(apad[r][:, 2:S + 2], ps[:, r], ACT.Copy).then_inc(evac[0], 1)
                    split(j + 1, 0)
                    for r in range(2):
                        act.wait_ge(conv_done, f + r + 1)
                        A(sil[:, r], cv[:, r], ACT.Silu).then_inc(silu_done, 1)
                    for r in range(2):
                        act.wait_ge(evac[1], done_value(j, r))
                        A(row(act_hi, i * 2 + r), prod[:, r], ACT.Copy).then_inc(acth, 1)
                tiles += nf
                squares = (f"mix1" if l == 0 else "final") if hf == 1 else None
                with act.Fori(0, DT // 2) as i:
                    for b in range(2):
                        j = i + FIRST[f"down{l}{hf}"] // 2
                        split(j + b, 1 - b)
                        residual(squares, 1)(j, b, i * 2 + b)

        norm("final")
        for m in range(DT):
            act.wait_ge(norm_h, NTILE["final"] + m + 1)
            square("in2", m, m % 2, h[:, m])
        norm("in2", xn_hi)
        layer("sb_q", copy_out(b_q, HD ** -0.5))
        layer("sb_k", copy_out(b_k))
        layer("sb_v", rows_out(b_v))
        attention("sb", H2, o_sb)

        def compressed_out(j, b, i):
            for r in range(2):
                if 2 * i + r < 5:
                    act.wait_ge(done[b], done_value(j, r))
                    A(cc[:, 2 * i + r], ps[:, 2 * b + r], ACT.Copy).then_inc(evac[b], 1)

        def query_out(j, b, i):
            for r in range(2):
                act.wait_ge(done[b], done_value(j, r))
                A(m_q[0:64, 2 * i + r], ps[0:64, 2 * b + r], ACT.Copy).then_inc(mq_nope, 1)

        def key_out(j, b, i):
            for r in range(2):
                act.wait_ge(done[b], done_value(j, r))
                for p in range(2):
                    ins = A(m_k[0:64, 2 * (2 * i + r) + p], ps[64 * p:64 * p + 64, 2 * b + r], ACT.Copy)
                ins.then_inc(evac[b], 1)

        layer("mla_c", compressed_out)
        after_layer(act, "mla_c")
        for m in range(3):
            square("cq", m, m % 2, cc[:, m])
        norm("cq", cq_hi, QL)
        for m in range(2):
            square("ckv", m, m % 2, cc[:, 3 + m])
        norm("ckv", ck_hi, KVL)
        layer("mla_q", query_out)
        layer("mla_k", key_out)
        layer("mla_v", rows_out(m_v))
        attention("mla", H2, o_mla, QK ** -0.5)
        layer("gate_sb", gated("gate_sb", ACT.Silu, osb_hi))
        layer("gate_mla", gated("gate_mla", ACT.Silu, omla_hi))
        for m in range(4):
            for branch, tmp in (("0", nt), ("1", hn)):
                def gate_out(j, b, i):
                    for r in range(2):
                        act.wait_ge(done[b], done_value(j, r))
                        A(tmp[:, r], ps[:, 2 * b + r], ACT.Sigmoid,
                          bias=pcol("b_gate", int(branch) * DT + 2 * m + r)).then_inc(evac[b], 1)
                layer(f"g{branch}_{m}", gate_out)
                layer(f"o{'sb' if branch == '0' else 'mla'}_{m}", lambda j, b, i: None)
            for r in range(2):
                act.wait_ge(m_sum, 2 * m + r + 1)
                A(mg_hi[:, 2 * m + r], sq[:, r], ACT.Copy).then_inc(m_hi, 1)
        layer("mix_out", residual("out"))
        norm("out")

    @block.vector
    def _(dve):
        V = nc.vector
        modf = mod[:].rearrange("p a t -> p (a t)")

        def split(j, b, words=2048):
            dve.wait_ge(split_hi, j * 2 + (b + 1))
            dve.wait_ge(done[b], done_value(j, -1))
            V.tensor_tensor(w_lo[:, b, 0:words], raw[:, b, 0:words], f32(w_hi[:, b, 0:words]), ALU.subtract).then_inc(split_lo, 1)

        def layer(name, evacuate=None):
            for i in range(COUNT[name]):
                n = FIRST[name] + i
                if n + 1 < N_CHUNKS:
                    split((n + 1) // 2, (n + 1) % 2, size(n + 1))
                if evacuate:
                    evacuate(n // 2, n % 2, i)

        def ada(first, count):
            for q in range(first, first + count):
                dve.wait_ge(ada_in[q % 2], 16 * (q // 2 + 1))
                V.tensor_tensor_reduce(adaw[:, q % 2], adaw[:, q % 2], cvec[:], 1.0, 0.0, ALU.mult, ALU.add,
                                       modf[:, q:q + 1]).then_inc(ada_used, 1)

        def ada_loop(q, b):
            dve.wait_ge(ada_in[b], q * 8 + 16)
            V.tensor_tensor_reduce(adaw[:, b], adaw[:, b], cvec[:], 1.0, 0.0, ALU.mult, ALU.add, adat[:, b:b + 1]).then_inc(ada_used, 1)
            dve.wait_ge(ada_used, q + (b + 1))
            V.tensor_copy(col(modf, q + b), adat[:, b:b + 1]).then_inc(mod_copy, 1)

        def modulation(a):
            dve.wait_ge(ada_used, 24 * (a + 1))
            V.tensor_tensor(mod[:, a], mod[:, a], par[:, PCOL["ada_b"] + 24 * a:PCOL["ada_b"] + 24 * a + 24], ALU.add).then_inc(mod_step, 1)
            dve.wait_ge(mod_step, 2 * a + 1)
            g = par[:, PCOL["norm_g"] + DT * a:PCOL["norm_g"] + DT * a + DT]
            V.scalar_tensor_tensor(gain[:, a], mod[:, a, DT:2 * DT], 1.0, g, ALU.add, ALU.mult).then_inc(mod_step, 1)
            dve.wait_ge(mod_step, 2 * a + 2)

        def add_square(name, m, r):
            dve.wait_ge(sq_ready, m + (SQ[name] + 1))
            dve.wait_ge(ssq_ready, m + SSQ[name])
            V.tensor_tensor(ssq[:], ssq[:], sq[:, r], ALU.add).then_inc(ssq_ready, 1)

        def residual(gate, squares, tiles=2, permuted=False):
            def evacuate(j, b, i):
                for r in range(tiles):
                    m = i * tiles + r
                    dve.wait_ge(done[b], done_value(j, r if tiles == 2 else 1))
                    src, dst = ps[:, 2 * b + r], row(h, m)
                    if permuted:
                        src, dst = src.rearrange("p (j k) -> p k j", j=TC), dst.rearrange("p (k j) -> p k j", j=TC)
                    if gate is None:
                        ins = V.tensor_tensor(dst, src, dst, ALU.add)
                    else:
                        ins = V.scalar_tensor_tensor(dst, src, col(mod[:, gate], m + 2 * DT), dst, ALU.mult, ALU.add)
                    ins.then_inc(evac[b], 2 // tiles)
                if squares:
                    for r in range(tiles):
                        add_square(squares, i * tiles + r, r if tiles == 2 else b)
            return evacuate

        def norm(name, src, scale, shift=None, hi=None, lo=None, dst=None):
            i, n, t0, x0 = NIDX[name], dict(NORMS)[name], NTILE[name], XTILE[name]
            dve.wait_ge(std_ready, i + 1)
            V.reciprocal(rstd[:], rstd[:]).then_inc(rstd_ready, 1)
            if name != "out":
                V.memset(ssq[:], 0.0).then_inc(ssq_ready, 1)
            dve.wait_ge(rstd_ready, i + 1)

            def low(m):
                dve.wait_ge(xh, x0 + m + 1)
                V.tensor_tensor(lo[:, m], hn[:, m % 2], f32(hi[:, m]), ALU.subtract).then_inc(xl, 1)

            for m in range(n):
                V.tensor_tensor(nt[:, m % 2], src(m), rstd[:], ALU.mult).then_inc(norm_t, 1)
                dve.wait_ge(norm_t, t0 + m + 1)
                to = hn[:, m % 2] if hi is not None else dst(m)
                if shift:
                    ins = V.tensor_scalar(to, nt[:, m % 2], scale(m), shift(m), ALU.mult, ALU.add)
                else:
                    ins = V.tensor_scalar(to, nt[:, m % 2], scale(m), None, ALU.mult)
                ins.then_inc(norm_h, 1)
                if hi is not None and m:
                    low(m - 1)
            if hi is not None:
                low(n - 1)

        def ada_norm(name, a):
            norm(name, lambda m: h[:, m], lambda m: gain[:, a, m:m + 1], lambda m: mod[:, a, m:m + 1], xn_hi, xn_lo)

        def gated(name, src, dst_hi, dst_lo):
            base = GATED[name]

            def evacuate(j, b, i):
                if base + i:
                    dve.wait_ge(gm_lo, base + 2 * i)
                for r in range(2):
                    dve.wait_ge(evac[b], done_value(j, r))
                    V.tensor_tensor(hn[:, r], src[:, 2 * i + r], nt[:, r], ALU.mult).then_inc(gm_prod, 1)
                for r in range(2):
                    dve.wait_ge(gm_hi, base + 2 * i + r + 1)
                    V.tensor_tensor(dst_lo[:, 2 * i + r], hn[:, r], f32(dst_hi[:, 2 * i + r]), ALU.subtract).then_inc(gm_lo, 1)
            return evacuate

        def attention(kind, heads, scale=1.0):
            n, base = 4 * heads, UNIT[kind]

            def first(u):
                g, hd, i = base + u, u // 4, u % 4
                w = (i + 1) * P
                z, p, st = ps[:, 4 + g % 3, 0:w], pw[:, g % 3, 0:w], stat[:, g % 4]
                if kind == "fox":
                    dve.wait_ge(s_done, g + 1)
                    if i == 0:
                        dve.wait_ge(bias_in[hd % 2], 16 * (hd // 2 + 1))
                    if g >= 3:
                        dve.wait_ge(tr_done, g - 2)
                    V.tensor_tensor_reduce(p, z, fbias[:, hd % 2, 0:w], 1.0, -3e38, ALU.add, ALU.max, st[:, 0:1]).then_inc(s_free, 1)
                    dve.wait_ge(s_free, g + 1)
                    V.tensor_scalar(st[:, 1:2], st[:, 0:1], -1.0, None, ALU.mult).then_inc(nm_done, 1)
                elif kind == "mla":
                    dve.wait_ge(s_done, g + 1)
                    V.tensor_reduce(st[:, 0:1], z, AX.X, ALU.max).then_inc(mx_done, 1)
                    dve.wait_ge(mx_done, u + 1)
                    V.tensor_scalar(st[:, 1:2], st[:, 0:1], -scale, None, ALU.mult).then_inc(nm_done, 1)
                else:
                    t = hn[:, g % 2, 0:w]
                    dve.wait_ge(ln_done, u + 1)
                    V.scalar_tensor_tensor(t, z, 0.0, nt[:, g % 2, 0:w], ALU.max, ALU.add).then_inc(sp_done, 1)
                    dve.wait_ge(sp_done, u + 1)
                    dve.wait_ge(tr_done, g - 2)
                    V.tensor_tensor_scan(p[:, ::-1], ones[:, 0:1].to_broadcast([P, w]), t[:, ::-1], 0.0, ALU.mult, ALU.add).then_inc(sc_done, 1)
                    dve.wait_ge(sc_done, u + 1)
                    V.tensor_tensor(p, z, p, ALU.subtract).then_inc(s_free, 1)

            def normalise(u):
                g, w = base + u, (u % 4 + 1) * P
                p, st = pw[:, g % 3, 0:w], stat[:, g % 4]
                if kind == "fox":
                    dve.wait_ge(exp_done, u + 1)
                else:
                    dve.wait_ge(s_free, g + 1)
                k = u + (4 * HEADS if kind == "mla" else 0)
                V.reciprocal(st[:, 3:4], st[:, 2:3]).then_inc(rc_done, 1)
                dve.wait_ge(rc_done, k + 1)
                V.tensor_scalar(p, p, st[:, 3:4], None, ALU.mult).then_inc(w_ready, 1)

            for s in range(n + 5):
                if s < n:
                    first(s)
                if kind != "sb" and 1 <= s < n + 1:
                    normalise(s - 1)
                if kind == "fox" and (s >= 12 and s % 8 == 4 or s == n + 4):
                    pair = (s - 5) // 8 if s < n + 4 else heads // 2 - 1
                    dve.wait_ge(o_hi, pair + 1)
                    V.tensor_tensor(xn_lo[:, pair], ps[:, (1, 2)[pair % 2]], f32(xn_hi[:, pair]), ALU.subtract).then_inc(o_done, 1)

        V.memset(ones[:], 1.0).then_inc(init, 1)
        V.memset(epsc[:], EPS).then_inc(init, 1)
        V.memset(Mt[:], 0.0).then_inc(init, 1)
        V.memset(Bz[:], 0.0).then_inc(init, 1)
        V.memset(ssq[:], 0.0).then_inc(ssq_ready, 1)
        split(0, 0)
        for m in range(DT):
            add_square("mix0", m, m % 2)
        dve.wait_ge(in_const, 32)
        dve.wait_ge(c_ready, 1)
        ada(0, 4)

        steps = [0]

        def link(ins):
            steps[0] += 1
            ins.then_inc(s5_step, 1)
            dve.wait_ge(s5_step, steps[0])

        lre, lim = lam[:, 0], lam[:, 1]
        q = lambda i: q5[:, i]
        TT, TS, STT = V.tensor_tensor, V.tensor_scalar, V.scalar_tensor_tensor
        TWO_PI = 2 * np.pi
        c1 = 6.28125
        c2 = float(np.float32(np.floor((TWO_PI - c1) * 2 ** 21) / 2 ** 21))
        c3 = float(TWO_PI - c1 - c2)
        MAGIC = float(1.5 * 2 ** 23)
        dve.wait_ge(in_s5, 32)
        dve.wait_ge(s5_act, 1)
        link(TT(q(1), lre, q(0), ALU.mult))
        link(TT(q(2), lim, q(0), ALU.mult))
        link(TS(q(3), q(2), 1 / TWO_PI, MAGIC, ALU.mult, ALU.add))
        link(TS(q(3), q(3), -MAGIC, None, ALU.add))
        link(STT(q(4), q(3), -c1, q(2), ALU.mult, ALU.add))
        link(STT(q(4), q(3), -c2, q(4), ALU.mult, ALU.add))
        link(STT(q(4), q(3), -c3, q(4), ALU.mult, ALU.add))
        PI_IN = float(np.nextafter(np.float32(np.pi), np.float32(0)))
        TS(q(4), q(4), PI_IN, -PI_IN, ALU.min, ALU.max).then_inc(s5_arg, 1)
        ada(4, 4)
        dve.wait_ge(s5_act, 4)
        link(TT(q(8), q(7), q(7), ALU.mult))
        link(TS(q(8), q(8), -2.0, 1.0, ALU.mult, ALU.add))
        link(TT(q(9), q(5), q(8), ALU.mult))
        link(TT(q(10), q(5), q(6), ALU.mult))
        link(TS(q(11), q(9), -1.0, None, ALU.add))
        link(TT(q(16), lre, lre, ALU.mult))
        link(TT(q(17), lim, lim, ALU.mult))
        link(TT(q(12), q(16), q(17), ALU.add))
        link(V.reciprocal(q(13), q(12)))
        link(TT(q(16), q(11), lre, ALU.mult))
        link(TT(q(17), q(10), lim, ALU.mult))
        link(TT(q(16), q(16), q(17), ALU.add))
        link(TT(q(14), q(16), q(13), ALU.mult))
        link(TT(q(16), q(10), lre, ALU.mult))
        link(TT(q(17), q(11), lim, ALU.mult))
        link(TT(q(16), q(16), q(17), ALU.subtract))
        link(TT(q(25), q(16), q(13), ALU.mult))
        link(TS(q(24), q(25), -1.0, None, ALU.mult))
        link(TS(q(20), q(10), -1.0, None, ALU.mult))
        link(V.tensor_copy(q(21), q(10)))
        link(V.tensor_copy(q(22), q(20)))
        wide = [P, 2, GP, CG]
        one = lambda i: q5[:, i].unsqueeze(1).unsqueeze(3).to_broadcast(wide)
        two = lambda i: q5[:, i:i + 2].unsqueeze(3).to_broadcast(wide)

        def complex_times(dst, src, swapped, re, im):
            link(TT(t5a[:], src, re, ALU.mult))
            link(TT(t5b[:], swapped, im, ALU.mult))
            link(TT(dst, t5a[:], t5b[:], ALU.add))

        dve.wait_ge(init, 4)
        complex_times(BW[:, :, :, TC - 1], bc[:, 0:2], bc[:, 1::-1], one(14), two(24))
        for j in range(TC - 2, -1, -1):
            complex_times(BW[:, :, :, j], BW[:, :, :, j + 1], BW[:, ::-1, :, j + 1], one(9), two(20))
            ada(8 + 2 * (TC - 2 - j), 2)
        link(V.tensor_copy(Bz[0:64, :, :, 0], BW[0:64, :, :, TC - 1]))
        V.tensor_copy(Bz[64:P, :, :, 1], BW[64:P, :, :, TC - 1]).then_inc(bw_ready, 1)
        dve.wait_ge(bw_ready, 1)
        link(V.tensor_copy(CL[:, 0, :, 0], bc[:, 2]))
        link(TS(CL[:, 1, :, 0], bc[:, 3], -1.0, None, ALU.mult))
        for d in range(TC):
            complex_times(CL[:, :, :, d + 1], CL[:, :, :, d], CL[:, ::-1, :, d], one(9), two(21))
            ada(14 + 2 * d, 2)
        link(TT(q(16), q(9), q(9), ALU.mult))
        link(TT(q(17), q(10), q(10), ALU.mult))
        link(TT(q(18), q(16), q(17), ALU.subtract))
        link(TT(q(19), q(9), q(10), ALU.mult))
        link(TS(q(19), q(19), 2.0, None, ALU.mult))
        link(TT(q(16), q(18), q(18), ALU.mult))
        link(TT(q(17), q(19), q(19), ALU.mult))
        link(TT(coef[:, 0, 0], q(16), q(17), ALU.subtract))
        link(V.tensor_copy(coef[:, 0, 1], coef[:, 0, 0]))
        link(TT(q(16), q(18), q(19), ALU.mult))
        link(TS(coef[:, 1, 0], q(16), 2.0, None, ALU.mult))
        TS(coef[:, 1, 1], q(16), -2.0, None, ALU.mult).then_inc(cl_ready, 1)
        dve.wait_ge(cl_ready, 1)
        ada(22, 2)
        modulation(0)
        ada_norm("mix0", 0)

        layer("s5_in", lambda j, b, i: ada(24 + 4 * i, 4))
        dve.wait_ge(x_out, 16)
        V.sem_inc(scan, 1)
        work = nt[:, 0, 0:3 * 2 * GP].rearrange("p (n r g) -> p n r g", n=3, r=2)

        def state(t, k):
            return t[:, bass.ds(k, 1)].rearrange("p o r g -> p (o r) g")

        with dve.Fori(0, (NCK - 2) // 2) as i:
            for s in range(2):
                k, before = i * 2 + (s + 1), i * 8 + (4 * s + 1)
                dve.wait_ge(scan, before)
                TT(work[:, 0], state(X, k - 1), coef[:, 0], ALU.mult).then_inc(scan, 1)
                TT(work[:, 1, ::-1], state(X, k - 1), coef[:, 1], ALU.mult).then_inc(scan, 1)
                dve.wait_ge(scan, before + 1)
                TT(work[:, 2], work[:, 0], state(X, k), ALU.add).then_inc(scan, 1)
                dve.wait_ge(scan, before + 3)
                TT(state(X, k), work[:, 2], work[:, 1], ALU.add).then_inc(scan, 1)
        dve.wait_ge(y_in, 16)

        def low_g(m):
            dve.wait_ge(gh_done, m + 1)
            TT(xn_lo[:, m], g32[:, m], f32(xn_hi[:, m]), ALU.subtract).then_inc(gl_done, 1)

        for m in range(DT):
            if m >= 2:
                dve.wait_ge(g_done, m - 1)
            STT(nt[:, m % 2], uT[:, m].rearrange("p j k -> p (j k)"), pcol("s5_d", m), yT[:, m], ALU.mult, ALU.add).then_inc(z_done, 1)
            if m:
                low_g(m - 1)
        low_g(DT - 1)
        glu = gated("s5_glu", g32, zg_hi, zg_lo)

        def glu_and_ada(j, b, i):
            glu(j, b, i)
            ada(40 + 2 * i, 2)

        layer("s5_glu", glu_and_ada)
        layer("s5_out", residual(0, "ffn0", permuted=True))
        modulation(1)

        for l in (0, 1):
            if l:
                ada(24 * 2 + 22, 2)
                dve.wait_ge(mod_copy, 22)
                modulation(2)
                ada_norm("mix1", 2)
                dve.wait_ge(f_done, 1)
                TS(fg[:, 0], ps[0:HEADS, 6], pcol("fox_b", 0, slice(0, HEADS)), -1.0, ALU.add, ALU.mult).then_inc(f_dve, 1)
                dve.wait_ge(f_act, 3)
                STT(fg[:, 1], fg[:, 0], 0.0, fg[:, 2], ALU.max, ALU.add).then_inc(f_dve, 1)
                dve.wait_ge(f_dve, 2)
                V.tensor_tensor_scan(fg[:, 3], ones[0:HEADS, 0:1].to_broadcast([HEADS, S]), fg[:, 1], 0.0, ALU.mult, ALU.add).then_inc(f_dve, 1)
                for n, name in enumerate(("fox_q", "fox_k", "fox_v")):
                    layer(name, lambda j, b, i: ada(72 + 8 * n + 2 * i, 2))
                attention("fox", HEADS)
                layer("fox_out", residual(2, "ffn1"))
                modulation(3)
            ada_norm(f"ffn{l}", 2 * l + 1)
            tiles = sum(HALVES) * l
            for hf, nf in enumerate(HALVES):
                for r in range(2):
                    V.memset(apad[r][:, 0:2], 0.0).then_inc(pad_ready, 1)
                dve.wait_ge(pad_ready, 4 * l + 2 * hf + 2)
                with dve.Fori(0, nf // 2) as i:
                    j = i + FIRST[f"up{l}{hf}"] // 2
                    f = i * 2 + tiles
                    of = i * 2 + (tiles - sum(HALVES) * l)
                    split(j, 1)
                    for r in range(2):
                        tap = lambda t: col(par, of + (conv_par(l, t, r)))
                        dve.wait_ge(evac[0], done_value(j, r))
                        TS(cv[:, r], apad[r][:, 0:S], tap(0), col(par, of + (PCOL["conv_b"] + l * FT + r)), ALU.mult, ALU.add).then_inc(cv_step, 1)
                        dve.wait_ge(cv_step, f * 2 + (2 * r + 1))
                        STT(cv[:, r], apad[r][:, 1:S + 1], tap(1), cv[:, r], ALU.mult, ALU.add).then_inc(cv_step, 1)
                        dve.wait_ge(cv_step, f * 2 + (2 * r + 2))
                        STT(cv[:, r], apad[r][:, 2:S + 2], tap(2), cv[:, r], ALU.mult, ALU.add).then_inc(conv_done, 1)
                    split(j + 1, 0)
                    for r in range(2):
                        dve.wait_ge(silu_done, f + (r + 1))
                        dve.wait_ge(done[1], done_value(j, r))
                        TT(prod[:, r], ps[:, 2 + r], sil[:, r], ALU.mult).then_inc(evac[1], 1)
                    for r in range(2):
                        dve.wait_ge(acth, f + (r + 1))
                        TT(row(act_lo, i * 2 + r), prod[:, r], f32(row(act_hi, i * 2 + r)), ALU.subtract).then_inc(actl, 1)
                    if l == 0:
                        for b in range(2):
                            ada_loop(i * 2 + (48 + sum(HALVES[:hf])), b)
                tiles += nf
                squares = (f"mix1" if l == 0 else "final") if hf == 1 else None
                with dve.Fori(0, DT // 2) as i:
                    for b in range(2):
                        j = i + FIRST[f"down{l}{hf}"] // 2
                        split(j + b, 1 - b)
                        residual(2 * l + 1, squares, 1)(j, b, i * 2 + b)

        norm("final", lambda m: h[:, m], lambda m: pcol("final_g", m), dst=lambda m: h[:, m])
        for m in range(DT):
            add_square("in2", m, m % 2)
        norm("in2", lambda m: h[:, m], lambda m: pcol("norm_in_g", m), hi=xn_hi, lo=xn_lo)
        layer("sb_q")
        layer("sb_k")
        layer("sb_v")
        attention("sb", H2)

        turns = [0]

        def rotate(dst, b, r, inc):
            bank = ps[:, 2 * b + r]
            TT(dst, bank[64:QK], ropt[64:QK], ALU.mult).then_inc(rope_t, 1)
            TT(rt[64:QK], bank[QK:P], ropt[QK:P], ALU.mult).then_inc(evac[b], 1)
            turns[0] += 1
            dve.wait_ge(rope_t, turns[0])
            dve.wait_ge(evac[b], inc)
            return TT(dst, dst, rt[64:QK], ALU.add)

        def shared_key(j, b, i):
            if i == 2:
                dve.wait_ge(in_rope, 16)
                dve.wait_ge(done[b], done_value(j, 1))
                dve.wait_ge(evac[b], done_value(j, 0))
                rotate(kr[64:QK], b, 1, done_value(j, 1)).then_inc(kr_ready, 1)

        layer("mla_c", shared_key)
        for m in range(3):
            add_square("cq", m, m % 2)
        norm("cq", lambda m: cc[:, m], lambda m: pcol("q_norm_g", m), hi=cq_hi, lo=cq_lo)
        for m in range(2):
            add_square("ckv", m, m % 2)
        norm("ckv", lambda m: cc[:, 3 + m], lambda m: pcol("kv_norm_g", m), hi=ck_hi, lo=ck_lo)

        def query_rope(j, b, i):
            for r in range(2):
                dve.wait_ge(mq_nope, 2 * i + r + 1)
                if i + r:
                    dve.wait_ge(mq_ready, 2 * i + r)
                rotate(m_q[64:QK, 2 * i + r], b, r, done_value(j, r)).then_inc(mq_ready, 1)

        layer("mla_q", query_rope)
        layer("mla_k")
        layer("mla_v")
        attention("mla", H2, QK ** -0.5)
        layer("gate_sb", gated("gate_sb", o_sb, osb_hi, osb_lo))
        layer("gate_mla", gated("gate_mla", o_mla, omla_hi, omla_lo))
        for m in range(4):
            for name, tmp in (("sb", nt), ("mla", hn)):
                def branch_out(j, b, i):
                    for r in range(2):
                        dve.wait_ge(evac[1 - b], done_value(j if b else j - 1, r))
                        dve.wait_ge(done[b], done_value(j, r))
                        TT(tmp[:, r], ps[:, 2 * b + r], tmp[:, r], ALU.mult).then_inc(evac[b], 1)
                layer(f"g{0 if name == 'sb' else 1}_{m}")
                layer(f"o{name}_{m}", branch_out)
            j, b = last_of(f"omla_{m}")
            dve.wait_ge(evac[b], done_value(j, 1))
            for r in range(2):
                TT(sq[:, r], nt[:, r], hn[:, r], ALU.add).then_inc(m_sum, 1)
            for r in range(2):
                dve.wait_ge(m_hi, 2 * m + r + 1)
                TT(mg_lo[:, 2 * m + r], sq[:, r], f32(mg_hi[:, 2 * m + r]), ALU.subtract).then_inc(m_lo, 1)
        layer("mix_out", residual(None, "out"))
        norm("out", lambda m: h[:, m], lambda m: pcol("norm_f_g", m), dst=lambda m: fin[:, m])


def _chunks(w, name):
    kt, cols, n = KT[name], COLS[name], COUNT[name]
    return np.ascontiguousarray(w.reshape(kt, P, n, cols).transpose(2, 1, 0, 3)).reshape(-1)


def _tiles(v):
    return np.ascontiguousarray(v.reshape(-1, P).T)


def _pairs(a):
    a = a.reshape(GP, 2, ST, *a.shape[2:])
    return np.ascontiguousarray(a.transpose(1, 2, 0, *range(3, a.ndim))).reshape(P, GP, *a.shape[3:])


def _constants():
    i, j = np.arange(P)[:, None], np.arange(P)[None, :]
    m = np.zeros((P, 4, P), np.float32)
    m[:, 0] = i == j
    m[:, 1] = np.where(j <= i, 0, NEG)
    m[:, 2] = np.where(j < i, 0, NEG)
    m[:, 3] = np.where(j // 64 <= i // 64, 0, NEG)
    half = ROPE // 2
    freq = (np.float32(10000.0) ** (-np.arange(half, dtype=np.float32) / np.float32(half))).astype(np.float32)
    ang = (np.arange(S, dtype=np.float32)[:, None] * freq[None, :]).astype(np.float32)
    co, si = np.cos(ang).T.astype(np.float32), np.sin(ang).T.astype(np.float32)
    return m, np.concatenate([co, co, -si, si], 0)


def kernel(**inputs):
    import concourse.bacc as bacc
    from concourse.bass_utils import run_bass_kernel_spmd

    a = {k: np.asarray(v) for k, v in inputs.items()}
    half = ROPE // 2
    swap = np.r_[half:ROPE, 0:half]
    w = {"s5_in": a["s5_w_in"][0], "s5_glu": a["s5_w_glu"][0], "s5_out": a["s5_w_out"][0]}
    fox = a["fox_w_in"][0]
    w.update(fox_q=fox[:, 0:D], fox_k=fox[:, D:2 * D], fox_v=fox[:, 2 * D:3 * D], fox_out=a["fox_w_out"][0])
    F = FT * P
    for l in (0, 1):
        for hf, nf in enumerate(HALVES):
            f0 = sum(HALVES[:hf]) * P
            up = a["ffn_w_up"][l]
            both = np.stack([up[:, f0:f0 + nf * P].reshape(D, nf // 2, 256),
                             up[:, F + f0:F + f0 + nf * P].reshape(D, nf // 2, 256)], 2)
            w[f"up{l}{hf}"] = both.reshape(D, nf * 256)
            w[f"down{l}{hf}"] = a["ffn_w_down"][l][f0:f0 + nf * P]
    wi = a["w_in_2"][0]
    w.update(sb_q=wi[:, 0:512], sb_k=wi[:, 512:1024], sb_v=wi[:, 1024:1536], gate_sb=wi[:, 1536:2048])
    r0 = 2048 + QL + KVL
    rope_cols = wi[:, r0:r0 + ROPE]
    w["mla_c"] = np.concatenate([wi[:, 2048:r0], np.zeros((D, 64), wi.dtype), rope_cols, rope_cols[:, swap]], 1)
    w["gate_mla"] = wi[:, r0 + ROPE:r0 + ROPE + 512]
    gl = wi[:, r0 + ROPE + 512:]
    q = a["w_q_up_2"][0].reshape(QL, H2, QK)
    w["mla_q"] = np.concatenate([q, q[:, :, 64:][:, :, swap]], 2).reshape(QL, H2 * P)
    kv = a["w_kv_up_2"][0].reshape(KVL, H2, P)
    w["mla_k"], w["mla_v"] = kv[:, :, 0:64].reshape(KVL, 512), kv[:, :, 64:].reshape(KVL, 512)
    for m in range(4):
        c = slice(256 * m, 256 * (m + 1))
        w[f"g0_{m}"], w[f"g1_{m}"] = gl[:, c], gl[:, D:][:, c]
        w[f"osb_{m}"], w[f"omla_{m}"] = a["w_o_sb_2"][0][:, c], a["w_o_mla_2"][0][:, c]
    w["mix_out"] = a["w_out_2"][0]
    fox_b = np.zeros((P, 1), np.float32)
    fox_b[0:HEADS, 0] = a["fox_b_f"][0]
    masks, rope = _constants()
    cmat = [_pairs(a[n][0].transpose(0, 2, 1)) for n in ("s5_c_re", "s5_c_im")]
    arrays = {
        "weights": np.concatenate([_chunks(w[name], name) for name, *_ in LAYERS]),
        "ada_w": np.ascontiguousarray(a["ada_w"].reshape(4, D, 24, P).transpose(0, 2, 3, 1)).reshape(96, P, D),
        "xT": np.ascontiguousarray(a["x"][0].T),
        "c": a["c"],
        "params": np.concatenate([_tiles(a[n]) for n in ("norm_g", "ada_b", "s5_d", "final_g", "norm_in_g_2", "b_gate_2",
                                                        "q_norm_g_2", "kv_norm_g_2", "norm_f_g_2", "ffn_conv_w", "ffn_conv_b")] + [fox_b], 1),
        "consts": masks,
        "rope": rope,
        "s5p": np.stack([_pairs(a["s5_lam_re"][0]), _pairs(a["s5_lam_im"][0]),
                         _pairs(np.repeat(a["s5_log_dt"][0][:, None], ST, 1))], 1),
        "s5bc": np.stack([_pairs(a["s5_b_re"][0]), _pairs(a["s5_b_im"][0]), *cmat], 1),
        "fox_f": np.ascontiguousarray(fox[:, 3 * D:].reshape(DT, P, HEADS).transpose(1, 0, 2)),
    }
    arrays = {f"in_{k}": np.ascontiguousarray(v) for k, v in arrays.items()}
    nc = bacc.Bacc("TRN2", target_bir_lowering=False, num_devices=1)
    args = [nc.dram_tensor(k, v.shape, mybir.dt.from_np(v.dtype), kind="ExternalInput").ap() for k, v in arrays.items()]
    out = nc.dram_tensor("out_T", (D, S), F32, kind="ExternalOutput").ap()
    build(nc, *args, out)
    r = run_bass_kernel_spmd(nc, [arrays], core_ids=[0])
    return np.ascontiguousarray(r.results[0]["out_T"].T)[None]
```

```python
from contextlib import ExitStack

import numpy as np
import concourse.bass as bass
from concourse import mybir

F32 = mybir.dt.float32
F32R = mybir.dt.float32r
ALU = mybir.AluOpType
ACT = mybir.ActivationFunctionType
AX = mybir.AxisListType

P = 128
S = 512
D = 1024
DT = D // P
EPS = 1e-6
NEG = -1e30

FT = 2816 // P
HALVES = (12, 10)
GRP, CG, ST = 64, 16, 64
GP = GRP // 2
TC = 4
NCK = S // TC
HEADS, HD = 16, 64
H2 = 8
ROPE, QK = 32, 96
QL, KVL = 384, 256
QBLK = S // P

LAYERS = [("s5_in", 8, 256, 4), ("s5_glu", 8, 256, 4), ("s5_out", 8, 256, 4)]
for _l in (0, 1):
    if _l == 1:
        LAYERS += [("fox_q", 8, 256, 4), ("fox_k", 8, 256, 4), ("fox_v", 8, 256, 4), ("fox_out", 8, 256, 4)]
    for _h, _n in enumerate(HALVES):
        LAYERS += [(f"up{_l}{_h}", 8, 256, _n), (f"down{_l}{_h}", _n, 128, 8)]
LAYERS += [("sb_q", 8, 256, 2), ("sb_k", 8, 256, 2), ("sb_v", 8, 256, 2), ("mla_c", 8, 256, 3),
           ("mla_q", 3, 256, 4), ("mla_k", 2, 256, 2), ("mla_v", 2, 256, 2),
           ("gate_sb", 8, 256, 2), ("gate_mla", 8, 256, 2)]
for _m in range(4):
    LAYERS += [(f"g0_{_m}", 8, 256, 1), (f"osb_{_m}", 4, 256, 1), (f"g1_{_m}", 8, 256, 1), (f"omla_{_m}", 4, 256, 1)]
LAYERS += [("mix_out", 8, 256, 4)]
FIRST, OFFSET, KT, COLS, COUNT = {}, {}, {}, {}, {}
_n = _o = 0
for _name, _kt, _c, _cnt in LAYERS:
    FIRST[_name], OFFSET[_name], KT[_name], COLS[_name], COUNT[_name] = _n, _o, _kt, _c, _cnt
    _n += _cnt
    _o += _cnt * P * _kt * _c
N_CHUNKS, W_WORDS = _n, _o
CREDIT = 2

PCOL = {}
_n = 0
for _name, _w in (("norm_g", 32), ("ada_b", 96), ("final_g", 8), ("norm_in_g", 8), ("b_gate", 16),
                  ("q_norm_g", 3), ("kv_norm_g", 2), ("norm_f_g", 8), ("conv_w", 6 * FT), ("conv_b", 2 * FT), ("fox_b", 1)):
    PCOL[_name] = _n
    _n += _w
N_PCOL = _n

NORMS = [("mix0", 8), ("ffn0", 8), ("mix1", 8), ("ffn1", 8), ("final", 8), ("in2", 8), ("cq", 3), ("ckv", 2), ("out", 8)]
NIDX = {n: i for i, (n, _) in enumerate(NORMS)}
NTILE = {n: sum(t for _, t in NORMS[:i]) for i, (n, _) in enumerate(NORMS)}
SSQ = {n: sum(t + 1 for _, t in NORMS[:i]) + 1 for i, (n, _) in enumerate(NORMS)}
SQ = {n: sum(t for _, t in NORMS[:i]) for i, (n, _) in enumerate(NORMS)}


def done_value(j, r):
    return j * 2 + (CREDIT + r + 1)


def row(t, m):
    return t[:, m] if isinstance(m, int) else t[:, bass.ds(m, 1)].rearrange("p o n -> p (o n)")


def col(t, m):
    return t[:, m:m + 1] if isinstance(m, int) else t[:, bass.ds(m, 1)]


def build(nc, weights, ada_w, xT, c, params, consts, rope, s5p, s5bc, s5d, fox_f, out):
    with ExitStack() as ctx:
        build_in(ctx, nc, weights, ada_w, xT, c, params, consts, rope, s5p, s5bc, s5d, fox_f, out)



XTILE = {n: sum(t for m, t in NORMS[:i] if m not in ("final", "out")) for i, (n, _) in enumerate(NORMS)}
UNIT = {"fox": 0, "sb": 4 * HEADS, "mla": 4 * HEADS + 4 * H2}
GATED = {"s5_glu": 0, "gate_sb": 8, "gate_mla": 12}


def build_in(ctx, nc, weights, ada_w, xT, c, params, consts, rope, s5p, s5bc, s5d, fox_f, out):
    place = [16512]

    def sb(name, shape, dt=F32):
        t = nc.alloc_sbuf_tensor_at(name, shape, dt, offset=place[0])
        place[0] += (int(np.prod(shape[1:])) * 4 + 31) // 32 * 32
        return t

    def sem(name):
        return ctx.enter_context(nc.semaphore(name))

    h = sb("h", [P, DT, S])
    xn_at = place[0]
    xn_hi, xn_lo = sb("xn_hi", [P, DT, S], F32R), sb("xn_lo", [P, DT, S], F32R)
    raw, w_hi, w_lo = sb("raw", [P, 2, 2048]), sb("w_hi", [P, 2, 2048], F32R), sb("w_lo", [P, 2, 2048], F32R)
    ada_at = place[0]
    adaw = sb("adaw", [P, 2, D])
    cvec = sb("cvec", [P, D])
    cst = sb("cst", [P, 4, P])
    par = sb("par", [P, N_PCOL])
    mod = sb("mod", [P, 4, 24])
    gain = sb("gain", [P, 4, DT])
    ones = sb("ones", [P, P])
    dd, ssq = sb("dd", [32, GP, CG]), sb("ssq", [P, S])
    stdc, rcol = sb("stdc", [P, 4]), sb("rcol", [P, 4])
    sq, nt, hn = sb("sq", [P, 2, S]), sb("nt", [P, 2, S]), sb("hn", [P, 2, S])
    stat = sb("stat", [P, 4, 4])
    coef = sb("coef", [P, GP])
    turn = sb("turn", [P, 4, GP])
    epsc, adat = sb("epsc", [P, 1]), sb("adat", [P, 2])
    arena = place[0]
    causal, strict, chunkm = (cst[:, i, :] for i in (1, 2, 3))
    ident = cst[:, 0, :]

    def put(name, address, shape, dt=F32):
        assert address + int(np.prod(shape[1:])) * 4 <= 229344, (name, arena)
        return nc.alloc_sbuf_tensor_at(name, shape, dt, offset=address)

    def at(name, kib, shape, dt=F32):
        return put(name, arena + int(kib * 1024), shape, dt)

    CL, Mt, Bm = at("CL", 0, [P, 2, GP, 5, CG]), at("Mt", 20, [P, GP, 64]), at("Bm", 28, [P, 2, GP, ST])
    BW, Bz = at("BW", 44, [P, 2, GP, CG, TC]), at("Bz", 60, [P, 2, GP, 2, CG])
    bc = put("bc", ada_at - 8192, [P, 4, GP, CG])
    Kt = at("Kt", 68, [P, GP, TC, CG])
    q5, lam = at("q5", 72, [P, 28, GP]), at("lam", 75.5, [P, 3, GP])
    t5, t5p = put("t5", ada_at, [P, 2, GP, CG]), at("t5p", 20, [P, 2, GP, CG])
    ada0 = put("ada0", xn_at, [P, 2, 4, D])
    rot = at("rot", 44, [P, 2, GP, NCK])
    rtmp = put("rtmp", ada_at, [P, 2, GP, 32])
    U = put("U", xn_at, [P, GP, NCK])
    t1, t2 = put("t1", xn_at + 16384, [P, 2, 4, NCK]), put("t2", xn_at + 20480, [P, 2, 4, NCK])
    X = put("X", xn_at + 24576, [P, 2, 2, 4, NCK])
    yT = rot[:, 0].rearrange("p (m g) k -> p m (g k)", g=4)
    g32 = rot[:, 1].rearrange("p (m g) k -> p m (g k)", g=4)
    zg_hi, zg_lo = at("zg_hi", 0, [P, DT, S], F32R), at("zg_lo", 20, [P, DT, S], F32R)
    act_hi, act_lo = at("act_hi", 0, [P, 12, S], F32R), at("act_lo", 24, [P, 12, S], F32R)
    apad = [at(f"apad{r}", 48 + r * 2.0625, [P, S + 2]) for r in range(2)]
    cv, sil, prod = at("cv", 53, [P, 2, S]), at("sil", 57, [P, 2, S]), at("prod", 61, [P, 2, S])
    fq, fk, fv = at("fq", 0, [P, DT, S]), at("fk", 16, [P, DT, S]), at("fv", 32, [P, QBLK, D])
    fbias, fg, fwf = at("fbias", 48, [P, 2, S]), at("fg", 52, [HEADS, 4, S]), at("fwf", 60, [P, DT, HEADS])
    fwf_hi, fwf_lo = at("fwf_hi", 60.5, [P, DT, HEADS], F32R), at("fwf_lo", 61, [P, DT, HEADS], F32R)
    b_q, b_k, b_v = at("b_q", 0, [P, 4, S]), at("b_k", 8, [P, 4, S]), at("b_v", 16, [P, QBLK, S])
    o_sb, o_mla = at("o_sb", 24, [P, 4, S]), at("o_mla", 48, [P, 4, S])
    cc = at("cc", 32, [P, 5, S])
    cq_hi, cq_lo = at("cq_hi", 42, [P, 3, S], F32R), at("cq_lo", 48, [P, 3, S], F32R)
    ck_hi, ck_lo = at("ck_hi", 54, [P, 2, S], F32R), at("ck_lo", 58, [P, 2, S], F32R)
    kr, rt = at("kr", 62, [P, S]), at("rt", 66, [P, S])
    m_q, m_v, m_k = at("m_q", 0, [P, H2, S]), at("m_v", 16, [P, QBLK, S]), at("m_k", 32, [P, H2, S])
    ropt = put("ropt", ada_at, [P, S])
    osb_hi, osb_lo = at("osb_hi", 0, [P, 4, S], F32R), at("osb_lo", 8, [P, 4, S], F32R)
    omla_hi, omla_lo = at("omla_hi", 32, [P, 4, S], F32R), at("omla_lo", 40, [P, 4, S], F32R)
    mg_hi, mg_lo = at("mg_hi", 16, [P, DT, S], F32R), at("mg_lo", 56, [P, DT, S], F32R)
    fin = at("fin", 0, [P, DT, S])
    pw = at("pw", 68, [P, 3, S])
    pt = sq

    ps = ctx.enter_context(nc.psum_tensor("ps", [P, 8, S], F32))
    u_dram = nc.dram_tensor("u_dram", [D, S], F32).ap()
    y_dram = nc.dram_tensor("y_dram", [D, S], F32).ap()
    f_dram = nc.dram_tensor("f_dram", [HEADS, S], F32).ap()

    in_c, in_const, in_x, in_s5, in_fw = sem("in_c"), sem("in_const"), sem("in_x"), sem("in_s5"), sem("in_fw")
    in_rope = sem("in_rope")
    raw_in = [sem("raw_in0"), sem("raw_in1")]
    split_hi, split_lo = sem("split_hi"), sem("split_lo")
    done = [sem("done0"), sem("done1")]
    evac = [sem("evac0"), sem("evac1")]
    ada_in, ada_used, c_ready = [sem("ada_in0"), sem("ada_in1")], sem("ada_used"), sem("c_ready")
    mod_step, mod_copy = sem("mod_step"), sem("mod_copy")
    init = sem("init")
    sq_ready, ssq_ready, stat_done, std_ready = sem("sq_ready"), sem("ssq_ready"), sem("stat_done"), sem("std_ready")
    rstd_ready, rstd_out, norm_t, xh, xl = sem("rstd_ready"), sem("rstd_out"), sem("norm_t"), sem("xh"), sem("xl")
    s5_act, s5_arg, s5_step, bw_ready, cl_ready = sem("s5_act"), sem("s5_arg"), sem("s5_step"), sem("bw_ready"), sem("cl_ready")
    cl_start, cl_step, rot_ready, kt_sum = sem("cl_start"), sem("cl_step"), sem("rot_ready"), sem("kt_sum")
    turned, turned_out, kt_done, kt_out, mt_in = sem("turned"), sem("turned_out"), sem("kt_done"), sem("kt_out"), sem("mt_in")
    u_saved, u_in, x_done, x_used, x_ready = [sem(f"u_saved{n}") for n in range(4)], [sem(f"u_in{m}") for m in range(DT)], sem("x_done"), sem("x_used"), sem("x_ready")
    y_done, y_out, y_saved, y_in = sem("y_done"), sem("y_out"), sem("y_saved"), [sem(f"y_in{m}") for m in range(DT)]
    ada0_in = [sem("ada0_in0"), sem("ada0_in1")]
    g_done, gh_done, gl_done = sem("g_done"), sem("gh_done"), sem("gl_done")
    gm_prod, gm_hi, gm_lo = sem("gm_prod"), sem("gm_hi"), sem("gm_lo")
    pad_ready, cv_step, conv_done, silu_done = sem("pad_ready"), sem("cv_step"), sem("conv_done"), sem("silu_done")
    acth, actl = sem("acth"), sem("actl")
    fw_hi, fw_lo = sem("fw_hi"), sem("fw_lo")
    f_done, f_dve, f_act, f_saved, bias_in = sem("f_done"), sem("f_dve"), sem("f_act"), sem("f_saved"), [sem("bias_in0"), sem("bias_in1")]
    s_done, s_free, mx_done, nm_done, exp_done, rc_done = (sem(n) for n in ("s_done", "s_free", "mx_done", "nm_done", "exp_done", "rc_done"))
    w_ready, tr_done, pt_done, pv_done, o_hi, o_done = (sem(n) for n in ("w_ready", "tr_done", "pt_done", "pv_done", "o_hi", "o_done"))
    a_step, ln_done, sp_done, sc_done = sem("a_step"), sem("ln_done"), sem("sp_done"), sem("sc_done")
    rope_t, kr_ready, mq_nope, mk_rope = sem("rope_t"), sem("kr_ready"), sem("mq_nope"), sem("mk_rope")
    mq_ready = sem("mq_ready")
    m_sum, m_hi, m_lo, out_saved = sem("m_sum"), sem("m_hi"), sem("m_lo"), sem("out_saved")

    def f32(ap):
        return ap.bitcast(F32)

    def pcol(name, i, p=slice(0, P)):
        return par[p, PCOL[name] + i:PCOL[name] + i + 1]

    def norm_buf(m):
        return (nt, hn)[m // 2 % 2][:, m % 2]

    def last_of(name):
        n = FIRST[name] + COUNT[name] - 1
        return n // 2, n % 2

    def size(n):
        for name, *_ in LAYERS:
            if FIRST[name] <= n < FIRST[name] + COUNT[name]:
                return KT[name] * COLS[name]

    def after_layer(eng, name, sems=evac):
        n = FIRST[name] + COUNT[name] - 1
        for m in (n, n - 1):
            eng.wait_ge(sems[m % 2], done_value(m // 2, 1))

    def conv_par(l, tap, f):
        return PCOL["conv_w"] + (l * 3 + tap) * FT + f

    block = ctx.enter_context(nc.Block())

    @block.sync
    def _(sp):
        sp.dma_start(lam[:], s5p).then_inc(in_s5, 16)
        sp.dma_start(bc[:], s5bc).then_inc(in_s5, 16)
        sp.dma_start(h[:], xT.rearrange("(m p) t -> p m t", p=P)).then_inc(in_x, 16)

        def ada_group(g):
            sp.dma_start(ada0[:, g % 2], ada_w[4 * g:4 * g + 4].rearrange("n p k -> p n k")).then_inc(ada0_in[g % 2], 16)

        ada_group(0)
        sp.dma_start(cst[:], consts).then_inc(in_const, 16)
        sp.dma_start(par[:], params).then_inc(in_const, 16)
        sp.dma_start(dd[:], s5d).then_inc(in_const, 16)
        ada_group(1)
        at_chunk = [0]

        def chunk_source(name, i):
            words = KT[name] * COLS[name]
            all_of = weights[OFFSET[name]:OFFSET[name] + COUNT[name] * P * words]
            all_of = all_of.rearrange("(n p f) -> p n f", p=P, f=words)
            return row(all_of, i)

        def load(j, b, name, i):
            if not (isinstance(j, int) and j == 0):
                sp.wait_ge(split_lo, j * 2 + (b - 1))
            sp.dma_start(raw[:, b, 0:KT[name] * COLS[name]], chunk_source(name, i)).then_inc(raw_in[b], 16)

        def upto(name, count=None):
            stop = FIRST[name] + (COUNT[name] if count is None else count)
            for layer, *_ in LAYERS:
                n0, n1 = FIRST[layer], FIRST[layer] + COUNT[layer]
                if n1 <= at_chunk[0] or n0 >= stop:
                    continue
                if layer[:2] in ("up", "do") and n0 == at_chunk[0]:
                    with sp.Fori(0, COUNT[layer] // 2) as i:
                        for b in range(2):
                            load(i + n0 // 2, b, layer, i * 2 + b)
                    at_chunk[0] = n1
                    continue
                for n in range(max(n0, at_chunk[0]), min(n1, stop)):
                    load(n // 2, n % 2, layer, n - n0)
                    at_chunk[0] = n + 1

        upto("s5_in", 1)
        for g in range(2, 4):
            sp.wait_ge(ada_used, 4 * (g - 1))
            ada_group(g)
        upto("s5_in")

        def save_u(n):
            sp.wait_ge(evac[n % 2], done_value(n // 2, 1))
            sp.dma_start(u_dram[n * 256:(n + 1) * 256, :].rearrange("(m p) t -> p m t", p=P), (nt, hn)[n % 2][:]).then_inc(u_saved[n], 16)

        def load_u(m):
            src = u_dram[m * P:(m + 1) * P, :].rearrange("(g x) (j k) -> (x j) g k", x=32, j=TC)
            sp.dma_start(U[:, 4 * m:4 * m + 4], src).then_inc(u_in[m], 16)

        save_u(0)
        upto("s5_glu", 1)
        save_u(1)
        sp.wait_ge(kt_sum, 1)
        sp.wait_ge(init, 4)
        for q in range(2):
            for j in range(TC):
                sp.dma_start(Mt[q * 64 + j:(q + 1) * 64:TC, :, j * CG:64],
                             Kt[q * CG:(q + 1) * CG, :, 0:TC - j, :].rearrange("p g d c -> p g (d c)")).then_inc(mt_in, 16)
        save_u(2)
        save_u(3)
        for m in range(DT):
            sp.wait_ge(u_saved[m // 2], 16)
            load_u(m)
        upto("s5_glu", 2)
        for m in range(DT):
            sp.wait_ge(y_out, m + 1)
            for q in range(2):
                for j in range(TC):
                    dst = y_dram[m * P:(m + 1) * P, :].rearrange("(g q c) (j k) -> q j c g k", q=2, c=CG, j=TC)[q, j]
                    sp.dma_start(dst, nt[q * 64 + j * CG:q * 64 + (j + 1) * CG, m % 2].rearrange("p (g k) -> p g k", g=4)).then_inc(y_saved, 16)
            sp.wait_ge(y_saved, 128 * (m + 1))
            sp.dma_start(yT[:, m], y_dram[m * P:(m + 1) * P, :]).then_inc(y_in[m], 16)
        upto("down01")
        upto("fox_q", 2)
        after_layer(sp, "down01")
        sp.dma_start(fwf[:], fox_f).then_inc(in_fw, 16)
        upto("fox_k", 2)
        sp.wait_ge(f_dve, 3)
        sp.dma_start(f_dram, fg[:, 3]).then_inc(f_saved, 16)
        upto("fox_out", 3)
        sp.wait_ge(f_saved, 16)
        for hd in range(HEADS):
            if hd >= 2:
                sp.wait_ge(s_free, 4 * (hd - 1))
            sp.dma_start(fbias[:, hd % 2], f_dram[hd:hd + 1, :].to_broadcast([P, S])).then_inc(bias_in[hd % 2], 16)
        upto("mix_out")
        sp.wait_ge(norm_t, NTILE["out"] + 8)
        sp.dma_start(out.rearrange("(m p) t -> p m t", p=P), fin[:]).then_inc(out_saved, 16)
        sp.wait_ge(out_saved, 16)

    @block.gpsimd
    def _(pool):
        pool.dma_start(cvec[:], c.to_broadcast([P, D])).then_inc(in_c, 16)
        pool.wait_ge(cl_start, 1)
        wide = [P, 2, GP, CG]
        for d in range(TC):
            re, im = q5[:, 9].unsqueeze(1).unsqueeze(3).to_broadcast(wide), q5[:, 21:23].unsqueeze(3).to_broadcast(wide)
            nc.gpsimd.tensor_tensor(CL[:, :, :, d + 1], CL[:, :, :, d], re, ALU.mult).then_inc(cl_step, 1)
            nc.gpsimd.tensor_tensor(t5p[:], CL[:, ::-1, :, d], im, ALU.mult).then_inc(cl_step, 1)
            pool.wait_ge(cl_step, 3 * d + 2)
            ins = nc.gpsimd.tensor_tensor(CL[:, :, :, d + 1], CL[:, :, :, d + 1], t5p[:], ALU.add)
            ins.then_inc(cl_step, 1)
            pool.wait_ge(cl_step, 3 * d + 3)
        nc.gpsimd.memset(Mt[:], 0.0).then_inc(init, 1)
        pool.wait_ge(rot_ready, 1)
        for b in range(2):
            pool.dma_start(adaw[:, b], ada_w[16 + b]).then_inc(ada_in[b], 16)
        with pool.Fori(1, 40) as i:
            for b in range(2):
                pool.wait_ge(ada_used, i * 2 + (b + 15))
                pool.dma_start(adaw[:, b], row(ada_w.rearrange("n p k -> p n k"), i * 2 + (b + 16))).then_inc(ada_in[b], 16)
        pool.wait_ge(ada_used, 96)
        pool.dma_start(ropt[64:P, :], rope).then_inc(in_rope, 16)
        pool.wait_ge(kr_ready, 1)
        after_layer(pool, "mla_q")
        for hd in range(H2):
            nc.gpsimd.tensor_copy(m_k[64:QK, hd], kr[64:QK, :]).then_inc(mk_rope, 1)

    @block.tensor
    def _(pe):
        def three(bank, hi_w, lo_w, hi_x, lo_x, start, stop):
            pe.matmul(bank, lo_w, hi_x, start=start, stop=False)
            pe.matmul(bank, hi_w, lo_x, start=False, stop=False)
            return pe.matmul(bank, hi_w, hi_x, start=False, stop=stop)

        def chunk_ready(j, b):
            pe.wait_ge(split_lo, j * 2 + (b + 1))
            pe.wait_ge(evac[b], done_value(j, -1))

        def product(name, j, b, x_hi, x_lo, x_ready=None):
            chunk_ready(j, b)
            kt, cols = KT[name], COLS[name]
            for k in range(kt):
                if x_ready:
                    pe.wait_ge(x_ready[0], x_ready[1] + k + 1)
                for r in range(cols // P):
                    w = slice(k * cols + r * P, k * cols + (r + 1) * P)
                    mm = three(ps[:, 2 * b + r], w_hi[:, b, w], w_lo[:, b, w], x_hi[:, k], x_lo[:, k], k == 0, k == kt - 1)
                    if k == kt - 1:
                        mm.then_inc(done[b], 2 * P // cols)

        def product_rows(name, j, b, x_hi, x_lo):
            chunk_ready(j, b)
            kt = KT[name]
            for t in range(QBLK):
                for k in range(kt):
                    x = slice(t * P, (t + 1) * P)
                    w = slice(k * 256, (k + 1) * 256)
                    mm = three(ps[:, 2 * b + t // 2, (t % 2) * 256:(t % 2 + 1) * 256], x_hi[:, k, x], x_lo[:, k, x],
                               w_hi[:, b, w], w_lo[:, b, w], k == 0, k == kt - 1)
                if t % 2:
                    mm.then_inc(done[b], 1)

        def layer(name, x_hi, x_lo, x_ready=None, rows=False):
            for i in range(COUNT[name]):
                n = FIRST[name] + i
                if rows:
                    product_rows(name, n // 2, n % 2, x_hi, x_lo)
                else:
                    product(name, n // 2, n % 2, x_hi, x_lo, x_ready if i == 0 else None)

        def layer_loop(name, x_hi, x_lo, x_ready=None):
            with pe.Fori(0, COUNT[name] // 2) as i:
                for b in range(2):
                    product(name, i + FIRST[name] // 2, b, x_hi, x_lo, None if b else x_ready)

        def norm_stat(name):
            pe.wait_ge(ssq_ready, SSQ[name] + dict(NORMS)[name])
            if NIDX[name]:
                pe.wait_ge(norm_t, NTILE[name])
            for t in range(QBLK):
                mm = pe.matmul(ps[:, 7, t:t + 1], ssq[:, t * P:(t + 1) * P], ones[:, 0:1], start=True, stop=True)
            mm.then_inc(stat_done, 1)
            pe.wait_ge(rstd_ready, NIDX[name] + 1)
            for t in range(QBLK):
                mm = pe.matmul(ps[:, 7, t * P:(t + 1) * P], rcol[:, t:t + 1].to_broadcast([P, P]), ident, start=True, stop=True)
            mm.then_inc(rstd_out, 1)

        def attention(kind, heads, q, k, v, rows, diag_mask):
            n = 4 * heads
            S_BANK, T_BANK, O_BANK = (4, 5, 6), (0, 3), (1, 2)

            def scores(u):
                g, hd, i = UNIT[kind] + u, u // 4, u % 4
                if g >= 3:
                    pe.wait_ge(s_free, g - 2)
                bank = ps[:, S_BANK[g % 3]]
                pe.matmul(bank[:, 0:(i + 1) * P], q(hd)[:, i * P:(i + 1) * P], k(hd)[:, 0:(i + 1) * P], start=True, stop=False)
                pe.matmul(bank[:, i * P:(i + 1) * P], ident, diag_mask, start=False, stop=True).then_inc(s_done, 1)

            def turn(u):
                g, i = UNIT[kind] + u, u % 4
                pe.wait_ge(w_ready, g + 1)
                if g >= 2:
                    pe.wait_ge(pt_done, g - 1)
                for t in range(i + 1):
                    mm = pe.transpose(ps[:, T_BANK[g % 2], t * P:(t + 1) * P], pw[:, g % 3, t * P:(t + 1) * P], ident)
                mm.then_inc(tr_done, 1)

            def weigh(u):
                g, hd, i = UNIT[kind] + u, u // 4, u % 4
                pe.wait_ge(pt_done, g + 1)
                if u % 8 == 0 and g // 8 >= 2:
                    pe.wait_ge(o_done, g // 8 - 1)
                half = hd % 2 * 64
                for t in range(i + 1):
                    mm = pe.matmul(ps[half:half + 64, O_BANK[g // 8 % 2], i * P:(i + 1) * P], v[:, t, hd * 64:(hd + 1) * 64],
                                   pt[:, g % 2, t * P:(t + 1) * P], start=t == 0, stop=t == i)
                mm.then_inc(pv_done, 1)

            for s in range(n + 3):
                if s < n:
                    scores(s)
                if 2 <= s < n + 2:
                    turn(s - 2)
                if s >= 3:
                    weigh(s - 3)

        for b in range(2):
            nc.tensor.sem_inc(done[b], CREDIT)
        pe.wait_ge(in_const, 48)
        pe.wait_ge(init, 1)
        norm_stat("mix0")
        for i in range(2):
            product("s5_in", i // 2, i % 2, xn_hi, xn_lo, None if i else (xl, XTILE["mix0"]))
        pe.wait_ge(bw_ready, 1)
        for n in range(16):
            q, ri = n // 2, n % 2
            if n >= 3:
                pe.wait_ge(turned_out, n - 2)
            for g in range(4):
                mm = pe.transpose(ps[0:64, 4 + n % 3, g * P:(g + 1) * P], BW[:, ri, 4 * q + g].rearrange("p c j -> p (c j)"), ident)
            mm.then_inc(turned, 1)
        pe.wait_ge(cl_step, 3 * TC)
        pe.wait_ge(turned_out, 16)
        for q in range(4):
            if q == 3:
                pe.wait_ge(kt_out, 1)
            for g in range(8 * q, 8 * q + 8):
                for ri in range(2):
                    mm = pe.matmul(ps[0:32, 4 + q % 3, (g % 8) * 64:(g % 8 + 1) * 64], Bz[:, ri, g].rearrange("p q c -> p (q c)"),
                                   CL[:, ri, g, 0:TC].rearrange("p d c -> p (d c)"), start=ri == 0, stop=ri == 1)
            mm.then_inc(kt_done, 1)
        for i in range(2, 4):
            product("s5_in", i // 2, i % 2, xn_hi, xn_lo)

        after_layer(pe, "s5_in")
        pe.wait_ge(kt_out, 4)
        pe.wait_ge(mt_in, 128)

        def from_input(q):
            if q >= 2:
                pe.wait_ge(x_used, q - 1)
            if q >= 4:
                pe.wait_ge(y_out, q - 3)
            pe.wait_ge(u_in[q], 16)
            for ri in range(2):
                for g in range(4):
                    for p in (slice(0, 64), slice(64, P)):
                        mm = pe.matmul(ps[p, q % 2 * 2 + ri, g * P:(g + 1) * P], Bm[p, ri, 4 * q + g], U[p, 4 * q + g], start=True, stop=True)
            mm.then_inc(x_done, 1)
            for g in range(4):
                for p in (slice(0, 64), slice(64, P)):
                    pe.matmul(ps[p, 4 + q % 4, g * P:(g + 1) * P], Mt[p, 4 * q + g], U[p, 4 * q + g], start=g == 0, stop=False,
                              skip_group_check=True)

        def from_states(q):
            pe.wait_ge(x_ready, q + 1)
            for g in range(4):
                for p in (slice(0, 64), slice(64, P)):
                    for ri in range(2):
                        mm = pe.matmul(ps[p, 4 + q % 4, g * P + 1:(g + 1) * P], CL[p, ri, 4 * q + g, 1:5].rearrange("p d c -> p (d c)"),
                                       X[p, q % 2, ri, g, 0:NCK - 1], start=False, stop=ri == 1, skip_group_check=True)
            mm.then_inc(y_done, 1)

        for q in range(DT + 2):
            if q < DT:
                from_input(q)
            if q >= 2:
                from_states(q - 2)
        pe.wait_ge(x_used, DT)
        layer("s5_glu", xn_hi, xn_lo, (gl_done, 0))
        layer("s5_out", zg_hi, zg_lo, (gm_lo, 0))

        for l in (0, 1):
            if l:
                norm_stat("mix1")
                layer("fox_q", xn_hi, xn_lo, (xl, XTILE["mix1"]))
                pe.wait_ge(fw_lo, 1)
                for k in range(DT):
                    mm = three(ps[0:HEADS, 6], fwf_hi[:, k], fwf_lo[:, k], xn_hi[:, k], xn_lo[:, k], k == 0, k == DT - 1)
                mm.then_inc(f_done, 1)
                layer("fox_k", xn_hi, xn_lo)
                layer("fox_v", xn_hi, xn_lo, rows=True)
                after_layer(pe, "fox_v")
                pe.wait_ge(f_dve, 1)
                attention("fox", HEADS, lambda hd: fq[hd % 2 * 64:hd % 2 * 64 + 64, hd // 2],
                          lambda hd: fk[hd % 2 * 64:hd % 2 * 64 + 64, hd // 2], fv, 64, causal)
                layer("fox_out", xn_hi, xn_lo, (o_done, 0))
            norm_stat(f"ffn{l}")
            tiles = sum(HALVES) * l
            for hf, nf in enumerate(HALVES):
                layer_loop(f"up{l}{hf}", xn_hi, xn_lo, None if hf else (xl, XTILE[f"ffn{l}"]))
                layer_loop(f"down{l}{hf}", act_hi, act_lo, (actl, tiles))
                tiles += nf

        norm_stat("final")
        norm_stat("in2")
        layer("sb_q", xn_hi, xn_lo, (xl, XTILE["in2"]))
        layer("sb_k", xn_hi, xn_lo)
        layer("sb_v", xn_hi, xn_lo, rows=True)
        after_layer(pe, "sb_v")
        attention("sb", H2, lambda hd: b_q[hd % 2 * 64:hd % 2 * 64 + 64, hd // 2],
                  lambda hd: b_k[hd % 2 * 64:hd % 2 * 64 + 64, hd // 2], b_v, 64, strict)
        pe.wait_ge(o_done, 12)
        layer("mla_c", xn_hi, xn_lo)
        norm_stat("cq")
        norm_stat("ckv")
        layer("mla_q", cq_hi, cq_lo, (xl, XTILE["cq"]))
        layer("mla_k", ck_hi, ck_lo, (xl, XTILE["ckv"]))
        layer("mla_v", ck_hi, ck_lo, rows=True)
        after_layer(pe, "mla_v")
        pe.wait_ge(mk_rope, H2)
        attention("mla", H2, lambda hd: m_q[0:QK, hd], lambda hd: m_k[0:QK, hd], m_v, QK, chunkm)
        pe.wait_ge(o_done, 16)
        layer("gate_sb", xn_hi, xn_lo)
        layer("gate_mla", xn_hi, xn_lo)
        for m in range(4):
            layer(f"g0_{m}", xn_hi, xn_lo)
            layer(f"osb_{m}", osb_hi, osb_lo, (gm_lo, GATED["gate_sb"]) if m == 0 else None)
            layer(f"g1_{m}", xn_hi, xn_lo)
            layer(f"omla_{m}", omla_hi, omla_lo, (gm_lo, GATED["gate_mla"]) if m == 0 else None)
        layer("mix_out", mg_hi, mg_lo, (m_lo, 0))
        norm_stat("out")

    @block.scalar
    def _(act):
        A = nc.scalar.activation

        def split(j, b, words=2048):
            act.wait_ge(raw_in[b], j * 16 + 16)
            act.wait_ge(done[b], done_value(j, -1))
            A(w_hi[:, b, 0:words], raw[:, b, 0:words], ACT.Copy).then_inc(split_hi, 1)

        def split_next(n):
            if n + 1 < N_CHUNKS:
                split((n + 1) // 2, (n + 1) % 2, size(n + 1))

        def layer(name, evacuate):
            for i in range(COUNT[name]):
                n = FIRST[name] + i
                split_next(n)
                evacuate(n // 2, n % 2, i)

        def copy_out(dst, scale=1.0):
            def evacuate(j, b, i):
                for r in range(2):
                    act.wait_ge(done[b], done_value(j, r))
                    A(dst[:, 2 * i + r], ps[:, 2 * b + r], ACT.Copy, scale=scale).then_inc(evac[b], 1)
            return evacuate

        def rows_out(dst):
            def evacuate(j, b, i):
                for r in range(2):
                    act.wait_ge(done[b], done_value(j, r))
                    A(dst[:, 2 * r:2 * r + 2, i * 256:(i + 1) * 256], ps[:, 2 * b + r].rearrange("p (t n) -> p t n", t=2),
                      ACT.Copy).then_inc(evac[b], 1)
            return evacuate

        def square(name, m, r, src):
            act.wait_ge(ssq_ready, m + (SSQ[name] - 1))
            A(sq[:, r], src, ACT.Square).then_inc(sq_ready, 1)

        def residual(squares, tiles=2):
            def evacuate(j, b, i):
                if squares:
                    for r in range(tiles):
                        act.wait_ge(evac[b], done_value(j, r if tiles == 2 else 1))
                        square(squares, i * tiles + r, r if tiles == 2 else b, row(h, i * tiles + r))
            return evacuate

        def norm(name, dst_hi=None, width=D, shift=None):
            i = NIDX[name]
            act.preload_act_table(ACT.Sqrt)
            act.wait_ge(stat_done, i + 1)
            A(stdc[:], ps[:, 7, 0:4], ACT.Sqrt, bias=epsc[:, 0:1], scale=1.0 / width).then_inc(std_ready, 1)
            if dst_hi is not None:
                for m in range(dict(NORMS)[name]):
                    act.wait_ge(norm_t, NTILE[name] + m + 1)
                    if shift is None:
                        A(dst_hi[:, m], norm_buf(m), ACT.Copy).then_inc(xh, 1)
                    else:
                        A(dst_hi[:, m], norm_buf(m), ACT.Identity, bias=mod[:, shift, m:m + 1]).then_inc(xh, 1)

        def gated(name, func, dst_hi):
            base = GATED[name]

            def evacuate(j, b, i):
                for r in range(2):
                    act.wait_ge(done[b], done_value(j, r))
                    A(nt[:, r], ps[:, 2 * b + r], func).then_inc(evac[b], 1)
                for r in range(2):
                    act.wait_ge(gm_prod, base + 2 * i + r + 1)
                    A(dst_hi[:, 2 * i + r], hn[:, r], ACT.Copy).then_inc(gm_hi, 1)
            return evacuate

        def turned_copy(u):
            act.wait_ge(tr_done, u + 1)
            if u >= 2:
                act.wait_ge(pv_done, u - 1)
            w = (u % 4 + 1) * P
            A(pt[:, u % 2, 0:w], ps[:, (0, 3)[u % 2], 0:w], ACT.Copy).then_inc(pt_done, 1)

        def attention(kind, heads, dst, scale=1.0):
            n, base = 4 * heads, UNIT[kind]
            if kind == "sb":
                act.preload_act_table_set("natural_log_exp_and_others")
            else:
                act.preload_act_table(ACT.Exp)

            def weights_of(u):
                g, w = base + u, (u % 4 + 1) * P
                p, st = pw[:, g % 3, 0:w], stat[:, g % 4]
                if kind == "fox":
                    act.wait_ge(nm_done, g + 1)
                    A(p, p, ACT.Exp, bias=st[:, 1:2], accum_out=st[:, 2:3]).then_inc(exp_done, 1)
                elif kind == "mla":
                    act.wait_ge(nm_done, g - 4 * H2 + 1)
                    act.wait_ge(tr_done, g - 2)
                    A(p, ps[:, 4 + g % 3, 0:w], ACT.Exp, bias=st[:, 1:2], scale=scale, accum_out=st[:, 2:3]).then_inc(s_free, 1)
                else:
                    t = nt[:, g % 2, 0:w]
                    act.wait_ge(s_done, g + 1)
                    if u >= 2:
                        act.wait_ge(sp_done, u - 1)
                    A(t, ps[:, 4 + g % 3, 0:w], ACT.Abs).then_inc(a_step, 1)
                    act.wait_ge(a_step, 2 * u + 1)
                    A(t, t, ACT.Exp, scale=-1.0).then_inc(a_step, 1)
                    act.wait_ge(a_step, 2 * u + 2)
                    A(t, t, ACT.Ln, bias=1.0).then_inc(ln_done, 1)

            def stick_weights(u):
                g, w = base + u, (u % 4 + 1) * P
                act.wait_ge(s_free, g + 1)
                A(pw[:, g % 3, 0:w], pw[:, g % 3, 0:w], ACT.Exp).then_inc(w_ready, 1)

            for s in range(n + 5):
                if s < n:
                    weights_of(s)
                if kind == "sb" and 1 <= s < n + 1:
                    stick_weights(s - 1)
                if 2 <= s < n + 2:
                    turned_copy(base + s - 2)
                if s >= 12 and s % 8 == 4 or s == n + 4:
                    pair = (s - 5) // 8 if s < n + 4 else heads // 2 - 1
                    act.wait_ge(pv_done, base + 8 * pair + 8)
                    g = base // 8 + pair
                    A(dst[:, pair], ps[:, (1, 2)[g % 2]], ACT.Copy).then_inc(o_hi if kind == "fox" else o_done, 1)

        for b in range(2):
            nc.scalar.sem_inc(evac[b], CREDIT)
        act.wait_ge(in_c, 16)
        A(cvec[:], cvec[:], ACT.Silu).then_inc(c_ready, 1)
        act.wait_ge(in_s5, 32)
        A(q5[:, 0], lam[:, 2], ACT.Exp).then_inc(s5_act, 1)
        act.wait_ge(s5_arg, 1)
        A(q5[:, 5], q5[:, 1], ACT.Exp).then_inc(s5_act, 1)
        A(q5[:, 6], q5[:, 4], ACT.Sin).then_inc(s5_act, 1)
        A(q5[:, 7], q5[:, 4], ACT.Sin, scale=0.5).then_inc(s5_act, 1)
        act.wait_ge(in_x, 16)
        for m in range(DT):
            square("mix0", m, m % 2, h[:, m])
        split(0, 0)
        norm("mix0", xn_hi, shift=0)

        def input_out(j, b, i):
            if i >= 2:
                act.wait_ge(u_saved[i - 2], 16)
            for r in range(2):
                act.wait_ge(done[b], done_value(j, r))
                A((nt, hn)[i % 2][:, r], ps[:, 2 * b + r].rearrange("p (k j) -> p j k", j=TC), ACT.Copy).then_inc(evac[b], 1)

        for i in range(2):
            split_next(i)
            input_out(0, i, i)
        for n in range(16):
            q, ri = n // 2, n % 2
            act.wait_ge(turned, n + 1)
            v = ps[0:64, 4 + n % 3].rearrange("p (g q s) -> p g q s", g=4, q=2)
            A(Bm[0:64, ri, 4 * q:4 * q + 4], v[:, :, 0], ACT.Copy)
            A(Bm[64:P, ri, 4 * q:4 * q + 4], v[:, :, 1], ACT.Copy).then_inc(turned_out, 1)
        for q in range(4):
            act.wait_ge(kt_done, q + 1)
            A(Kt[0:32, 8 * q:8 * q + 8].rearrange("p g d c -> p (g d c)"), ps[0:32, 4 + q % 3], ACT.Copy).then_inc(kt_out, 1)
        for i in range(2, 4):
            split_next(i)
            input_out(1, i % 2, i)

        def y_tile(m):
            act.wait_ge(y_done, m + 1)
            if m >= 2:
                act.wait_ge(y_saved, 128 * (m - 1))
            A(nt[:, m % 2], ps[:, 4 + m % 4], ACT.Copy).then_inc(y_out, 1)

        def gelu_tile(m):
            act.wait_ge(y_in[m], 16)
            A(g32[:, m], yT[:, m], ACT.Gelu_apprx_tanh).then_inc(g_done, 1)
            act.wait_ge(g_done, m + 1)
            A(xn_hi[:, m], g32[:, m], ACT.Copy).then_inc(gh_done, 1)

        for m in range(DT + 1):
            if m < DT:
                y_tile(m)
            if m:
                gelu_tile(m - 1)
        layer("s5_glu", gated("s5_glu", ACT.Sigmoid, zg_hi))
        layer("s5_out", residual("ffn0"))

        for l in (0, 1):
            if l:
                norm("mix1", xn_hi, shift=2)
                act.wait_ge(in_fw, 16)
                A(fwf_hi[:], fwf[:], ACT.Copy).then_inc(fw_hi, 1)
                layer("fox_q", copy_out(fq, HD ** -0.5))
                act.wait_ge(f_dve, 1)
                A(fg[:, 1], fg[:, 0], ACT.Abs).then_inc(f_act, 1)
                act.wait_ge(f_act, 1)
                A(fg[:, 1], fg[:, 1], ACT.Exp, scale=-1.0).then_inc(f_act, 1)
                act.wait_ge(f_act, 2)
                A(fg[:, 2], fg[:, 1], ACT.Ln, bias=1.0).then_inc(f_act, 1)
                layer("fox_k", copy_out(fk))
                layer("fox_v", rows_out(fv))
                attention("fox", HEADS, xn_hi)
                layer("fox_out", residual("ffn1"))
            norm(f"ffn{l}", xn_hi, shift=2 * l + 1)
            tiles = sum(HALVES) * l
            for hf, nf in enumerate(HALVES):
                act.preload_act_table(ACT.Silu)
                with act.Fori(0, nf // 2) as i:
                    j = i + FIRST[f"up{l}{hf}"] // 2
                    f = i * 2 + tiles
                    split(j, 1)
                    for r in range(2):
                        act.wait_ge(done[0], done_value(j, r))
                        A(apad[r][:, 2:S + 2], ps[:, r], ACT.Copy).then_inc(evac[0], 1)
                    split(j + 1, 0)
                    for r in range(2):
                        act.wait_ge(conv_done, f + r + 1)
                        A(sil[:, r], cv[:, r], ACT.Silu).then_inc(silu_done, 1)
                    for r in range(2):
                        act.wait_ge(evac[1], done_value(j, r))
                        A(row(act_hi, i * 2 + r), prod[:, r], ACT.Copy).then_inc(acth, 1)
                tiles += nf
                squares = (f"mix1" if l == 0 else "final") if hf == 1 else None
                with act.Fori(0, DT // 2) as i:
                    for b in range(2):
                        j = i + FIRST[f"down{l}{hf}"] // 2
                        split(j + b, 1 - b)
                        residual(squares, 1)(j, b, i * 2 + b)

        norm("final")
        for m in range(DT):
            act.wait_ge(norm_t, NTILE["final"] + m + 1)
            square("in2", m, m % 2, h[:, m])
        norm("in2", xn_hi)
        layer("sb_q", copy_out(b_q, HD ** -0.5))
        layer("sb_k", copy_out(b_k))
        layer("sb_v", rows_out(b_v))
        attention("sb", H2, o_sb)

        def compressed_out(j, b, i):
            for r in range(2):
                if 2 * i + r < 5:
                    act.wait_ge(done[b], done_value(j, r))
                    A(cc[:, 2 * i + r], ps[:, 2 * b + r], ACT.Copy).then_inc(evac[b], 1)

        def query_out(j, b, i):
            for r in range(2):
                act.wait_ge(done[b], done_value(j, r))
                A(m_q[0:64, 2 * i + r], ps[0:64, 2 * b + r], ACT.Copy).then_inc(mq_nope, 1)

        def key_out(j, b, i):
            for r in range(2):
                act.wait_ge(done[b], done_value(j, r))
                for p in range(2):
                    ins = A(m_k[0:64, 2 * (2 * i + r) + p], ps[64 * p:64 * p + 64, 2 * b + r], ACT.Copy)
                ins.then_inc(evac[b], 1)

        layer("mla_c", compressed_out)
        after_layer(act, "mla_c")
        for m in range(3):
            square("cq", m, m % 2, cc[:, m])
        norm("cq", cq_hi, QL)
        for m in range(2):
            square("ckv", m, m % 2, cc[:, 3 + m])
        norm("ckv", ck_hi, KVL)
        layer("mla_q", query_out)
        layer("mla_k", key_out)
        layer("mla_v", rows_out(m_v))
        attention("mla", H2, o_mla, QK ** -0.5)
        layer("gate_sb", gated("gate_sb", ACT.Silu, osb_hi))
        layer("gate_mla", gated("gate_mla", ACT.Silu, omla_hi))
        for m in range(4):
            for branch, tmp in (("0", nt), ("1", hn)):
                def gate_out(j, b, i):
                    for r in range(2):
                        act.wait_ge(done[b], done_value(j, r))
                        A(tmp[:, r], ps[:, 2 * b + r], ACT.Sigmoid,
                          bias=pcol("b_gate", int(branch) * DT + 2 * m + r)).then_inc(evac[b], 1)
                layer(f"g{branch}_{m}", gate_out)
                layer(f"o{'sb' if branch == '0' else 'mla'}_{m}", lambda j, b, i: None)
            for r in range(2):
                act.wait_ge(m_sum, 2 * m + r + 1)
                A(mg_hi[:, 2 * m + r], sq[:, r], ACT.Copy).then_inc(m_hi, 1)
        layer("mix_out", residual("out"))
        norm("out")

    @block.vector
    def _(dve):
        V = nc.vector
        modf = mod[:].rearrange("p a t -> p (a t)")

        def split(j, b, words=2048):
            dve.wait_ge(split_hi, j * 2 + (b + 1))
            dve.wait_ge(done[b], done_value(j, -1))
            V.tensor_tensor(w_lo[:, b, 0:words], raw[:, b, 0:words], f32(w_hi[:, b, 0:words]), ALU.subtract).then_inc(split_lo, 1)

        def layer(name, evacuate=None):
            for i in range(COUNT[name]):
                n = FIRST[name] + i
                if n + 1 < N_CHUNKS:
                    split((n + 1) // 2, (n + 1) % 2, size(n + 1))
                if evacuate:
                    evacuate(n // 2, n % 2, i)

        def ada(first, count):
            for q in range(first, first + count):
                if q < 16:
                    dve.wait_ge(ada0_in[q // 4 % 2], 16 * (q // 8 + 1))
                    w = ada0[:, q // 4 % 2, q % 4]
                else:
                    dve.wait_ge(ada_in[q % 2], 16 * (q // 2 - 7))
                    w = adaw[:, q % 2]
                V.tensor_tensor_reduce(w, w, cvec[:], 1.0, 0.0, ALU.mult, ALU.add, modf[:, q:q + 1]).then_inc(ada_used, 1)

        def ada_loop(q, b):
            dve.wait_ge(ada_in[b], q * 8 - 112)
            V.tensor_tensor_reduce(adaw[:, b], adaw[:, b], cvec[:], 1.0, 0.0, ALU.mult, ALU.add, adat[:, b:b + 1]).then_inc(ada_used, 1)
            dve.wait_ge(ada_used, q + (b + 1))
            V.tensor_copy(col(modf, q + b), adat[:, b:b + 1]).then_inc(mod_copy, 1)

        mod_steps = [0]

        def shift_and_scale(a):
            dve.wait_ge(ada_used, 24 * a + 16)
            V.tensor_tensor(mod[:, a, 0:16], mod[:, a, 0:16], par[:, PCOL["ada_b"] + 24 * a:PCOL["ada_b"] + 24 * a + 16], ALU.add).then_inc(mod_step, 1)
            dve.wait_ge(mod_step, mod_steps[0] + 1)
            g = par[:, PCOL["norm_g"] + DT * a:PCOL["norm_g"] + DT * a + DT]
            V.scalar_tensor_tensor(gain[:, a], mod[:, a, DT:2 * DT], 1.0, g, ALU.add, ALU.mult).then_inc(mod_step, 1)
            mod_steps[0] += 2
            dve.wait_ge(mod_step, mod_steps[0])

        def gates(a):
            dve.wait_ge(ada_used, 24 * a + 24)
            V.tensor_tensor(mod[:, a, 16:24], mod[:, a, 16:24], par[:, PCOL["ada_b"] + 24 * a + 16:PCOL["ada_b"] + 24 * a + 24], ALU.add).then_inc(mod_step, 1)
            mod_steps[0] += 1
            dve.wait_ge(mod_step, mod_steps[0])

        def modulation(a):
            shift_and_scale(a)
            gates(a)

        def add_square(name, m, r):
            dve.wait_ge(sq_ready, m + (SQ[name] + 1))
            dve.wait_ge(ssq_ready, m + SSQ[name])
            V.tensor_tensor(ssq[:], ssq[:], sq[:, r], ALU.add).then_inc(ssq_ready, 1)

        def residual(gate, squares, tiles=2, permuted=False):
            def evacuate(j, b, i):
                for r in range(tiles):
                    m = i * tiles + r
                    dve.wait_ge(done[b], done_value(j, r if tiles == 2 else 1))
                    src, dst = ps[:, 2 * b + r], row(h, m)
                    if permuted:
                        src, dst = src.rearrange("p (j k) -> p k j", j=TC), dst.rearrange("p (k j) -> p k j", j=TC)
                    if gate is None:
                        ins = V.tensor_tensor(dst, src, dst, ALU.add)
                    else:
                        ins = V.scalar_tensor_tensor(dst, src, col(mod[:, gate], m + 2 * DT), dst, ALU.mult, ALU.add)
                    ins.then_inc(evac[b], 2 // tiles)
                if squares:
                    for r in range(tiles):
                        add_square(squares, i * tiles + r, r if tiles == 2 else b)
            return evacuate

        def norm(name, src, scale, shift=None, hi=None, lo=None, dst=None):
            i, n, x0 = NIDX[name], dict(NORMS)[name], XTILE[name]
            dve.wait_ge(std_ready, i + 1)
            V.reciprocal(rcol[:], stdc[:]).then_inc(rstd_ready, 1)
            if name != "out":
                V.memset(ssq[:], 0.0).then_inc(ssq_ready, 1)

            def low(m):
                dve.wait_ge(xh, x0 + m + 1)
                if shift:
                    V.scalar_tensor_tensor(lo[:, m], norm_buf(m), shift(m), f32(hi[:, m]), ALU.add, ALU.subtract).then_inc(xl, 1)
                else:
                    V.tensor_tensor(lo[:, m], norm_buf(m), f32(hi[:, m]), ALU.subtract).then_inc(xl, 1)

            dve.wait_ge(rstd_out, i + 1)
            for m in range(n):
                to = norm_buf(m) if hi is not None else dst(m)
                V.scalar_tensor_tensor(to, src(m), scale(m), ps[:, 7], ALU.mult, ALU.mult).then_inc(norm_t, 1)
                if hi is not None and m:
                    low(m - 1)
            if hi is not None:
                low(n - 1)

        def ada_norm(name, a):
            norm(name, lambda m: h[:, m], lambda m: gain[:, a, m:m + 1], lambda m: mod[:, a, m:m + 1], xn_hi, xn_lo)

        def gated(name, src, dst_hi, dst_lo):
            base = GATED[name]

            def evacuate(j, b, i):
                if base + i:
                    dve.wait_ge(gm_lo, base + 2 * i)
                for r in range(2):
                    dve.wait_ge(evac[b], done_value(j, r))
                    V.tensor_tensor(hn[:, r], src[:, 2 * i + r], nt[:, r], ALU.mult).then_inc(gm_prod, 1)
                for r in range(2):
                    dve.wait_ge(gm_hi, base + 2 * i + r + 1)
                    V.tensor_tensor(dst_lo[:, 2 * i + r], hn[:, r], f32(dst_hi[:, 2 * i + r]), ALU.subtract).then_inc(gm_lo, 1)
            return evacuate

        def attention(kind, heads, scale=1.0):
            n, base = 4 * heads, UNIT[kind]

            def first(u):
                g, hd, i = base + u, u // 4, u % 4
                w = (i + 1) * P
                z, p, st = ps[:, 4 + g % 3, 0:w], pw[:, g % 3, 0:w], stat[:, g % 4]
                if kind == "fox":
                    dve.wait_ge(s_done, g + 1)
                    if i == 0:
                        dve.wait_ge(bias_in[hd % 2], 16 * (hd // 2 + 1))
                    if g >= 3:
                        dve.wait_ge(tr_done, g - 2)
                    V.tensor_tensor_reduce(p, z, fbias[:, hd % 2, 0:w], 1.0, -3e38, ALU.add, ALU.max, st[:, 0:1]).then_inc(s_free, 1)
                    dve.wait_ge(s_free, g + 1)
                    V.tensor_scalar(st[:, 1:2], st[:, 0:1], -1.0, None, ALU.mult).then_inc(nm_done, 1)
                elif kind == "mla":
                    dve.wait_ge(s_done, g + 1)
                    V.tensor_reduce(st[:, 0:1], z, AX.X, ALU.max).then_inc(mx_done, 1)
                    dve.wait_ge(mx_done, u + 1)
                    V.tensor_scalar(st[:, 1:2], st[:, 0:1], -scale, None, ALU.mult).then_inc(nm_done, 1)
                else:
                    t = hn[:, g % 2, 0:w]
                    dve.wait_ge(ln_done, u + 1)
                    V.scalar_tensor_tensor(t, z, 0.0, nt[:, g % 2, 0:w], ALU.max, ALU.add).then_inc(sp_done, 1)
                    dve.wait_ge(sp_done, u + 1)
                    dve.wait_ge(tr_done, g - 2)
                    V.tensor_tensor_scan(p[:, ::-1], ones[:, 0:1].to_broadcast([P, w]), t[:, ::-1], 0.0, ALU.mult, ALU.add).then_inc(sc_done, 1)
                    dve.wait_ge(sc_done, u + 1)
                    V.tensor_tensor(p, z, p, ALU.subtract).then_inc(s_free, 1)

            def normalise(u):
                g, w = base + u, (u % 4 + 1) * P
                p, st = pw[:, g % 3, 0:w], stat[:, g % 4]
                if kind == "fox":
                    dve.wait_ge(exp_done, u + 1)
                else:
                    dve.wait_ge(s_free, g + 1)
                k = u + (4 * HEADS if kind == "mla" else 0)
                V.reciprocal(st[:, 3:4], st[:, 2:3]).then_inc(rc_done, 1)
                dve.wait_ge(rc_done, k + 1)
                V.tensor_scalar(p, p, st[:, 3:4], None, ALU.mult).then_inc(w_ready, 1)

            for s in range(n + 5):
                if s < n:
                    first(s)
                if kind != "sb" and 1 <= s < n + 1:
                    normalise(s - 1)
                if kind == "fox" and (s >= 12 and s % 8 == 4 or s == n + 4):
                    pair = (s - 5) // 8 if s < n + 4 else heads // 2 - 1
                    dve.wait_ge(o_hi, pair + 1)
                    V.tensor_tensor(xn_lo[:, pair], ps[:, (1, 2)[pair % 2]], f32(xn_hi[:, pair]), ALU.subtract).then_inc(o_done, 1)

        V.memset(ones[:], 1.0).then_inc(init, 1)
        V.memset(epsc[:], EPS).then_inc(init, 1)
        V.memset(Bz[:], 0.0).then_inc(init, 1)
        V.memset(ssq[:], 0.0).then_inc(ssq_ready, 1)

        steps = [0]

        def link(ins):
            steps[0] += 1
            ins.then_inc(s5_step, 1)
            dve.wait_ge(s5_step, steps[0])

        lre, lim = lam[:, 0], lam[:, 1]
        q = lambda i: q5[:, i]
        TT, TS, STT = V.tensor_tensor, V.tensor_scalar, V.scalar_tensor_tensor
        TWO_PI = 2 * np.pi
        c1 = 6.28125
        c2 = float(np.float32(np.floor((TWO_PI - c1) * 2 ** 21) / 2 ** 21))
        c3 = float(TWO_PI - c1 - c2)
        MAGIC = float(1.5 * 2 ** 23)
        dve.wait_ge(in_s5, 32)
        dve.wait_ge(s5_act, 1)
        link(TT(q(1), lre, q(0), ALU.mult))
        link(TT(q(2), lim, q(0), ALU.mult))
        link(TS(q(3), q(2), 1 / TWO_PI, MAGIC, ALU.mult, ALU.add))
        link(TS(q(3), q(3), -MAGIC, None, ALU.add))
        link(STT(q(4), q(3), -c1, q(2), ALU.mult, ALU.add))
        link(STT(q(4), q(3), -c2, q(4), ALU.mult, ALU.add))
        link(STT(q(4), q(3), -c3, q(4), ALU.mult, ALU.add))
        PI_IN = float(np.nextafter(np.float32(np.pi), np.float32(0)))
        TS(q(4), q(4), PI_IN, -PI_IN, ALU.min, ALU.max).then_inc(s5_arg, 1)
        dve.wait_ge(s5_act, 4)
        link(TT(q(8), q(7), q(7), ALU.mult))
        link(TS(q(8), q(8), -2.0, 1.0, ALU.mult, ALU.add))
        link(TT(q(9), q(5), q(8), ALU.mult))
        link(TT(q(10), q(5), q(6), ALU.mult))
        link(TS(q(11), q(9), -1.0, None, ALU.add))
        link(TT(q(16), lre, lre, ALU.mult))
        link(TT(q(17), lim, lim, ALU.mult))
        link(TT(q(12), q(16), q(17), ALU.add))
        link(V.reciprocal(q(13), q(12)))
        link(TT(q(16), q(11), lre, ALU.mult))
        link(TT(q(17), q(10), lim, ALU.mult))
        link(TT(q(16), q(16), q(17), ALU.add))
        link(TT(q(14), q(16), q(13), ALU.mult))
        link(TT(q(16), q(10), lre, ALU.mult))
        link(TT(q(17), q(11), lim, ALU.mult))
        link(TT(q(16), q(16), q(17), ALU.subtract))
        link(TT(q(25), q(16), q(13), ALU.mult))
        link(TS(q(24), q(25), -1.0, None, ALU.mult))
        link(TS(q(20), q(10), -1.0, None, ALU.mult))
        link(V.tensor_copy(q(21), q(10)))
        link(V.tensor_copy(q(22), q(20)))
        wide = [P, 2, GP, CG]
        one = lambda i: q5[:, i].unsqueeze(1).unsqueeze(3).to_broadcast(wide)
        two = lambda i: q5[:, i:i + 2].unsqueeze(3).to_broadcast(wide)

        def complex_times(dst, src, swapped, re, im):
            link(TT(dst, src, re, ALU.mult))
            link(TT(t5[:], swapped, im, ALU.mult))
            link(TT(dst, dst, t5[:], ALU.add))

        link(V.tensor_copy(CL[:, 0, :, 0], bc[:, 2]))
        link(TS(CL[:, 1, :, 0], bc[:, 3], -1.0, None, ALU.mult))
        complex_times(BW[:, :, :, :, TC - 1], bc[:, 0:2], bc[:, 1::-1], one(14), two(24))
        link(TT(q(16), q(5), q(5), ALU.mult))
        link(TT(coef[:], q(16), q(16), ALU.mult))
        V.sem_inc(cl_start, 1)
        c_s, s_s, c_n, s_n = (turn[:, i] for i in range(4))
        link(TT(q(16), q(8), q(8), ALU.mult))
        link(TT(q(17), q(6), q(6), ALU.mult))
        link(TT(c_s, q(16), q(17), ALU.subtract))
        link(STT(s_s, q(6), 2.0, q(8), ALU.mult, ALU.mult))
        link(TT(q(16), c_s, c_s, ALU.mult))
        link(TT(q(17), s_s, s_s, ALU.mult))
        link(STT(s_s, s_s, 2.0, c_s, ALU.mult, ALU.mult))
        link(TT(c_s, q(16), q(17), ALU.subtract))

        for m in range(DT):
            add_square("mix0", m, m % 2)
        dve.wait_ge(in_const, 48)
        dve.wait_ge(c_ready, 1)
        ada(0, 8)
        ada(8, 4)
        complex_times(BW[:, :, :, :, TC - 2], BW[:, :, :, :, TC - 1], BW[:, ::-1, :, :, TC - 1], one(9), two(20))
        ada(12, 4)
        shift_and_scale(0)
        split(0, 0)
        ada_norm("mix0", 0)
        split(0, 1)
        for j in range(TC - 3, -1, -1):
            complex_times(BW[:, :, :, :, j], BW[:, :, :, :, j + 1], BW[:, ::-1, :, :, j + 1], one(9), two(20))
        dve.wait_ge(init, 3)
        link(V.tensor_copy(Bz[0:64, :, :, 0], BW[0:64, :, :, :, TC - 1]))
        V.tensor_copy(Bz[64:P, :, :, 1], BW[64:P, :, :, :, TC - 1]).then_inc(bw_ready, 1)
        split(1, 0)
        split(1, 1)
        dve.wait_ge(kt_out, 4)
        TT(Kt[0:32, :, 0], Kt[0:32, :, 0], dd[:], ALU.add).then_inc(kt_sum, 1)

        def normalised(c, s):
            link(TT(c_n, c, c, ALU.mult))
            link(TT(s_n, s, s, ALU.mult))
            link(TT(c_n, c_n, s_n, ALU.add))
            link(TS(c_n, c_n, -0.5, 1.5, ALU.mult, ALU.add))
            link(TT(c, c, c_n, ALU.mult))
            link(TT(s, s, c_n, ALU.mult))

        normalised(c_s, s_s)
        dve.wait_ge(mt_in, 128)
        dve.wait_ge(turned_out, 16)
        V.memset(rot[:, 0, :, 0:1], 1.0)
        V.memset(rot[:, 1, :, 0:1], 0.0)
        V.tensor_copy(rot[:, 0, :, 1], c_s)
        link(V.tensor_copy(rot[:, 1, :, 1], s_s))
        for n, first, count in ((1, 1, 1), (2, 1, 2), (4, 1, 4), (8, 1, 8), (16, 1, 16), (32, 1, 32), (64, 1, 32), (64, 33, 31)):
            if n == 8:
                normalised(rot[:, 0, :, 8], rot[:, 1, :, 8])
            src, dst = rot[:, :, :, first:first + count], rot[:, :, :, n + first:n + first + count]
            c_k, s_k = (rot[:, i:i + 1, :, n:n + 1].to_broadcast([P, 2, GP, count]) for i in range(2))
            TT(dst, src, c_k, ALU.mult)
            link(TT(rtmp[:, :, :, 0:count], src[:, ::-1], s_k, ALU.mult))
            TT(dst[:, 0], dst[:, 0], rtmp[:, 0, :, 0:count], ALU.subtract)
            link(TT(dst[:, 1], dst[:, 1], rtmp[:, 1, :, 0:count], ALU.add))
        V.sem_inc(rot_ready, 1)
        split(2, 0)

        for m in range(DT):
            b_in = ps[:, m % 2 * 2:m % 2 * 2 + 2].rearrange("p r (g k) -> p r g k", g=4)
            c_k, s_k = (rot[:, i:i + 1, 4 * m:4 * m + 4].to_broadcast([P, 2, 4, NCK]) for i in range(2))
            x = X[:, m % 2]
            dve.wait_ge(x_done, m + 1)
            if m:
                dve.wait_ge(x_ready, m)
            TT(t1[:], b_in, c_k, ALU.mult)
            TT(t2[:], b_in[:, ::-1], s_k, ALU.mult).then_inc(x_used, 1)
            dve.wait_ge(x_used, m + 1)
            TT(t1[:, 0], t1[:, 0], t2[:, 0], ALU.add)
            link(TT(t1[:, 1], t1[:, 1], t2[:, 1], ALU.subtract))
            for ri in range(2):
                for g in range(4):
                    ins = V.tensor_tensor_scan(t2[:, ri, g], coef[:, 4 * m + g:4 * m + g + 1].to_broadcast([P, NCK]), t1[:, ri, g],
                                               0.0, ALU.mult, ALU.add)
            link(ins)
            if m >= 2:
                dve.wait_ge(y_done, m - 1)
            TT(t1[:], t2[:], c_k, ALU.mult)
            link(TT(x, t2[:, ::-1], s_k, ALU.mult))
            TT(x[:, 0], t1[:, 0], x[:, 0], ALU.subtract)
            TT(x[:, 1], t1[:, 1], x[:, 1], ALU.add).then_inc(x_ready, 1)
        dve.wait_ge(x_ready, DT)
        for m in range(DT):
            dve.wait_ge(gh_done, m + 1)
            if m >= 4:
                dve.wait_ge(y_done, 7 if m < 6 else 8)
            TT(xn_lo[:, m], g32[:, m], f32(xn_hi[:, m]), ALU.subtract).then_inc(gl_done, 1)
        glu = gated("s5_glu", g32, zg_hi, zg_lo)

        def glu_and_ada(j, b, i):
            glu(j, b, i)
            ada(16 + 4 * i, 4)

        layer("s5_glu", glu_and_ada)
        gates(0)
        into_h = residual(0, "ffn0", permuted=True)

        def out_and_ada(j, b, i):
            into_h(j, b, i)
            ada(32 + 4 * i, 4)

        layer("s5_out", out_and_ada)
        modulation(1)

        for l in (0, 1):
            if l:
                ada(24 * 2 + 22, 2)
                dve.wait_ge(mod_copy, 22)
                modulation(2)
                ada_norm("mix1", 2)
                dve.wait_ge(fw_hi, 1)
                TT(fwf_lo[:], fwf[:], f32(fwf_hi[:]), ALU.subtract).then_inc(fw_lo, 1)
                for n, name in enumerate(("fox_q", "fox_k", "fox_v")):
                    layer(name, lambda j, b, i: ada(72 + 8 * n + 2 * i, 2))
                    if n == 0:
                        dve.wait_ge(f_done, 1)
                        TS(fg[:, 0], ps[0:HEADS, 6], pcol("fox_b", 0, slice(0, HEADS)), -1.0, ALU.add, ALU.mult).then_inc(f_dve, 1)
                        dve.wait_ge(f_act, 3)
                        STT(fg[:, 1], fg[:, 0], 0.0, fg[:, 2], ALU.max, ALU.add).then_inc(f_dve, 1)
                        dve.wait_ge(f_dve, 2)
                        V.tensor_tensor_scan(fg[:, 3], ones[0:HEADS, 0:1].to_broadcast([HEADS, S]), fg[:, 1], 0.0, ALU.mult, ALU.add).then_inc(f_dve, 1)
                attention("fox", HEADS)
                layer("fox_out", residual(2, "ffn1"))
                modulation(3)
            ada_norm(f"ffn{l}", 2 * l + 1)
            tiles = sum(HALVES) * l
            for hf, nf in enumerate(HALVES):
                for r in range(2):
                    V.memset(apad[r][:, 0:2], 0.0).then_inc(pad_ready, 1)
                dve.wait_ge(pad_ready, 4 * l + 2 * hf + 2)
                with dve.Fori(0, nf // 2) as i:
                    j = i + FIRST[f"up{l}{hf}"] // 2
                    f = i * 2 + tiles
                    of = i * 2 + (tiles - sum(HALVES) * l)
                    split(j, 1)
                    for r in range(2):
                        tap = lambda t: col(par, of + (conv_par(l, t, r)))
                        dve.wait_ge(evac[0], done_value(j, r))
                        TS(cv[:, r], apad[r][:, 0:S], tap(0), col(par, of + (PCOL["conv_b"] + l * FT + r)), ALU.mult, ALU.add).then_inc(cv_step, 1)
                        dve.wait_ge(cv_step, f * 2 + (2 * r + 1))
                        STT(cv[:, r], apad[r][:, 1:S + 1], tap(1), cv[:, r], ALU.mult, ALU.add).then_inc(cv_step, 1)
                        dve.wait_ge(cv_step, f * 2 + (2 * r + 2))
                        STT(cv[:, r], apad[r][:, 2:S + 2], tap(2), cv[:, r], ALU.mult, ALU.add).then_inc(conv_done, 1)
                    split(j + 1, 0)
                    for r in range(2):
                        dve.wait_ge(silu_done, f + (r + 1))
                        dve.wait_ge(done[1], done_value(j, r))
                        TT(prod[:, r], ps[:, 2 + r], sil[:, r], ALU.mult).then_inc(evac[1], 1)
                    for r in range(2):
                        dve.wait_ge(acth, f + (r + 1))
                        TT(row(act_lo, i * 2 + r), prod[:, r], f32(row(act_hi, i * 2 + r)), ALU.subtract).then_inc(actl, 1)
                    if l == 0:
                        for b in range(2):
                            ada_loop(i * 2 + (48 + sum(HALVES[:hf])), b)
                tiles += nf
                squares = (f"mix1" if l == 0 else "final") if hf == 1 else None
                with dve.Fori(0, DT // 2) as i:
                    for b in range(2):
                        j = i + FIRST[f"down{l}{hf}"] // 2
                        split(j + b, 1 - b)
                        residual(2 * l + 1, squares, 1)(j, b, i * 2 + b)

        norm("final", lambda m: h[:, m], lambda m: pcol("final_g", m), dst=lambda m: h[:, m])
        for m in range(DT):
            add_square("in2", m, m % 2)
        norm("in2", lambda m: h[:, m], lambda m: pcol("norm_in_g", m), hi=xn_hi, lo=xn_lo)
        layer("sb_q")
        layer("sb_k")
        layer("sb_v")
        attention("sb", H2)

        turns = [0]

        def rotate(dst, b, r, inc):
            bank = ps[:, 2 * b + r]
            TT(dst, bank[64:QK], ropt[64:QK], ALU.mult).then_inc(rope_t, 1)
            TT(rt[64:QK], bank[QK:P], ropt[QK:P], ALU.mult).then_inc(evac[b], 1)
            turns[0] += 1
            dve.wait_ge(rope_t, turns[0])
            dve.wait_ge(evac[b], inc)
            return TT(dst, dst, rt[64:QK], ALU.add)

        def shared_key(j, b, i):
            if i == 2:
                dve.wait_ge(in_rope, 16)
                dve.wait_ge(done[b], done_value(j, 1))
                dve.wait_ge(evac[b], done_value(j, 0))
                rotate(kr[64:QK], b, 1, done_value(j, 1)).then_inc(kr_ready, 1)

        layer("mla_c", shared_key)
        for m in range(3):
            add_square("cq", m, m % 2)
        norm("cq", lambda m: cc[:, m], lambda m: pcol("q_norm_g", m), hi=cq_hi, lo=cq_lo)
        for m in range(2):
            add_square("ckv", m, m % 2)
        norm("ckv", lambda m: cc[:, 3 + m], lambda m: pcol("kv_norm_g", m), hi=ck_hi, lo=ck_lo)

        def query_rope(j, b, i):
            for r in range(2):
                dve.wait_ge(mq_nope, 2 * i + r + 1)
                if i + r:
                    dve.wait_ge(mq_ready, 2 * i + r)
                rotate(m_q[64:QK, 2 * i + r], b, r, done_value(j, r)).then_inc(mq_ready, 1)

        layer("mla_q", query_rope)
        layer("mla_k")
        layer("mla_v")
        attention("mla", H2, QK ** -0.5)
        layer("gate_sb", gated("gate_sb", o_sb, osb_hi, osb_lo))
        layer("gate_mla", gated("gate_mla", o_mla, omla_hi, omla_lo))
        for m in range(4):
            for name, tmp in (("sb", nt), ("mla", hn)):
                def branch_out(j, b, i):
                    for r in range(2):
                        dve.wait_ge(evac[1 - b], done_value(j if b else j - 1, r))
                        dve.wait_ge(done[b], done_value(j, r))
                        TT(tmp[:, r], ps[:, 2 * b + r], tmp[:, r], ALU.mult).then_inc(evac[b], 1)
                layer(f"g{0 if name == 'sb' else 1}_{m}")
                layer(f"o{name}_{m}", branch_out)
            j, b = last_of(f"omla_{m}")
            dve.wait_ge(evac[b], done_value(j, 1))
            for r in range(2):
                TT(sq[:, r], nt[:, r], hn[:, r], ALU.add).then_inc(m_sum, 1)
            for r in range(2):
                dve.wait_ge(m_hi, 2 * m + r + 1)
                TT(mg_lo[:, 2 * m + r], sq[:, r], f32(mg_hi[:, 2 * m + r]), ALU.subtract).then_inc(m_lo, 1)
        layer("mix_out", residual(None, "out"))
        norm("out", lambda m: h[:, m], lambda m: pcol("norm_f_g", m), dst=lambda m: fin[:, m])


def _chunks(w, name):
    kt, cols, n = KT[name], COLS[name], COUNT[name]
    return np.ascontiguousarray(w.reshape(kt, P, n, cols).transpose(2, 1, 0, 3)).reshape(-1)


def _tiles(v):
    return np.ascontiguousarray(v.reshape(-1, P).T)


def _pairs(a):
    a = a.reshape(GP, 2, ST, *a.shape[2:])
    return np.ascontiguousarray(a.transpose(1, 2, 0, *range(3, a.ndim))).reshape(P, GP, *a.shape[3:])


def _constants():
    i, j = np.arange(P)[:, None], np.arange(P)[None, :]
    m = np.zeros((P, 4, P), np.float32)
    m[:, 0] = i == j
    m[:, 1] = np.where(j <= i, 0, NEG)
    m[:, 2] = np.where(j < i, 0, NEG)
    m[:, 3] = np.where(j // 64 <= i // 64, 0, NEG)
    half = ROPE // 2
    freq = (np.float32(10000.0) ** (-np.arange(half, dtype=np.float32) / np.float32(half))).astype(np.float32)
    ang = (np.arange(S, dtype=np.float32)[:, None] * freq[None, :]).astype(np.float32)
    co, si = np.cos(ang).T.astype(np.float32), np.sin(ang).T.astype(np.float32)
    return m, np.concatenate([co, co, -si, si], 0)


def kernel(**inputs):
    import concourse.bacc as bacc
    from concourse.bass_utils import run_bass_kernel_spmd

    a = {k: np.asarray(v) for k, v in inputs.items()}
    half = ROPE // 2
    swap = np.r_[half:ROPE, 0:half]
    w = {"s5_in": a["s5_w_in"][0], "s5_glu": a["s5_w_glu"][0], "s5_out": a["s5_w_out"][0]}
    fox = a["fox_w_in"][0]
    w.update(fox_q=fox[:, 0:D], fox_k=fox[:, D:2 * D], fox_v=fox[:, 2 * D:3 * D], fox_out=a["fox_w_out"][0])
    F = FT * P
    for l in (0, 1):
        for hf, nf in enumerate(HALVES):
            f0 = sum(HALVES[:hf]) * P
            up = a["ffn_w_up"][l]
            both = np.stack([up[:, f0:f0 + nf * P].reshape(D, nf // 2, 256),
                             up[:, F + f0:F + f0 + nf * P].reshape(D, nf // 2, 256)], 2)
            w[f"up{l}{hf}"] = both.reshape(D, nf * 256)
            w[f"down{l}{hf}"] = a["ffn_w_down"][l][f0:f0 + nf * P]
    wi = a["w_in_2"][0]
    w.update(sb_q=wi[:, 0:512], sb_k=wi[:, 512:1024], sb_v=wi[:, 1024:1536], gate_sb=wi[:, 1536:2048])
    r0 = 2048 + QL + KVL
    rope_cols = wi[:, r0:r0 + ROPE]
    w["mla_c"] = np.concatenate([wi[:, 2048:r0], np.zeros((D, 64), wi.dtype), rope_cols, rope_cols[:, swap]], 1)
    w["gate_mla"] = wi[:, r0 + ROPE:r0 + ROPE + 512]
    gl = wi[:, r0 + ROPE + 512:]
    q = a["w_q_up_2"][0].reshape(QL, H2, QK)
    w["mla_q"] = np.concatenate([q, q[:, :, 64:][:, :, swap]], 2).reshape(QL, H2 * P)
    kv = a["w_kv_up_2"][0].reshape(KVL, H2, P)
    w["mla_k"], w["mla_v"] = kv[:, :, 0:64].reshape(KVL, 512), kv[:, :, 64:].reshape(KVL, 512)
    for m in range(4):
        c = slice(256 * m, 256 * (m + 1))
        w[f"g0_{m}"], w[f"g1_{m}"] = gl[:, c], gl[:, D:][:, c]
        w[f"osb_{m}"], w[f"omla_{m}"] = a["w_o_sb_2"][0][:, c], a["w_o_mla_2"][0][:, c]
    w["mix_out"] = a["w_out_2"][0]
    fox_b = np.zeros((P, 1), np.float32)
    fox_b[0:HEADS, 0] = a["fox_b_f"][0]
    masks, rope = _constants()
    cmat = [_pairs(a[n][0].transpose(0, 2, 1)) for n in ("s5_c_re", "s5_c_im")]
    s5d = np.zeros((2, CG, GP, CG), np.float32)
    for i in range(CG):
        s5d[:, i, :, i] = a["s5_d"].reshape(GP, 2, CG)[:, :, i].T
    s5d = s5d.reshape(2 * CG, GP, CG)
    arrays = {
        "weights": np.concatenate([_chunks(w[name], name) for name, *_ in LAYERS]),
        "ada_w": np.ascontiguousarray(a["ada_w"].reshape(4, D, 24, P).transpose(0, 2, 3, 1)).reshape(96, P, D),
        "xT": np.ascontiguousarray(a["x"][0].T),
        "c": a["c"],
        "params": np.concatenate([_tiles(a[n]) for n in ("norm_g", "ada_b", "final_g", "norm_in_g_2", "b_gate_2",
                                                        "q_norm_g_2", "kv_norm_g_2", "norm_f_g_2", "ffn_conv_w", "ffn_conv_b")] + [fox_b], 1),
        "consts": masks,
        "rope": rope,
        "s5p": np.stack([_pairs(a["s5_lam_re"][0]), _pairs(a["s5_lam_im"][0]),
                         _pairs(np.repeat(a["s5_log_dt"][0][:, None], ST, 1))], 1),
        "s5bc": np.stack([_pairs(a["s5_b_re"][0]), _pairs(a["s5_b_im"][0]), *cmat], 1),
        "s5d": s5d,
        "fox_f": np.ascontiguousarray(fox[:, 3 * D:].reshape(DT, P, HEADS).transpose(1, 0, 2)),
    }
    arrays = {f"in_{k}": np.ascontiguousarray(v) for k, v in arrays.items()}
    nc = bacc.Bacc("TRN2", target_bir_lowering=False, num_devices=1)
    args = [nc.dram_tensor(k, v.shape, mybir.dt.from_np(v.dtype), kind="ExternalInput").ap() for k, v in arrays.items()]
    out = nc.dram_tensor("out_T", (D, S), F32, kind="ExternalOutput").ap()
    build(nc, *args, out)
    r = run_bass_kernel_spmd(nc, [arrays], core_ids=[0])
    return np.ascontiguousarray(r.results[0]["out_T"].T)[None]
```

```python
from contextlib import ExitStack

import numpy as np
import concourse.bass as bass
from concourse import mybir

F32 = mybir.dt.float32
F32R = mybir.dt.float32r
ALU = mybir.AluOpType
ACT = mybir.ActivationFunctionType
AX = mybir.AxisListType

P = 128
S = 512
D = 1024
DT = D // P
EPS = 1e-6
NEG = -1e30

FT = 2816 // P
HALVES = (12, 10)
GRP, CG, ST = 64, 16, 64
GP = GRP // 2
TC = 4
NCK = S // TC
HEADS, HD = 16, 64
H2 = 8
ROPE, QK = 32, 96
QL, KVL = 384, 256
QBLK = S // P

LAYERS = [("s5_in", 8, 256, 4), ("s5_glu", 8, 256, 4), ("s5_out", 8, 256, 4)]
for _l in (0, 1):
    if _l == 1:
        LAYERS += [("fox_q", 8, 256, 4), ("fox_k", 8, 256, 4), ("fox_v", 8, 256, 4), ("fox_out", 8, 256, 4)]
    for _h, _n in enumerate(HALVES):
        LAYERS += [(f"up{_l}{_h}", 8, 256, _n), (f"down{_l}{_h}", _n, 128, 8)]
LAYERS += [("sb_q", 8, 256, 2), ("sb_k", 8, 256, 2), ("sb_v", 8, 256, 2), ("mla_c", 8, 256, 3),
           ("mla_q", 3, 256, 4), ("mla_k", 2, 256, 2), ("mla_v", 2, 256, 2),
           ("gate_sb", 8, 256, 2), ("gate_mla", 8, 256, 2)]
for _m in range(4):
    LAYERS += [(f"g0_{_m}", 8, 256, 1), (f"osb_{_m}", 4, 256, 1), (f"g1_{_m}", 8, 256, 1), (f"omla_{_m}", 4, 256, 1)]
LAYERS += [("mix_out", 8, 256, 4)]
FIRST, OFFSET, KT, COLS, COUNT = {}, {}, {}, {}, {}
_n = _o = 0
for _name, _kt, _c, _cnt in LAYERS:
    FIRST[_name], OFFSET[_name], KT[_name], COLS[_name], COUNT[_name] = _n, _o, _kt, _c, _cnt
    _n += _cnt
    _o += _cnt * P * _kt * _c
N_CHUNKS, W_WORDS = _n, _o
CREDIT = 2

PCOL = {}
_n = 0
for _name, _w in (("norm_g", 32), ("ada_b", 96), ("final_g", 8), ("norm_in_g", 8), ("b_gate", 16),
                  ("q_norm_g", 3), ("kv_norm_g", 2), ("norm_f_g", 8), ("conv_w", 6 * FT), ("conv_b", 2 * FT), ("fox_b", 1)):
    PCOL[_name] = _n
    _n += _w
N_PCOL = _n

NORMS = [("mix0", 8), ("ffn0", 8), ("mix1", 8), ("ffn1", 8), ("in2", 8), ("final", 8), ("cq", 3), ("ckv", 2), ("out", 8)]
SUMS = [(n, t) for n, t in NORMS if n not in ("final", "ckv")]
NIDX = {n: i for i, (n, _) in enumerate(SUMS)}
NTILE = {n: sum(t for _, t in NORMS[:i]) for i, (n, _) in enumerate(NORMS)}
SSQ = {n: sum(t + 1 for _, t in SUMS[:i]) + 1 for i, (n, _) in enumerate(SUMS)}
SQ = {n: sum(t for _, t in SUMS[:i]) for i, (n, _) in enumerate(SUMS)}
SECOND = {"in2": (0, DT), "cq": (DT, 2)}


def done_value(j, r):
    return j * 2 + (CREDIT + r + 1)


def row(t, m):
    return t[:, m] if isinstance(m, int) else t[:, bass.ds(m, 1)].rearrange("p o n -> p (o n)")


def col(t, m):
    return t[:, m:m + 1] if isinstance(m, int) else t[:, bass.ds(m, 1)]


def build(nc, weights, ada_w, xT, c, params, consts, rope, s5p, s5bc, s5d, fox_f, out):
    with ExitStack() as ctx:
        build_in(ctx, nc, weights, ada_w, xT, c, params, consts, rope, s5p, s5bc, s5d, fox_f, out)



XTILE = {n: sum(t for m, t in NORMS[:i] if m not in ("final", "out")) for i, (n, _) in enumerate(NORMS)}
UNIT = {"fox": 0, "sb": 4 * HEADS, "mla": 4 * HEADS + 4 * H2}
GATED = {"s5_glu": 0, "gate_sb": 8, "gate_mla": 12}


def build_in(ctx, nc, weights, ada_w, xT, c, params, consts, rope, s5p, s5bc, s5d, fox_f, out):
    place = [16512]

    def sb(name, shape, dt=F32):
        t = nc.alloc_sbuf_tensor_at(name, shape, dt, offset=place[0])
        place[0] += (int(np.prod(shape[1:])) * mybir.dt.size(dt) + 31) // 32 * 32
        return t

    def sem(name):
        return ctx.enter_context(nc.semaphore(name))

    h = sb("h", [P, DT, S])
    xn_at = place[0]
    xn_hi, xn_lo = sb("xn_hi", [P, DT, S], F32R), sb("xn_lo", [P, DT, S], F32R)
    raw, w_hi, w_lo = sb("raw", [P, 2, 2048]), sb("w_hi", [P, 2, 2048], F32R), sb("w_lo", [P, 2, 2048], F32R)
    ada_at = place[0]
    adaw = sb("adaw", [P, 2, D])
    cvec = sb("cvec", [P, D])
    ident = sb("ident", [P, P])
    cst16 = sb("cst16", [P, 4, P], mybir.dt.bfloat16)
    par = sb("par", [P, N_PCOL])
    mod = sb("mod", [P, 4, 24])
    gain = sb("gain", [P, 4, DT])
    ones = sb("ones", [P, P])
    dd, ssq = sb("dd", [32, GP, CG]), sb("ssq", [P, S])
    ssq2, stdc, rcol = sb("ssq2", [P, S]), sb("stdc", [P, 8]), sb("rcol", [P, 8])
    sq = sb("sq", [P, 2, S])
    nt_at = place[0]
    nt, hn = sb("nt", [P, 2, S]), sb("hn", [P, 2, S])
    stat = sb("stat", [P, 4, 4])
    coef = sb("coef", [P, GP])
    turn = sb("turn", [P, 4, GP])
    epsc, adat = sb("epsc", [P, 1]), sb("adat", [P, 2])
    arena = place[0]

    def put(name, address, shape, dt=F32):
        assert address + int(np.prod(shape[1:])) * 4 <= 229344, (name, arena)
        return nc.alloc_sbuf_tensor_at(name, shape, dt, offset=address)

    def at(name, kib, shape, dt=F32):
        return put(name, arena + int(kib * 1024), shape, dt)

    CL, Mt, Bm = at("CL", 0, [P, 2, GP, 5, CG]), at("Mt", 20, [P, GP, 64]), at("Bm", 28, [P, 2, GP, ST])
    BW, Bz = at("BW", 44, [P, 2, GP, CG, TC]), at("Bz", 20, [P, 2, GP, 2, CG])
    bc = put("bc", ada_at - 8192, [P, 4, GP, CG])
    Kt = put("Kt", nt_at, [P, GP, TC, CG])
    q5, lam = at("q5", 72, [P, 28, GP]), at("lam", 75.5, [P, 3, GP])
    t5, t5p = put("t5", ada_at, [P, 2, GP, CG]), at("t5p", 20, [P, 2, GP, CG])
    spare = [arena + 28 * 1024, arena + 36 * 1024, ada_at - 16384, ada_at]
    ada0 = [put(f"ada0_{g}", a, [P, 2, D]) for g, a in enumerate([xn_at + g * 8192 for g in range(4)] + spare)]
    cst = at("cst", 68, [P, 4, P])
    rot = at("rot", 44, [P, 2, GP, NCK])
    rtmp = put("rtmp", ada_at, [P, 2, GP, 32])
    U = put("U", xn_at, [P, GP, NCK])
    t1, t2 = put("t1", xn_at + 16384, [P, 2, 4, NCK]), put("t2", xn_at + 20480, [P, 2, 4, NCK])
    X = put("X", xn_at + 24576, [P, 2, 2, 4, NCK])
    yT = rot[:, 0].rearrange("p (m g) k -> p m (g k)", g=4)
    g32 = rot[:, 1].rearrange("p (m g) k -> p m (g k)", g=4)
    zg_hi, zg_lo = at("zg_hi", 0, [P, DT, S], F32R), at("zg_lo", 20, [P, DT, S], F32R)
    act_hi, act_lo = at("act_hi", 0, [P, 12, S], F32R), at("act_lo", 24, [P, 12, S], F32R)
    apad = [at(f"apad{r}", 48 + r * 2.0625, [P, S + 2]) for r in range(2)]
    cv, sil, prod = at("cv", 53, [P, 2, S]), at("sil", 57, [P, 2, S]), at("prod", 61, [P, 2, S])
    fq, fk, fv = at("fq", 0, [P, DT, S]), at("fk", 16, [P, DT, S]), at("fv", 32, [P, QBLK, D])
    fbias, fg, fwf = at("fbias", 48, [P, 2, S]), at("fg", 52, [HEADS, 4, S]), at("fwf", 60, [P, DT, HEADS])
    fwf_hi, fwf_lo = at("fwf_hi", 60.5, [P, DT, HEADS], F32R), at("fwf_lo", 61, [P, DT, HEADS], F32R)
    b_q, b_k, b_v = at("b_q", 0, [P, 4, S]), at("b_k", 8, [P, 4, S]), at("b_v", 16, [P, QBLK, S])
    o_sb, o_mla = at("o_sb", 24, [P, 4, S]), at("o_mla", 48, [P, 4, S])
    cc = at("cc", 32, [P, 5, S])
    cq_hi, cq_lo = at("cq_hi", 42, [P, 3, S], F32R), at("cq_lo", 48, [P, 3, S], F32R)
    ck_hi, ck_lo = at("ck_hi", 54, [P, 2, S], F32R), at("ck_lo", 58, [P, 2, S], F32R)
    kr, rt = at("kr", 62, [P, S]), at("rt", 66, [P, S])
    m_q, m_v, m_k = at("m_q", 0, [P, H2, S]), at("m_v", 16, [P, QBLK, S]), at("m_k", 32, [P, H2, S])
    ropt = put("ropt", ada_at, [P, S])
    osb_hi, osb_lo = at("osb_hi", 0, [P, 4, S], F32R), at("osb_lo", 8, [P, 4, S], F32R)
    omla_hi, omla_lo = at("omla_hi", 32, [P, 4, S], F32R), at("omla_lo", 40, [P, 4, S], F32R)
    mg_hi, mg_lo = at("mg_hi", 16, [P, DT, S], F32R), at("mg_lo", 56, [P, DT, S], F32R)
    fin = at("fin", 0, [P, DT, S])
    pw = at("pw", 68, [P, 4, S])
    pt = sq

    ps = ctx.enter_context(nc.psum_tensor("ps", [P, 8, S], F32))
    u_dram = nc.dram_tensor("u_dram", [D, S], F32).ap()
    y_dram = nc.dram_tensor("y_dram", [DT, 2, CG, TC, S], F32).ap()
    f_dram = nc.dram_tensor("f_dram", [HEADS, S], F32).ap()

    in_c, in_const, in_x, in_s5, in_fw = sem("in_c"), sem("in_const"), sem("in_x"), sem("in_s5"), sem("in_fw")
    in_rope = sem("in_rope")
    raw_in = [sem("raw_in0"), sem("raw_in1")]
    split_hi, split_lo = sem("split_hi"), sem("split_lo")
    done = [sem("done0"), sem("done1")]
    evac = [sem("evac0"), sem("evac1")]
    ada_in, ada_used, c_ready = [sem("ada_in0"), sem("ada_in1")], sem("ada_used"), sem("c_ready")
    mod_step, mod_copy = sem("mod_step"), sem("mod_copy")
    init, cst_ready = sem("init"), sem("cst_ready")
    sq_ready, ssq_ready, stat_done, std_ready = sem("sq_ready"), sem("ssq_ready"), sem("stat_done"), sem("std_ready")
    sq2_ready, ssq2_ready, var2_ready, rc2 = sem("sq2_ready"), sem("ssq2_ready"), sem("var2_ready"), sem("rc2")
    rstd_ready, rstd_out, norm_t, xh, xl = sem("rstd_ready"), sem("rstd_out"), sem("norm_t"), sem("xh"), sem("xl")
    s5_act, s5_arg, s5_step, bw_ready, cl_ready = sem("s5_act"), sem("s5_arg"), sem("s5_step"), sem("bw_ready"), sem("cl_ready")
    cl_start, cl_step, rot_ready, kt_sum = sem("cl_start"), sem("cl_step"), sem("rot_ready"), sem("kt_sum")
    turned, turned_out, kt_done, kt_out, mt_in = sem("turned"), sem("turned_out"), sem("kt_done"), sem("kt_out"), sem("mt_in")
    u_saved, u_in, x_done, x_used, x_ready = [sem(f"u_saved{n}") for n in range(4)], [sem(f"u_in{m}") for m in range(DT)], sem("x_done"), sem("x_used"), sem("x_ready")
    y_done, y_out, y_saved, y_in = sem("y_done"), sem("y_out"), [sem(f"y_saved{b}") for b in range(2)], [sem(f"y_in{m}") for m in range(DT)]
    ada0_in = [sem(f"ada0_in{g}") for g in range(8)]
    g_done, gh_done, gl_done = sem("g_done"), sem("gh_done"), sem("gl_done")
    gm_prod, gm_hi, gm_lo = sem("gm_prod"), sem("gm_hi"), sem("gm_lo")
    pad_ready, cv_step, conv_done, silu_done = sem("pad_ready"), sem("cv_step"), sem("conv_done"), sem("silu_done")
    acth, actl = sem("acth"), sem("actl")
    fw_hi, fw_lo = sem("fw_hi"), sem("fw_lo")
    f_done, f_dve, f_act, f_saved, bias_in = sem("f_done"), sem("f_dve"), sem("f_act"), sem("f_saved"), [sem("bias_in0"), sem("bias_in1")]
    s_done, s_free, mx_done, nm_done, exp_done, rc_done = (sem(n) for n in ("s_done", "s_free", "mx_done", "nm_done", "exp_done", "rc_done"))
    w_ready, tr_done, pt_done, pv_done, o_hi, o_done = (sem(n) for n in ("w_ready", "tr_done", "pt_done", "pv_done", "o_hi", "o_done"))
    abs_done, e_done, ln_done, sp_done, sc_done = sem("abs_done"), sem("e_done"), sem("ln_done"), sem("sp_done"), sem("sc_done")
    rope_t, kr_ready, mq_nope, mk_rope = sem("rope_t"), sem("kr_ready"), sem("mq_nope"), sem("mk_rope")
    mq_ready = sem("mq_ready")
    m_sum, m_hi, m_lo, out_saved = sem("m_sum"), sem("m_hi"), sem("m_lo"), sem("out_saved")

    def f32(ap):
        return ap.bitcast(F32)

    def pcol(name, i, p=slice(0, P)):
        return par[p, PCOL[name] + i:PCOL[name] + i + 1]

    LAG = {"fox": 0, "mla": 0, "sb": 2}

    def norm_buf(m):
        return (nt, hn)[m // 2 % 2][:, m % 2]

    def last_of(name):
        n = FIRST[name] + COUNT[name] - 1
        return n // 2, n % 2

    def size(n):
        for name, *_ in LAYERS:
            if FIRST[name] <= n < FIRST[name] + COUNT[name]:
                return KT[name] * COLS[name]

    def after_layer(eng, name, sems=evac):
        n = FIRST[name] + COUNT[name] - 1
        for m in (n, n - 1):
            eng.wait_ge(sems[m % 2], done_value(m // 2, 1))

    def conv_par(l, tap, f):
        return PCOL["conv_w"] + (l * 3 + tap) * FT + f

    block = ctx.enter_context(nc.Block())

    @block.sync
    def _(sp):
        sp.dma_start(lam[:], s5p).then_inc(in_s5, 16)
        sp.dma_start(bc[:], s5bc).then_inc(in_s5, 16)
        sp.dma_start(h[:], xT.rearrange("(m p) t -> p m t", p=P)).then_inc(in_x, 16)

        for g in range(8):
            sp.dma_start(ada0[g][:], ada_w[2 * g:2 * g + 2].rearrange("n p k -> p n k")).then_inc(ada0_in[g], 16)
            if g == 3:
                sp.dma_start(cst[:], consts).then_inc(in_const, 16)
                sp.dma_start(ident[:], consts[:, 0]).then_inc(in_const, 16)
                sp.dma_start(par[:], params).then_inc(in_const, 16)
                sp.dma_start(dd[:], s5d).then_inc(in_const, 16)
        at_chunk = [0]

        def chunk_source(name, i):
            words = KT[name] * COLS[name]
            all_of = weights[OFFSET[name]:OFFSET[name] + COUNT[name] * P * words]
            all_of = all_of.rearrange("(n p f) -> p n f", p=P, f=words)
            return row(all_of, i)

        def load(j, b, name, i):
            if not (isinstance(j, int) and j == 0):
                sp.wait_ge(split_lo, j * 2 + (b - 1))
            sp.dma_start(raw[:, b, 0:KT[name] * COLS[name]], chunk_source(name, i)).then_inc(raw_in[b], 16)

        def upto(name, count=None):
            stop = FIRST[name] + (COUNT[name] if count is None else count)
            for layer, *_ in LAYERS:
                n0, n1 = FIRST[layer], FIRST[layer] + COUNT[layer]
                if n1 <= at_chunk[0] or n0 >= stop:
                    continue
                if layer[:2] in ("up", "do") and n0 == at_chunk[0]:
                    with sp.Fori(0, COUNT[layer] // 2) as i:
                        for b in range(2):
                            load(i + n0 // 2, b, layer, i * 2 + b)
                    at_chunk[0] = n1
                    continue
                for n in range(max(n0, at_chunk[0]), min(n1, stop)):
                    load(n // 2, n % 2, layer, n - n0)
                    at_chunk[0] = n + 1

        upto("s5_in")

        def save_u(n):
            sp.wait_ge(evac[n % 2], done_value(n // 2, 1))
            sp.dma_start(u_dram[n * 256:(n + 1) * 256, :].rearrange("(m p) t -> p m t", p=P), (nt, hn)[n % 2][:]).then_inc(u_saved[n], 16)

        def load_u(m):
            src = u_dram[m * P:(m + 1) * P, :].rearrange("(g x) (j k) -> (x j) g k", x=32, j=TC)
            sp.dma_start(U[:, 4 * m:4 * m + 4], src).then_inc(u_in[m], 16)

        save_u(0)
        upto("s5_glu", 1)
        save_u(1)
        sp.wait_ge(kt_sum, 1)
        sp.wait_ge(init, 4)
        for q in range(2):
            for j in range(TC):
                sp.dma_start(Mt[q * 64 + j:(q + 1) * 64:TC, :, j * CG:64],
                             Kt[q * CG:(q + 1) * CG, :, 0:TC - j, :].rearrange("p g d c -> p g (d c)")).then_inc(mt_in, 16)
        save_u(2)
        after_layer(sp, "s5_in", done)
        for m in range(DT):
            if m == 6:
                save_u(3)
            sp.wait_ge(u_saved[m // 2], 16)
            load_u(m)
        upto("s5_glu", 2)
        for m in range(DT + 1):
            if m < DT:
                sp.wait_ge(y_out, m + 1)
                for q in range(2):
                    sp.dma_start(y_dram[m, q].rearrange("c j f -> j c f"), nt[q * 64:(q + 1) * 64, m % 2]).then_inc(y_saved[m % 2], 16)
            if m:
                sp.wait_ge(y_saved[(m - 1) % 2], 32 * ((m - 1) // 2 + 1))
                for g in range(4):
                    src = y_dram[m - 1, :, :, :, g * NCK:(g + 1) * NCK].rearrange("q c j k -> (q c) j k")
                    sp.dma_start(yT[g * 32:(g + 1) * 32, m - 1].rearrange("p (j k) -> p j k", j=TC), src).then_inc(y_in[m - 1], 16)
        upto("down01")
        upto("fox_q", 2)
        after_layer(sp, "down01")
        sp.dma_start(fwf[:], fox_f).then_inc(in_fw, 16)
        upto("fox_k", 2)
        sp.wait_ge(f_dve, 3)
        sp.dma_start(f_dram, fg[:, 3]).then_inc(f_saved, 16)
        upto("fox_out", 3)
        sp.wait_ge(f_saved, 16)
        for hd in range(HEADS):
            if hd >= 2:
                sp.wait_ge(s_free, 4 * (hd - 1))
            sp.dma_start(fbias[:, hd % 2], f_dram[hd:hd + 1, :].to_broadcast([P, S])).then_inc(bias_in[hd % 2], 16)
        upto("mix_out")
        sp.wait_ge(norm_t, NTILE["out"] + 8)
        sp.dma_start(out.rearrange("(m p) t -> p m t", p=P), fin[:]).then_inc(out_saved, 16)
        sp.wait_ge(out_saved, 16)

    @block.gpsimd
    def _(pool):
        pool.dma_start(cvec[:], c.to_broadcast([P, D])).then_inc(in_c, 16)
        pool.wait_ge(cl_start, 1)
        wide = [P, 2, GP, CG]
        one, two = q5[:, 9].unsqueeze(1).unsqueeze(3).to_broadcast(wide), q5[:, 21:23].unsqueeze(3).to_broadcast(wide)
        k_re, k_im = q5[:, 14].unsqueeze(1).unsqueeze(3).to_broadcast(wide), q5[:, 24:26].unsqueeze(3).to_broadcast(wide)
        steps = [(BW[:, :, :, :, TC - 1], bc[:, 0:2], bc[:, 1::-1], k_re, k_im)]
        steps += [(CL[:, :, :, d + 1], CL[:, :, :, d], CL[:, ::-1, :, d], one, two) for d in range(TC)]
        for n, (dst, src, swapped, re, im) in enumerate(steps):
            nc.gpsimd.tensor_tensor(dst, src, re, ALU.mult).then_inc(cl_step, 1)
            nc.gpsimd.tensor_tensor(t5p[:], swapped, im, ALU.mult).then_inc(cl_step, 1)
            pool.wait_ge(cl_step, 3 * n + 2)
            nc.gpsimd.tensor_tensor(dst, dst, t5p[:], ALU.add).then_inc(cl_step, 1)
            pool.wait_ge(cl_step, 3 * n + 3)
        nc.gpsimd.memset(Bz[:], 0.0).then_inc(init, 1)
        pool.wait_ge(kt_done, 4)
        nc.gpsimd.memset(Mt[:], 0.0).then_inc(init, 1)
        pool.wait_ge(rot_ready, 1)
        for b in range(2):
            pool.dma_start(adaw[:, b], ada_w[16 + b]).then_inc(ada_in[b], 16)
        with pool.Fori(1, 40) as i:
            for b in range(2):
                pool.wait_ge(ada_used, i * 2 + (b + 15))
                pool.dma_start(adaw[:, b], row(ada_w.rearrange("n p k -> p n k"), i * 2 + (b + 16))).then_inc(ada_in[b], 16)
        pool.wait_ge(ada_used, 96)
        pool.dma_start(ropt[64:P, :], rope).then_inc(in_rope, 16)


    @block.tensor
    def _(pe):
        def three(bank, hi_w, lo_w, hi_x, lo_x, start, stop):
            pe.matmul(bank, lo_w, hi_x, start=start, stop=False)
            pe.matmul(bank, hi_w, lo_x, start=False, stop=False)
            return pe.matmul(bank, hi_w, hi_x, start=False, stop=stop)

        def chunk_ready(j, b):
            pe.wait_ge(split_lo, j * 2 + (b + 1))
            pe.wait_ge(evac[b], done_value(j, -1))

        def product(name, j, b, x_hi, x_lo, x_ready=None):
            chunk_ready(j, b)
            kt, cols = KT[name], COLS[name]
            for k in range(kt):
                if x_ready:
                    pe.wait_ge(x_ready[0], x_ready[1] + k + 1)
                for r in range(cols // P):
                    w = slice(k * cols + r * P, k * cols + (r + 1) * P)
                    mm = three(ps[:, 2 * b + r], w_hi[:, b, w], w_lo[:, b, w], x_hi[:, k], x_lo[:, k], k == 0, k == kt - 1)
                    if k == kt - 1:
                        mm.then_inc(done[b], 2 * P // cols)

        def product_rows(name, j, b, x_hi, x_lo):
            chunk_ready(j, b)
            kt = KT[name]
            for t in range(QBLK):
                for k in range(kt):
                    x = slice(t * P, (t + 1) * P)
                    w = slice(k * 256, (k + 1) * 256)
                    mm = three(ps[:, 2 * b + t // 2, (t % 2) * 256:(t % 2 + 1) * 256], x_hi[:, k, x], x_lo[:, k, x],
                               w_hi[:, b, w], w_lo[:, b, w], k == 0, k == kt - 1)
                if t % 2:
                    mm.then_inc(done[b], 1)

        def layer(name, x_hi, x_lo, x_ready=None, rows=False):
            for i in range(COUNT[name]):
                n = FIRST[name] + i
                if rows:
                    product_rows(name, n // 2, n % 2, x_hi, x_lo)
                else:
                    product(name, n // 2, n % 2, x_hi, x_lo, x_ready if i == 0 else None)

        def layer_loop(name, x_hi, x_lo, x_ready=None):
            with pe.Fori(0, COUNT[name] // 2) as i:
                for b in range(2):
                    product(name, i + FIRST[name] // 2, b, x_hi, x_lo, None if b else x_ready)

        def norm_stat(name, summed=False):
            if not summed:
                pe.wait_ge(ssq_ready, SSQ[name] + dict(NORMS)[name])
                pe.wait_ge(norm_t, NTILE[name])
                for t in range(QBLK):
                    mm = pe.matmul(ps[:, 7, t:t + 1], ssq[:, t * P:(t + 1) * P], ones[:, 0:1], start=True, stop=True)
                if name in SECOND:
                    before, count = SECOND[name]
                    pe.wait_ge(ssq2_ready, before + count + (2 if before else 1))
                    for t in range(QBLK):
                        mm = pe.matmul(ps[:, 7, 4 + t:5 + t], ssq2[:, t * P:(t + 1) * P], ones[:, 0:1], start=True, stop=True)
                mm.then_inc(stat_done, 1)
            pe.wait_ge(rstd_ready, NIDX[name] + 1)
            for t in range(QBLK):
                mm = pe.matmul(ps[:, 7, t * P:(t + 1) * P], rcol[:, t:t + 1].to_broadcast([P, P]), ident[:], start=True, stop=True)
            if name in SECOND:
                for t in range(QBLK):
                    mm = pe.matmul(ps[:, 6, t * P:(t + 1) * P], rcol[:, 4 + t:5 + t].to_broadcast([P, P]), ident[:], start=True, stop=True)
            mm.then_inc(rstd_out, 1)

        def attention(kind, heads, q, k, v, rows, diag_mask):
            n = 4 * heads
            pe.wait_ge(cst_ready, 1)
            S_BANK, T_BANK, O_BANK = (4, 5, 6, 7), (0, 3), (1, 2)

            def scores(u):
                g, hd, i = UNIT[kind] + u, u // 4, u % 4
                if g >= 4:
                    pe.wait_ge(s_free, g - 3)
                bank = ps[:, S_BANK[g % 4]]
                pe.matmul(bank[:, 0:(i + 1) * P], q(hd)[:, i * P:(i + 1) * P], k(hd)[:, 0:(i + 1) * P], start=True, stop=False)
                pe.matmul(bank[:, i * P:(i + 1) * P], cst16[:, 0], cst16[:, diag_mask], start=False, stop=True).then_inc(s_done, 1)

            def turn(u):
                g, i = UNIT[kind] + u, u % 4
                pe.wait_ge(w_ready, g + 1)
                if g >= 2:
                    pe.wait_ge(pt_done, g - 1)
                for t in range(i + 1):
                    mm = pe.transpose(ps[:, T_BANK[g % 2], t * P:(t + 1) * P], pw[:, g % 4, t * P:(t + 1) * P], ident[:])
                mm.then_inc(tr_done, 1)

            def weigh(u):
                g, hd, i = UNIT[kind] + u, u // 4, u % 4
                pe.wait_ge(pt_done, g + 1)
                if u % 8 == 0 and g // 8 >= 2:
                    pe.wait_ge(o_done, g // 8 - 1)
                half = hd % 2 * 64
                for t in range(i + 1):
                    mm = pe.matmul(ps[half:half + 64, O_BANK[g // 8 % 2], i * P:(i + 1) * P], v[:, t, hd * 64:(hd + 1) * 64],
                                   pt[:, g % 2, t * P:(t + 1) * P], start=t == 0, stop=t == i)
                mm.then_inc(pv_done, 1)

            lag = LAG[kind]
            for s in range(n + 5 + lag):
                if s < n:
                    scores(s)
                if 3 + lag <= s < n + 3 + lag:
                    turn(s - 3 - lag)
                if s >= 5 + lag:
                    weigh(s - 5 - lag)

        for b in range(2):
            nc.tensor.sem_inc(done[b], CREDIT)
        pe.wait_ge(in_const, 64)
        pe.wait_ge(init, 1)
        for m in range(DT):
            pe.wait_ge(sq_ready, m + 1)
            for t in range(QBLK):
                mm = pe.matmul(ps[:, 7, t:t + 1], sq[:, m % 2, t * P:(t + 1) * P], ones[:, 0:1], start=m == t == 0,
                               stop=m == DT - 1 and t == QBLK - 1, skip_group_check=True)
            mm.then_inc(ssq_ready, 1)
        norm_stat("mix0", summed=True)
        for i in range(2):
            product("s5_in", i // 2, i % 2, xn_hi, xn_lo, None if i else (xl, XTILE["mix0"]))
        pe.wait_ge(bw_ready, 1)
        for n in range(16):
            q, ri = n // 2, n % 2
            if n >= 3:
                pe.wait_ge(turned_out, n - 2)
            for g in range(4):
                mm = pe.transpose(ps[0:64, 4 + n % 3, g * P:(g + 1) * P], BW[:, ri, 4 * q + g].rearrange("p c j -> p (c j)"), ident[:])
            mm.then_inc(turned, 1)
        pe.wait_ge(cl_step, 3 * TC + 3)
        pe.wait_ge(turned_out, 16)
        for q in range(4):
            if q == 3:
                pe.wait_ge(kt_out, 1)
            for g in range(8 * q, 8 * q + 8):
                for ri in range(2):
                    mm = pe.matmul(ps[0:32, 4 + q % 3, (g % 8) * 64:(g % 8 + 1) * 64], Bz[:, ri, g].rearrange("p q c -> p (q c)"),
                                   CL[:, ri, g, 0:TC].rearrange("p d c -> p (d c)"), start=ri == 0, stop=ri == 1)
            mm.then_inc(kt_done, 1)
        for i in range(2, 4):
            product("s5_in", i // 2, i % 2, xn_hi, xn_lo)

        after_layer(pe, "s5_in")
        pe.wait_ge(kt_out, 4)
        pe.wait_ge(mt_in, 128)

        def from_input(q):
            if q >= 2:
                pe.wait_ge(x_used, q - 1)
            if q >= 4:
                pe.wait_ge(y_out, q - 3)
            pe.wait_ge(u_in[q], 16)
            for ri in range(2):
                for g in range(4):
                    for p in (slice(0, 64), slice(64, P)):
                        mm = pe.matmul(ps[p, q % 2 * 2 + ri, g * P:(g + 1) * P], Bm[p, ri, 4 * q + g], U[p, 4 * q + g], start=True, stop=True)
            mm.then_inc(x_done, 1)
            for g in range(4):
                for p in (slice(0, 64), slice(64, P)):
                    pe.matmul(ps[p, 4 + q % 4, g * P:(g + 1) * P], Mt[p, 4 * q + g], U[p, 4 * q + g], start=g == 0, stop=False,
                              skip_group_check=True)

        def from_states(q):
            pe.wait_ge(x_ready, q + 1)
            for g in range(4):
                for p in (slice(0, 64), slice(64, P)):
                    for ri in range(2):
                        mm = pe.matmul(ps[p, 4 + q % 4, g * P + 1:(g + 1) * P], CL[p, ri, 4 * q + g, 1:5].rearrange("p d c -> p (d c)"),
                                       X[p, q % 2, ri, g, 0:NCK - 1], start=False, stop=ri == 1, skip_group_check=True)
            mm.then_inc(y_done, 1)

        for q in range(DT + 2):
            if q < DT:
                from_input(q)
            if q >= 2:
                from_states(q - 2)
        pe.wait_ge(x_used, DT)
        layer("s5_glu", xn_hi, xn_lo, (gl_done, 0))
        layer("s5_out", zg_hi, zg_lo, (gm_lo, 0))

        for l in (0, 1):
            if l:
                norm_stat("mix1")
                layer("fox_q", xn_hi, xn_lo, (xl, XTILE["mix1"]))
                pe.wait_ge(fw_lo, 1)
                for k in range(DT):
                    mm = three(ps[0:HEADS, 6], fwf_hi[:, k], fwf_lo[:, k], xn_hi[:, k], xn_lo[:, k], k == 0, k == DT - 1)
                mm.then_inc(f_done, 1)
                layer("fox_k", xn_hi, xn_lo)
                layer("fox_v", xn_hi, xn_lo, rows=True)
                after_layer(pe, "fox_v")
                pe.wait_ge(f_dve, 1)
                attention("fox", HEADS, lambda hd: fq[hd % 2 * 64:hd % 2 * 64 + 64, hd // 2],
                          lambda hd: fk[hd % 2 * 64:hd % 2 * 64 + 64, hd // 2], fv, 64, 1)
                layer("fox_out", xn_hi, xn_lo, (o_done, 0))
            norm_stat(f"ffn{l}")
            tiles = sum(HALVES) * l
            for hf, nf in enumerate(HALVES):
                layer_loop(f"up{l}{hf}", xn_hi, xn_lo, None if hf else (xl, XTILE[f"ffn{l}"]))
                layer_loop(f"down{l}{hf}", act_hi, act_lo, (actl, tiles))
                tiles += nf

        norm_stat("in2")
        layer("sb_q", xn_hi, xn_lo, (xl, XTILE["in2"]))
        layer("sb_k", xn_hi, xn_lo)
        layer("sb_v", xn_hi, xn_lo, rows=True)
        after_layer(pe, "sb_v")
        attention("sb", H2, lambda hd: b_q[hd % 2 * 64:hd % 2 * 64 + 64, hd // 2],
                  lambda hd: b_k[hd % 2 * 64:hd % 2 * 64 + 64, hd // 2], b_v, 64, 2)
        pe.wait_ge(o_done, 12)
        layer("mla_c", xn_hi, xn_lo)
        norm_stat("cq")
        layer("mla_q", cq_hi, cq_lo, (xl, XTILE["cq"]))
        layer("mla_k", ck_hi, ck_lo, (xl, XTILE["ckv"]))
        layer("mla_v", ck_hi, ck_lo, rows=True)
        after_layer(pe, "mla_v")
        pe.wait_ge(mk_rope, H2)
        attention("mla", H2, lambda hd: m_q[0:QK, hd], lambda hd: m_k[0:QK, hd], m_v, QK, 3)
        pe.wait_ge(o_done, 16)
        layer("gate_sb", xn_hi, xn_lo)
        layer("gate_mla", xn_hi, xn_lo)
        for m in range(4):
            layer(f"g0_{m}", xn_hi, xn_lo)
            layer(f"osb_{m}", osb_hi, osb_lo, (gm_lo, GATED["gate_sb"]) if m == 0 else None)
            layer(f"g1_{m}", xn_hi, xn_lo)
            layer(f"omla_{m}", omla_hi, omla_lo, (gm_lo, GATED["gate_mla"]) if m == 0 else None)
        layer("mix_out", mg_hi, mg_lo, (m_lo, 0))
        norm_stat("out")

    @block.scalar
    def _(act):
        A = nc.scalar.activation

        def split(j, b, words=2048):
            act.wait_ge(raw_in[b], j * 16 + 16)
            act.wait_ge(done[b], done_value(j, -1))
            A(w_hi[:, b, 0:words], raw[:, b, 0:words], ACT.Copy).then_inc(split_hi, 1)

        def split_next(n):
            if n + 1 < N_CHUNKS:
                split((n + 1) // 2, (n + 1) % 2, size(n + 1))

        def layer(name, evacuate):
            for i in range(COUNT[name]):
                n = FIRST[name] + i
                split_next(n)
                evacuate(n // 2, n % 2, i)

        def copy_out(dst, scale=1.0):
            def evacuate(j, b, i):
                for r in range(2):
                    act.wait_ge(done[b], done_value(j, r))
                    A(dst[:, 2 * i + r], ps[:, 2 * b + r], ACT.Copy, scale=scale).then_inc(evac[b], 1)
            return evacuate

        def rows_out(dst):
            def evacuate(j, b, i):
                for r in range(2):
                    act.wait_ge(done[b], done_value(j, r))
                    A(dst[:, 2 * r:2 * r + 2, i * 256:(i + 1) * 256], ps[:, 2 * b + r].rearrange("p (t n) -> p t n", t=2),
                      ACT.Copy).then_inc(evac[b], 1)
            return evacuate

        def square(name, m, r, src):
            act.wait_ge(ssq_ready, m + (SSQ[name] - 1))
            A(sq[:, r], src, ACT.Square).then_inc(sq_ready, 1)

        def square2(before, m, r, src, scale=1.0):
            act.wait_ge(ssq2_ready, m + before)
            A(nt[:, r], src, ACT.Square, scale=scale).then_inc(sq2_ready, 1)

        def residual(squares, tiles=2):
            def evacuate(j, b, i):
                if squares:
                    for r in range(tiles):
                        act.wait_ge(evac[b], done_value(j, r if tiles == 2 else 1))
                        m = i * tiles + r
                        square(squares, m, r if tiles == 2 else b, row(h, m))
                        if squares == "in2":
                            square2(1, m, b, row(h, m), col(par, m + PCOL["final_g"]))
            return evacuate

        def norm(name, dst_hi=None, width=D, shift=None):
            i = NIDX[name]
            act.preload_act_table(ACT.Sqrt)
            if i:
                act.wait_ge(stat_done, i)
            else:
                act.wait_ge(ssq_ready, DT + 1)
            root = A(stdc[:, 0:4], ps[:, 7, 0:4], ACT.Sqrt, bias=epsc[:, 0:1], scale=1.0 / width)
            if name == "cq":
                root = A(stdc[:, 4:8], ps[:, 7, 4:8], ACT.Sqrt, bias=epsc[:, 0:1], scale=1.0 / KVL)
            root.then_inc(std_ready, 1)
            if name == "in2":
                act.wait_ge(var2_ready, 2)
                A(stdc[:, 4:8], stdc[:, 4:8], ACT.Sqrt, bias=epsc[:, 0:1], scale=1.0 / D).then_inc(var2_ready, 1)
            rounded(name, dst_hi, shift)

        def rounded(name, dst_hi, shift=None):
            if dst_hi is not None:
                for m in range(dict(NORMS)[name]):
                    act.wait_ge(norm_t, NTILE[name] + m + 1)
                    if shift is None:
                        A(dst_hi[:, m], norm_buf(m), ACT.Copy).then_inc(xh, 1)
                    else:
                        A(dst_hi[:, m], norm_buf(m), ACT.Identity, bias=mod[:, shift, m:m + 1]).then_inc(xh, 1)

        def gated(name, func, dst_hi):
            base = GATED[name]

            def evacuate(j, b, i):
                for r in range(2):
                    act.wait_ge(done[b], done_value(j, r))
                    A(nt[:, r], ps[:, 2 * b + r], func).then_inc(evac[b], 1)
                for r in range(2):
                    act.wait_ge(gm_prod, base + 2 * i + r + 1)
                    A(dst_hi[:, 2 * i + r], hn[:, r], ACT.Copy).then_inc(gm_hi, 1)
            return evacuate

        def turned_copy(u):
            act.wait_ge(tr_done, u + 1)
            if u >= 2:
                act.wait_ge(pv_done, u - 1)
            w = (u % 4 + 1) * P
            A(pt[:, u % 2, 0:w], ps[:, (0, 3)[u % 2], 0:w], ACT.Copy).then_inc(pt_done, 1)

        def attention(kind, heads, dst, scale=1.0):
            n, base = 4 * heads, UNIT[kind]
            if kind == "sb":
                act.preload_act_table_set("natural_log_exp_and_others")
            else:
                act.preload_act_table(ACT.Exp)

            def weights_of(u):
                g, w = base + u, (u % 4 + 1) * P
                p, st = pw[:, g % 4, 0:w], stat[:, g % 4]
                if kind == "fox":
                    act.wait_ge(s_free, g + 1)
                    A(p, p, ACT.Exp, bias=st[:, 1:2], scale=-1.0, accum_out=st[:, 2:3]).then_inc(exp_done, 1)
                elif kind == "mla":
                    act.wait_ge(nm_done, g - 4 * H2 - 4 * HEADS + 1)
                    act.wait_ge(tr_done, g - 3)
                    A(p, ps[:, 4 + g % 4, 0:w], ACT.Exp, bias=st[:, 1:2], scale=scale, accum_out=st[:, 2:3]).then_inc(s_free, 1)
                else:
                    t = norm_buf(g % 4)[:, 0:w]
                    act.wait_ge(s_done, g + 1)
                    if u >= 4:
                        act.wait_ge(sc_done, u - 3)
                    A(t, ps[:, 4 + g % 4, 0:w], ACT.Abs).then_inc(abs_done, 1)
                    if u >= 3:
                        stick_weights(u - 3)
                    act.wait_ge(abs_done, u + 1)
                    A(t, t, ACT.Exp, scale=-1.0).then_inc(e_done, 1)
                    if u >= 6:
                        turned_copy(g - 6)
                    act.wait_ge(e_done, u + 1)
                    A(t, t, ACT.Ln, bias=1.0).then_inc(ln_done, 1)

            def stick_weights(u):
                g, w = base + u, (u % 4 + 1) * P
                act.wait_ge(s_free, g + 1)
                A(pw[:, g % 4, 0:w], pw[:, g % 4, 0:w], ACT.Exp).then_inc(w_ready, 1)

            lag = LAG[kind]
            for s in range(n + 6 + lag):
                if 4 + lag <= s < n + 4 + lag and not (kind == "sb" and s < n):
                    turned_copy(base + s - 4 - lag)
                if s < n:
                    weights_of(s)
                elif kind == "sb" and s < n + 3:
                    stick_weights(s - 3)
                if s >= 13 + lag and s % 8 == 5 + lag:
                    pair = (s - 13 - lag) // 8
                    act.wait_ge(pv_done, base + 8 * pair + 8)
                    g = base // 8 + pair
                    A(dst[:, pair], ps[:, (1, 2)[g % 2]], ACT.Copy).then_inc(o_hi if kind == "fox" else o_done, 1)

        for b in range(2):
            nc.scalar.sem_inc(evac[b], CREDIT)
        act.wait_ge(in_c, 16)
        A(cvec[:], cvec[:], ACT.Silu).then_inc(c_ready, 1)
        act.wait_ge(in_s5, 32)
        A(q5[:, 0], lam[:, 2], ACT.Exp).then_inc(s5_act, 1)
        act.wait_ge(s5_arg, 1)
        A(q5[:, 5], q5[:, 1], ACT.Exp).then_inc(s5_act, 1)
        A(q5[:, 6], q5[:, 4], ACT.Sin).then_inc(s5_act, 1)
        A(q5[:, 7], q5[:, 4], ACT.Sin, scale=0.5).then_inc(s5_act, 1)
        act.wait_ge(in_x, 16)
        for m in range(DT):
            square("mix0", m, m % 2, h[:, m])
        split(0, 0)
        norm("mix0", xn_hi, shift=0)

        def input_out(j, b, i):
            for r in range(2):
                act.wait_ge(done[b], done_value(j, r))
                A((nt, hn)[i % 2][:, r], ps[:, 2 * b + r].rearrange("p (k j) -> p j k", j=TC), ACT.Copy).then_inc(evac[b], 1)

        for i in range(2):
            split_next(i)
            input_out(0, i, i)
        for n in range(16):
            q, ri = n // 2, n % 2
            act.wait_ge(turned, n + 1)
            v = ps[0:64, 4 + n % 3].rearrange("p (g q s) -> p g q s", g=4, q=2)
            A(Bm[0:64, ri, 4 * q:4 * q + 4], v[:, :, 0], ACT.Copy)
            A(Bm[64:P, ri, 4 * q:4 * q + 4], v[:, :, 1], ACT.Copy).then_inc(turned_out, 1)
        split_next(2)
        for n in range(2):
            act.wait_ge(u_saved[n], 16)
        for q in range(4):
            act.wait_ge(kt_done, q + 1)
            A(Kt[0:32, 8 * q:8 * q + 8].rearrange("p g d c -> p (g d c)"), ps[0:32, 4 + q % 3], ACT.Copy).then_inc(kt_out, 1)
        for i in range(2, 4):
            if i == 3:
                split_next(i)
            act.wait_ge(mt_in, 128)
            input_out(1, i % 2, i)

        def y_tile(m):
            act.wait_ge(y_done, m + 1)
            if m >= 2:
                act.wait_ge(y_saved[m % 2], 32 * (m // 2))
            A(nt[:, m % 2], ps[:, 4 + m % 4], ACT.Copy).then_inc(y_out, 1)

        def gelu_tile(m):
            act.wait_ge(y_in[m], 64)
            A(g32[:, m], yT[:, m], ACT.Gelu_apprx_tanh).then_inc(g_done, 1)
            act.wait_ge(g_done, m + 1)
            A(xn_hi[:, m], g32[:, m], ACT.Copy).then_inc(gh_done, 1)

        for m in range(DT + 2):
            if m < DT:
                y_tile(m)
            if m >= 2:
                gelu_tile(m - 2)
        layer("s5_glu", gated("s5_glu", ACT.Sigmoid, zg_hi))
        layer("s5_out", residual("ffn0"))

        for l in (0, 1):
            if l:
                norm("mix1", xn_hi, shift=2)
                act.wait_ge(in_fw, 16)
                A(fwf_hi[:], fwf[:], ACT.Copy).then_inc(fw_hi, 1)
                layer("fox_q", copy_out(fq, HD ** -0.5))
                act.wait_ge(f_dve, 1)
                A(fg[:, 1], fg[:, 0], ACT.Abs).then_inc(f_act, 1)
                act.wait_ge(f_act, 1)
                A(fg[:, 1], fg[:, 1], ACT.Exp, scale=-1.0).then_inc(f_act, 1)
                act.wait_ge(f_act, 2)
                A(fg[:, 2], fg[:, 1], ACT.Ln, bias=1.0).then_inc(f_act, 1)
                layer("fox_k", copy_out(fk))
                layer("fox_v", rows_out(fv))
                attention("fox", HEADS, xn_hi)
                layer("fox_out", residual("ffn1"))
            norm(f"ffn{l}", xn_hi, shift=2 * l + 1)
            tiles = sum(HALVES) * l
            for hf, nf in enumerate(HALVES):
                act.preload_act_table(ACT.Silu)
                with act.Fori(0, nf // 2) as i:
                    j = i + FIRST[f"up{l}{hf}"] // 2
                    f = i * 2 + tiles
                    split(j, 1)
                    for r in range(2):
                        act.wait_ge(done[0], done_value(j, r))
                        A(apad[r][:, 2:S + 2], ps[:, r], ACT.Copy).then_inc(evac[0], 1)
                    split(j + 1, 0)
                    for r in range(2):
                        act.wait_ge(conv_done, f + r + 1)
                        A(sil[:, r], cv[:, r], ACT.Silu).then_inc(silu_done, 1)
                    for r in range(2):
                        act.wait_ge(evac[1], done_value(j, r))
                        A(row(act_hi, i * 2 + r), prod[:, r], ACT.Copy).then_inc(acth, 1)
                tiles += nf
                squares = (f"mix1" if l == 0 else "in2") if hf == 1 else None
                with act.Fori(0, DT // 2) as i:
                    for b in range(2):
                        j = i + FIRST[f"down{l}{hf}"] // 2
                        split(j + b, 1 - b)
                        residual(squares, 1)(j, b, i * 2 + b)

        norm("in2", xn_hi)
        layer("sb_q", copy_out(b_q, HD ** -0.5))
        layer("sb_k", copy_out(b_k))
        layer("sb_v", rows_out(b_v))
        attention("sb", H2, o_sb)

        def compressed_out(j, b, i):
            for r in range(2):
                if 2 * i + r < 5:
                    act.wait_ge(done[b], done_value(j, r))
                    A(cc[:, 2 * i + r], ps[:, 2 * b + r], ACT.Copy).then_inc(evac[b], 1)

        def query_out(j, b, i):
            for r in range(2):
                act.wait_ge(done[b], done_value(j, r))
                A(m_q[0:64, 2 * i + r], ps[0:64, 2 * b + r], ACT.Copy).then_inc(mq_nope, 1)

        def key_out(j, b, i):
            for r in range(2):
                act.wait_ge(done[b], done_value(j, r))
                for p in range(2):
                    ins = A(m_k[0:64, 2 * (2 * i + r) + p], ps[64 * p:64 * p + 64, 2 * b + r], ACT.Copy)
                ins.then_inc(evac[b], 1)

        layer("mla_c", compressed_out)
        after_layer(act, "mla_c")
        for m in range(3):
            square("cq", m, m % 2, cc[:, m])
        for m in range(2):
            square2(DT + 2, m, m % 2, cc[:, 3 + m])
        norm("cq", cq_hi, QL)
        rounded("ckv", ck_hi)
        layer("mla_q", query_out)
        layer("mla_k", key_out)
        layer("mla_v", rows_out(m_v))
        attention("mla", H2, o_mla, QK ** -0.5)
        layer("gate_sb", gated("gate_sb", ACT.Silu, osb_hi))
        layer("gate_mla", gated("gate_mla", ACT.Silu, omla_hi))
        for m in range(4):
            for branch, tmp in (("0", nt), ("1", hn)):
                def gate_out(j, b, i):
                    for r in range(2):
                        act.wait_ge(done[b], done_value(j, r))
                        A(tmp[:, r], ps[:, 2 * b + r], ACT.Sigmoid,
                          bias=pcol("b_gate", int(branch) * DT + 2 * m + r)).then_inc(evac[b], 1)
                layer(f"g{branch}_{m}", gate_out)
                layer(f"o{'sb' if branch == '0' else 'mla'}_{m}", lambda j, b, i: None)
            for r in range(2):
                act.wait_ge(m_sum, 2 * m + r + 1)
                A(mg_hi[:, 2 * m + r], sq[:, r], ACT.Copy).then_inc(m_hi, 1)
        layer("mix_out", residual("out"))
        norm("out")

    @block.vector
    def _(dve):
        V = nc.vector
        modf = mod[:].rearrange("p a t -> p (a t)")

        def split(j, b, words=2048):
            dve.wait_ge(split_hi, j * 2 + (b + 1))
            dve.wait_ge(done[b], done_value(j, -1))
            V.tensor_tensor(w_lo[:, b, 0:words], raw[:, b, 0:words], f32(w_hi[:, b, 0:words]), ALU.subtract).then_inc(split_lo, 1)

        def layer(name, evacuate=None):
            for i in range(COUNT[name]):
                n = FIRST[name] + i
                if n + 1 < N_CHUNKS:
                    split((n + 1) // 2, (n + 1) % 2, size(n + 1))
                if evacuate:
                    evacuate(n // 2, n % 2, i)

        def ada(first, count):
            for q in range(first, first + count):
                if q < 16:
                    dve.wait_ge(ada0_in[q // 2], 16)
                    w = ada0[q // 2][:, q % 2]
                else:
                    dve.wait_ge(ada_in[q % 2], 16 * (q // 2 - 7))
                    w = adaw[:, q % 2]
                V.tensor_tensor_reduce(w, w, cvec[:], 1.0, 0.0, ALU.mult, ALU.add, modf[:, q:q + 1]).then_inc(ada_used, 1)

        def ada_loop(q, b):
            dve.wait_ge(ada_in[b], q * 8 - 112)
            V.tensor_tensor_reduce(adaw[:, b], adaw[:, b], cvec[:], 1.0, 0.0, ALU.mult, ALU.add, adat[:, b:b + 1]).then_inc(ada_used, 1)
            dve.wait_ge(ada_used, q + (b + 1))
            V.tensor_copy(col(modf, q + b), adat[:, b:b + 1]).then_inc(mod_copy, 1)

        mod_steps = [0]

        def shift_and_scale(a):
            dve.wait_ge(ada_used, 24 * a + 16)
            V.tensor_tensor(mod[:, a, 0:16], mod[:, a, 0:16], par[:, PCOL["ada_b"] + 24 * a:PCOL["ada_b"] + 24 * a + 16], ALU.add).then_inc(mod_step, 1)
            dve.wait_ge(mod_step, mod_steps[0] + 1)
            g = par[:, PCOL["norm_g"] + DT * a:PCOL["norm_g"] + DT * a + DT]
            V.scalar_tensor_tensor(gain[:, a], mod[:, a, DT:2 * DT], 1.0, g, ALU.add, ALU.mult).then_inc(mod_step, 1)
            mod_steps[0] += 2
            dve.wait_ge(mod_step, mod_steps[0])

        def gates(a):
            dve.wait_ge(ada_used, 24 * a + 24)
            V.tensor_tensor(mod[:, a, 16:24], mod[:, a, 16:24], par[:, PCOL["ada_b"] + 24 * a + 16:PCOL["ada_b"] + 24 * a + 24], ALU.add).then_inc(mod_step, 1)
            mod_steps[0] += 1
            dve.wait_ge(mod_step, mod_steps[0])

        def modulation(a):
            shift_and_scale(a)
            gates(a)

        def add_square(name, m, r):
            dve.wait_ge(sq_ready, m + (SQ[name] + 1))
            dve.wait_ge(ssq_ready, m + SSQ[name])
            V.tensor_tensor(ssq[:], ssq[:], sq[:, r], ALU.add).then_inc(ssq_ready, 1)

        def residual(gate, squares, tiles=2, permuted=False):
            def evacuate(j, b, i):
                for r in range(tiles):
                    m = i * tiles + r
                    dve.wait_ge(done[b], done_value(j, r if tiles == 2 else 1))
                    src, dst = ps[:, 2 * b + r], row(h, m)
                    if permuted:
                        src, dst = src.rearrange("p (j k) -> p k j", j=TC), dst.rearrange("p (k j) -> p k j", j=TC)
                    if gate is None:
                        ins = V.tensor_tensor(dst, src, dst, ALU.add)
                    else:
                        ins = V.scalar_tensor_tensor(dst, src, col(mod[:, gate], m + 2 * DT), dst, ALU.mult, ALU.add)
                    ins.then_inc(evac[b], 2 // tiles)
                if squares:
                    for r in range(tiles):
                        add_square(squares, i * tiles + r, r if tiles == 2 else b)
                        if squares == "in2":
                            add_square2(0, i * tiles + r, b)
            return evacuate

        def add_square2(before, m, r):
            dve.wait_ge(sq2_ready, m + (before + 1))
            dve.wait_ge(ssq2_ready, m + (before + (2 if before else 1)))
            V.tensor_tensor(ssq2[:], ssq2[:], nt[:, r], ALU.add).then_inc(ssq2_ready, 1)

        def norm_stat(name):
            i = NIDX[name]
            dve.wait_ge(std_ready, i + 1)
            if name == "in2":
                V.reciprocal(rcol[:, 0:4], stdc[:, 0:4]).then_inc(rc2, 1)
                dve.wait_ge(rc2, 1)
                V.tensor_tensor(stdc[:, 4:8], rcol[:, 0:4], rcol[:, 0:4], ALU.mult).then_inc(var2_ready, 1)
                dve.wait_ge(var2_ready, 1)
                V.tensor_tensor(stdc[:, 4:8], stdc[:, 4:8], ps[:, 7, 4:8], ALU.mult).then_inc(var2_ready, 1)
                dve.wait_ge(var2_ready, 3)
                V.reciprocal(rcol[:, 4:8], stdc[:, 4:8]).then_inc(rc2, 1)
                dve.wait_ge(rc2, 2)
                V.tensor_tensor(rcol[:, 4:8], rcol[:, 4:8], rcol[:, 0:4], ALU.mult).then_inc(rstd_ready, 1)
            else:
                n = 8 if name == "cq" else 4
                V.reciprocal(rcol[:, 0:n], stdc[:, 0:n]).then_inc(rstd_ready, 1)
            if name == "in2":
                V.memset(ssq2[:], 0.0).then_inc(ssq2_ready, 1)
            if name != "out":
                V.memset(ssq[:], 0.0).then_inc(ssq_ready, 1)
            dve.wait_ge(rstd_out, i + 1)

        def norm_tiles(name, src, scale, shift=None, hi=None, lo=None, dst=None, bank=7):
            n, x0 = dict(NORMS)[name], XTILE[name]

            def low(m):
                dve.wait_ge(xh, x0 + m + 1)
                if shift:
                    V.scalar_tensor_tensor(lo[:, m], norm_buf(m), shift(m), f32(hi[:, m]), ALU.add, ALU.subtract).then_inc(xl, 1)
                else:
                    V.tensor_tensor(lo[:, m], norm_buf(m), f32(hi[:, m]), ALU.subtract).then_inc(xl, 1)

            if x0:
                dve.wait_ge(xl, x0)
            for m in range(n):
                to = norm_buf(m) if hi is not None else dst(m)
                V.scalar_tensor_tensor(to, src(m), scale(m), ps[:, bank], ALU.mult, ALU.mult).then_inc(norm_t, 1)
                if hi is not None and m:
                    low(m - 1)
            if hi is not None:
                low(n - 1)

        def norm(name, *args, **kwargs):
            norm_stat(name)
            norm_tiles(name, *args, **kwargs)

        def ada_norm(name, a):
            norm(name, lambda m: h[:, m], lambda m: gain[:, a, m:m + 1], lambda m: mod[:, a, m:m + 1], xn_hi, xn_lo)

        def gated(name, src, dst_hi, dst_lo):
            base = GATED[name]

            def evacuate(j, b, i):
                if base + i:
                    dve.wait_ge(gm_lo, base + 2 * i)
                for r in range(2):
                    dve.wait_ge(evac[b], done_value(j, r))
                    V.tensor_tensor(hn[:, r], src[:, 2 * i + r], nt[:, r], ALU.mult).then_inc(gm_prod, 1)
                for r in range(2):
                    dve.wait_ge(gm_hi, base + 2 * i + r + 1)
                    V.tensor_tensor(dst_lo[:, 2 * i + r], hn[:, r], f32(dst_hi[:, 2 * i + r]), ALU.subtract).then_inc(gm_lo, 1)
            return evacuate

        def attention(kind, heads, scale=1.0):
            n, base = 4 * heads, UNIT[kind]

            def first(u):
                g, hd, i = base + u, u // 4, u % 4
                w = (i + 1) * P
                z, p, st = ps[:, 4 + g % 4, 0:w], pw[:, g % 4, 0:w], stat[:, g % 4]
                if kind == "fox":
                    dve.wait_ge(s_done, g + 1)
                    if i == 0:
                        dve.wait_ge(bias_in[hd % 2], 16 * (hd // 2 + 1))
                    if g >= 4:
                        dve.wait_ge(tr_done, g - 3)
                    V.tensor_tensor_reduce(p, z, fbias[:, hd % 2, 0:w], -1.0, 3e38, ALU.add, ALU.min, st[:, 1:2]).then_inc(s_free, 1)
                elif kind == "mla":
                    dve.wait_ge(s_done, g + 1)
                    V.tensor_reduce(st[:, 0:1], z, AX.X, ALU.max).then_inc(mx_done, 1)
                    dve.wait_ge(mx_done, u + 1)
                    V.tensor_scalar(st[:, 1:2], st[:, 0:1], -scale, None, ALU.mult).then_inc(nm_done, 1)
                else:
                    t = norm_buf(g % 4)[:, 0:w]
                    dve.wait_ge(ln_done, u + 1)
                    V.scalar_tensor_tensor(t, z, 0.0, t, ALU.max, ALU.add).then_inc(sp_done, 1)
                    dve.wait_ge(sp_done, u + 1)
                    dve.wait_ge(tr_done, g - 3)
                    V.tensor_tensor_scan(p[:, ::-1], ones[:, 0:1].to_broadcast([P, w]), t[:, ::-1], 0.0, ALU.mult, ALU.add).then_inc(sc_done, 1)
                    dve.wait_ge(sc_done, u + 1)
                    V.tensor_tensor(p, z, p, ALU.subtract).then_inc(s_free, 1)

            def normalise(u):
                g, w = base + u, (u % 4 + 1) * P
                p, st = pw[:, g % 4, 0:w], stat[:, g % 4]
                if kind == "fox":
                    dve.wait_ge(exp_done, u + 1)
                else:
                    dve.wait_ge(s_free, g + 1)
                k = u + (4 * HEADS if kind == "mla" else 0)
                V.reciprocal(st[:, 3:4], st[:, 2:3]).then_inc(rc_done, 1)
                dve.wait_ge(rc_done, k + 1)
                V.tensor_scalar(p, p, st[:, 3:4], None, ALU.mult).then_inc(w_ready, 1)

            for s in range(n + 6):
                if kind == "sb":
                    if s < n:
                        first(s)
                else:
                    if 2 <= s < n + 2:
                        normalise(s - 2)
                    if s < n:
                        first(s)
                if kind == "fox" and s >= 13 and s % 8 == 5:
                    pair = (s - 13) // 8
                    dve.wait_ge(o_hi, pair + 1)
                    V.tensor_tensor(xn_lo[:, pair], ps[:, (1, 2)[pair % 2]], f32(xn_hi[:, pair]), ALU.subtract).then_inc(o_done, 1)

        V.memset(ones[:], 1.0).then_inc(init, 1)
        V.memset(epsc[:], EPS).then_inc(init, 1)
        V.memset(ssq[:], 0.0).then_inc(ssq_ready, 1)
        V.memset(ssq2[:], 0.0).then_inc(ssq2_ready, 1)

        steps = [0]

        def link(ins):
            steps[0] += 1
            ins.then_inc(s5_step, 1)
            dve.wait_ge(s5_step, steps[0])

        lre, lim = lam[:, 0], lam[:, 1]
        q = lambda i: q5[:, i]
        TT, TS, STT = V.tensor_tensor, V.tensor_scalar, V.scalar_tensor_tensor
        TWO_PI = 2 * np.pi
        c1 = 6.28125
        c2 = float(np.float32(np.floor((TWO_PI - c1) * 2 ** 21) / 2 ** 21))
        c3 = float(TWO_PI - c1 - c2)
        MAGIC = float(1.5 * 2 ** 23)
        dve.wait_ge(in_s5, 32)
        dve.wait_ge(s5_act, 1)
        link(TT(q(1), lre, q(0), ALU.mult))
        link(TT(q(2), lim, q(0), ALU.mult))
        link(TS(q(3), q(2), 1 / TWO_PI, MAGIC, ALU.mult, ALU.add))
        link(TS(q(3), q(3), -MAGIC, None, ALU.add))
        link(STT(q(4), q(3), -c1, q(2), ALU.mult, ALU.add))
        link(STT(q(4), q(3), -c2, q(4), ALU.mult, ALU.add))
        link(STT(q(4), q(3), -c3, q(4), ALU.mult, ALU.add))
        PI_IN = float(np.nextafter(np.float32(np.pi), np.float32(0)))
        TS(q(4), q(4), PI_IN, -PI_IN, ALU.min, ALU.max).then_inc(s5_arg, 1)
        dve.wait_ge(s5_act, 4)
        link(TT(q(8), q(7), q(7), ALU.mult))
        link(TS(q(8), q(8), -2.0, 1.0, ALU.mult, ALU.add))
        link(TT(q(9), q(5), q(8), ALU.mult))
        link(TT(q(10), q(5), q(6), ALU.mult))
        link(TS(q(11), q(9), -1.0, None, ALU.add))
        link(TT(q(16), lre, lre, ALU.mult))
        link(TT(q(17), lim, lim, ALU.mult))
        link(TT(q(12), q(16), q(17), ALU.add))
        link(V.reciprocal(q(13), q(12)))
        link(TT(q(16), q(11), lre, ALU.mult))
        link(TT(q(17), q(10), lim, ALU.mult))
        link(TT(q(16), q(16), q(17), ALU.add))
        link(TT(q(14), q(16), q(13), ALU.mult))
        link(TT(q(16), q(10), lre, ALU.mult))
        link(TT(q(17), q(11), lim, ALU.mult))
        link(TT(q(16), q(16), q(17), ALU.subtract))
        link(TT(q(25), q(16), q(13), ALU.mult))
        link(TS(q(24), q(25), -1.0, None, ALU.mult))
        link(TS(q(20), q(10), -1.0, None, ALU.mult))
        link(V.tensor_copy(q(21), q(10)))
        link(V.tensor_copy(q(22), q(20)))
        wide = [P, 2, GP, CG]
        one = lambda i: q5[:, i].unsqueeze(1).unsqueeze(3).to_broadcast(wide)
        two = lambda i: q5[:, i:i + 2].unsqueeze(3).to_broadcast(wide)

        def complex_times(dst, src, swapped, re, im):
            link(TT(dst, src, re, ALU.mult))
            link(TT(t5[:], swapped, im, ALU.mult))
            link(TT(dst, dst, t5[:], ALU.add))

        link(V.tensor_copy(CL[:, 0, :, 0], bc[:, 2]))
        link(TS(CL[:, 1, :, 0], bc[:, 3], -1.0, None, ALU.mult))
        link(TT(q(16), q(5), q(5), ALU.mult))
        link(TT(coef[:], q(16), q(16), ALU.mult))
        V.sem_inc(cl_start, 1)
        dve.wait_ge(c_ready, 1)
        ada(0, 16)
        dve.wait_ge(in_const, 64)
        V.tensor_copy(cst16[:], cst[:]).then_inc(cst_ready, 1)
        shift_and_scale(0)
        split(0, 0)
        ada_norm("mix0", 0)
        dve.wait_ge(cl_step, 3)
        split(0, 1)
        for j in range(TC - 2, -1, -1):
            complex_times(BW[:, :, :, :, j], BW[:, :, :, :, j + 1], BW[:, ::-1, :, :, j + 1], one(9), two(20))
        dve.wait_ge(init, 3)
        link(V.tensor_copy(Bz[0:64, :, :, 0], BW[0:64, :, :, :, TC - 1]))
        V.tensor_copy(Bz[64:P, :, :, 1], BW[64:P, :, :, :, TC - 1]).then_inc(bw_ready, 1)
        split(1, 0)
        c_s, s_s, c_n, s_n = (turn[:, i] for i in range(4))

        def normalised(c, s):
            link(TT(c_n, c, c, ALU.mult))
            link(TT(s_n, s, s, ALU.mult))
            link(TT(c_n, c_n, s_n, ALU.add))
            link(TS(c_n, c_n, -0.5, 1.5, ALU.mult, ALU.add))
            link(TT(c, c, c_n, ALU.mult))
            link(TT(s, s, c_n, ALU.mult))

        link(TT(q(16), q(8), q(8), ALU.mult))
        link(TT(q(17), q(6), q(6), ALU.mult))
        link(TT(c_s, q(16), q(17), ALU.subtract))
        link(STT(s_s, q(6), 2.0, q(8), ALU.mult, ALU.mult))
        link(TT(q(16), c_s, c_s, ALU.mult))
        link(TT(q(17), s_s, s_s, ALU.mult))
        link(STT(s_s, s_s, 2.0, c_s, ALU.mult, ALU.mult))
        link(TT(c_s, q(16), q(17), ALU.subtract))
        normalised(c_s, s_s)
        dve.wait_ge(turned_out, 16)
        V.memset(rot[:, 0, :, 0:1], 1.0)
        V.memset(rot[:, 1, :, 0:1], 0.0)
        V.tensor_copy(rot[:, 0, :, 1], c_s)
        link(V.tensor_copy(rot[:, 1, :, 1], s_s))

        def further(n, first, count):
            src, dst = rot[:, :, :, first:first + count], rot[:, :, :, n + first:n + first + count]
            c_k, s_k = (rot[:, i:i + 1, :, n:n + 1].to_broadcast([P, 2, GP, count]) for i in range(2))
            tmp = rtmp[:, :, :, 0:count]
            TT(dst, src, c_k, ALU.mult)
            link(TT(tmp, src[:, ::-1], s_k, ALU.mult))
            TT(dst[:, 0], dst[:, 0], tmp[:, 0], ALU.subtract)
            link(TT(dst[:, 1], dst[:, 1], tmp[:, 1], ALU.add))

        for n, first, count in ((1, 1, 1), (2, 1, 2), (4, 1, 4), (8, 1, 8), (16, 1, 16), (32, 1, 32), (64, 1, 32), (64, 33, 31)):
            if n == 8:
                normalised(rot[:, 0, :, 8], rot[:, 1, :, 8])
            further(n, first, count)
            if n == 4:
                split(1, 1)
            if n == 16:
                dve.wait_ge(kt_out, 4)
                TT(Kt[0:32, :, 0], Kt[0:32, :, 0], dd[:], ALU.add).then_inc(kt_sum, 1)

        V.sem_inc(rot_ready, 1)

        for m in range(DT):
            b_in = ps[:, m % 2 * 2:m % 2 * 2 + 2].rearrange("p r (g k) -> p r g k", g=4)
            c_k, s_k = (rot[:, i:i + 1, 4 * m:4 * m + 4].to_broadcast([P, 2, 4, NCK]) for i in range(2))
            x = X[:, m % 2]
            if m == 1:
                split(2, 0)
            dve.wait_ge(x_done, m + 1)
            if m:
                dve.wait_ge(x_ready, m)
            TT(t1[:], b_in, c_k, ALU.mult)
            TT(t2[:], b_in[:, ::-1], s_k, ALU.mult).then_inc(x_used, 1)
            dve.wait_ge(x_used, m + 1)
            TT(t1[:, 0], t1[:, 0], t2[:, 0], ALU.add)
            link(TT(t1[:, 1], t1[:, 1], t2[:, 1], ALU.subtract))
            for ri in range(2):
                for g in range(4):
                    ins = V.tensor_tensor_scan(t2[:, ri, g], coef[:, 4 * m + g:4 * m + g + 1].to_broadcast([P, NCK]), t1[:, ri, g],
                                               0.0, ALU.mult, ALU.add)
            link(ins)
            if m >= 2:
                dve.wait_ge(y_done, m - 1)
            TT(t1[:], t2[:], c_k, ALU.mult)
            link(TT(x, t2[:, ::-1], s_k, ALU.mult))
            TT(x[:, 0], t1[:, 0], x[:, 0], ALU.subtract)
            TT(x[:, 1], t1[:, 1], x[:, 1], ALU.add).then_inc(x_ready, 1)
        dve.wait_ge(x_ready, DT)
        for m in range(DT):
            dve.wait_ge(gh_done, m + 1)
            if m >= 4:
                dve.wait_ge(y_done, 7 if m < 6 else 8)
            TT(xn_lo[:, m], g32[:, m], f32(xn_hi[:, m]), ALU.subtract).then_inc(gl_done, 1)
        glu = gated("s5_glu", g32, zg_hi, zg_lo)

        def glu_and_ada(j, b, i):
            ada(16 + 3 * i, 1)
            glu(j, b, i)
            ada(17 + 3 * i, 2)

        layer("s5_glu", glu_and_ada)
        gates(0)
        into_h = residual(0, "ffn0", permuted=True)

        def out_and_ada(j, b, i):
            ada(28 + 3 * i, 1)
            into_h(j, b, i)
            ada(29 + 3 * i, 2)

        layer("s5_out", out_and_ada)
        shift_and_scale(1)

        for l in (0, 1):
            if l:
                ada(24 * 2 + 22, 2)
                dve.wait_ge(mod_copy, 30)
                modulation(2)
                ada_norm("mix1", 2)
                dve.wait_ge(fw_hi, 1)
                TT(fwf_lo[:], fwf[:], f32(fwf_hi[:]), ALU.subtract).then_inc(fw_lo, 1)
                for n, name in enumerate(("fox_q", "fox_k", "fox_v")):
                    layer(name, lambda j, b, i: ada(72 + 8 * n + 2 * i, 2))
                    if n == 0:
                        dve.wait_ge(f_done, 1)
                        TS(fg[:, 0], ps[0:HEADS, 6], pcol("fox_b", 0, slice(0, HEADS)), -1.0, ALU.add, ALU.mult).then_inc(f_dve, 1)
                        dve.wait_ge(f_act, 3)
                        STT(fg[:, 1], fg[:, 0], 0.0, fg[:, 2], ALU.max, ALU.add).then_inc(f_dve, 1)
                        dve.wait_ge(f_dve, 2)
                        V.tensor_tensor_scan(fg[:, 3], ones[0:HEADS, 0:1].to_broadcast([HEADS, S]), fg[:, 1], 0.0, ALU.mult, ALU.add).then_inc(f_dve, 1)
                attention("fox", HEADS)
                layer("fox_out", residual(2, "ffn1"))
                modulation(3)
            ada_norm(f"ffn{l}", 2 * l + 1)
            tiles = sum(HALVES) * l
            for hf, nf in enumerate(HALVES):
                for r in range(2):
                    V.memset(apad[r][:, 0:2], 0.0).then_inc(pad_ready, 1)
                dve.wait_ge(pad_ready, 4 * l + 2 * hf + 2)
                with dve.Fori(0, nf // 2) as i:
                    j = i + FIRST[f"up{l}{hf}"] // 2
                    f = i * 2 + tiles
                    of = i * 2 + (tiles - sum(HALVES) * l)
                    split(j, 1)
                    for r in range(2):
                        tap = lambda t: col(par, of + (conv_par(l, t, r)))
                        dve.wait_ge(evac[0], done_value(j, r))
                        TS(cv[:, r], apad[r][:, 0:S], tap(0), col(par, of + (PCOL["conv_b"] + l * FT + r)), ALU.mult, ALU.add).then_inc(cv_step, 1)
                        dve.wait_ge(cv_step, f * 2 + (2 * r + 1))
                        STT(cv[:, r], apad[r][:, 1:S + 1], tap(1), cv[:, r], ALU.mult, ALU.add).then_inc(cv_step, 1)
                        dve.wait_ge(cv_step, f * 2 + (2 * r + 2))
                        STT(cv[:, r], apad[r][:, 2:S + 2], tap(2), cv[:, r], ALU.mult, ALU.add).then_inc(conv_done, 1)
                    split(j + 1, 0)
                    for r in range(2):
                        dve.wait_ge(silu_done, f + (r + 1))
                        dve.wait_ge(done[1], done_value(j, r))
                        TT(prod[:, r], ps[:, 2 + r], sil[:, r], ALU.mult).then_inc(evac[1], 1)
                    for r in range(2):
                        dve.wait_ge(acth, f + (r + 1))
                        TT(row(act_lo, i * 2 + r), prod[:, r], f32(row(act_hi, i * 2 + r)), ALU.subtract).then_inc(actl, 1)
                    if l == 0:
                        for b in range(2):
                            ada_loop(i * 2 + (60 if hf else 40), b)
                tiles += nf
                squares = (f"mix1" if l == 0 else "in2") if hf == 1 else None
                if l == hf == 0:
                    dve.wait_ge(mod_copy, 12)
                    gates(1)
                with dve.Fori(0, DT // 2) as i:
                    for b in range(2):
                        j = i + FIRST[f"down{l}{hf}"] // 2
                        split(j + b, 1 - b)
                        residual(2 * l + 1, squares, 1)(j, b, i * 2 + b)
                        if l == hf == 0:
                            ada_loop(i * 2 + 52, b)

        norm_stat("in2")
        TT(gain[:, 0], par[:, PCOL["final_g"]:PCOL["final_g"] + DT], par[:, PCOL["norm_in_g"]:PCOL["norm_in_g"] + DT], ALU.mult).then_inc(rc2, 1)
        dve.wait_ge(rc2, 3)
        norm_tiles("in2", lambda m: h[:, m], lambda m: gain[:, 0, m:m + 1], hi=xn_hi, lo=xn_lo, bank=6)
        layer("sb_q")
        norm_tiles("final", lambda m: h[:, m], lambda m: pcol("final_g", m), dst=lambda m: h[:, m])
        layer("sb_k")
        layer("sb_v")
        attention("sb", H2)

        turns = [0]

        def rotate(dst, b, r, inc):
            bank = ps[:, 2 * b + r]
            TT(dst, bank[64:QK], ropt[64:QK], ALU.mult).then_inc(rope_t, 1)
            TT(rt[64:QK], bank[QK:P], ropt[QK:P], ALU.mult).then_inc(evac[b], 1)
            turns[0] += 1
            dve.wait_ge(rope_t, turns[0])
            dve.wait_ge(evac[b], inc)
            return TT(dst, dst, rt[64:QK], ALU.add)

        def shared_key(j, b, i):
            if i == 2:
                dve.wait_ge(in_rope, 16)
                dve.wait_ge(done[b], done_value(j, 1))
                dve.wait_ge(evac[b], done_value(j, 0))
                rotate(kr[64:QK], b, 1, done_value(j, 1)).then_inc(kr_ready, 1)

        layer("mla_c", shared_key)
        for m in range(3):
            add_square("cq", m, m % 2)
        for m in range(2):
            add_square2(DT, m, m % 2)
        norm("cq", lambda m: cc[:, m], lambda m: pcol("q_norm_g", m), hi=cq_hi, lo=cq_lo)
        norm_tiles("ckv", lambda m: cc[:, 3 + m], lambda m: pcol("kv_norm_g", m), hi=ck_hi, lo=ck_lo, bank=6)

        def query_rope(j, b, i):
            for r in range(2):
                dve.wait_ge(mq_nope, 2 * i + r + 1)
                if i + r:
                    dve.wait_ge(mq_ready, 2 * i + r)
                rotate(m_q[64:QK, 2 * i + r], b, r, done_value(j, r)).then_inc(mq_ready, 1)

        layer("mla_q", query_rope)
        after_layer(dve, "mla_q")
        dve.wait_ge(kr_ready, 1)
        for hd in range(H2):
            V.tensor_copy(m_k[64:QK, hd], kr[64:QK, :]).then_inc(mk_rope, 1)
        layer("mla_k")
        layer("mla_v")
        attention("mla", H2, QK ** -0.5)
        layer("gate_sb", gated("gate_sb", o_sb, osb_hi, osb_lo))
        layer("gate_mla", gated("gate_mla", o_mla, omla_hi, omla_lo))
        for m in range(4):
            for name, tmp in (("sb", nt), ("mla", hn)):
                def branch_out(j, b, i):
                    for r in range(2):
                        dve.wait_ge(evac[1 - b], done_value(j if b else j - 1, r))
                        dve.wait_ge(done[b], done_value(j, r))
                        TT(tmp[:, r], ps[:, 2 * b + r], tmp[:, r], ALU.mult).then_inc(evac[b], 1)
                layer(f"g{0 if name == 'sb' else 1}_{m}")
                layer(f"o{name}_{m}", branch_out)
            j, b = last_of(f"omla_{m}")
            dve.wait_ge(evac[b], done_value(j, 1))
            for r in range(2):
                TT(sq[:, r], nt[:, r], hn[:, r], ALU.add).then_inc(m_sum, 1)
            for r in range(2):
                dve.wait_ge(m_hi, 2 * m + r + 1)
                TT(mg_lo[:, 2 * m + r], sq[:, r], f32(mg_hi[:, 2 * m + r]), ALU.subtract).then_inc(m_lo, 1)
        layer("mix_out", residual(None, "out"))
        norm("out", lambda m: h[:, m], lambda m: pcol("norm_f_g", m), dst=lambda m: fin[:, m])


def _chunks(w, name):
    kt, cols, n = KT[name], COLS[name], COUNT[name]
    return np.ascontiguousarray(w.reshape(kt, P, n, cols).transpose(2, 1, 0, 3)).reshape(-1)


def _tiles(v):
    return np.ascontiguousarray(v.reshape(-1, P).T)


def _pairs(a):
    a = a.reshape(GP, 2, ST, *a.shape[2:])
    return np.ascontiguousarray(a.transpose(1, 2, 0, *range(3, a.ndim))).reshape(P, GP, *a.shape[3:])


def _constants():
    i, j = np.arange(P)[:, None], np.arange(P)[None, :]
    m = np.zeros((P, 4, P), np.float32)
    m[:, 0] = i == j
    m[:, 1] = np.where(j <= i, 0, NEG)
    m[:, 2] = np.where(j < i, 0, NEG)
    m[:, 3] = np.where(j // 64 <= i // 64, 0, NEG)
    half = ROPE // 2
    freq = (np.float32(10000.0) ** (-np.arange(half, dtype=np.float32) / np.float32(half))).astype(np.float32)
    ang = (np.arange(S, dtype=np.float32)[:, None] * freq[None, :]).astype(np.float32)
    co, si = np.cos(ang).T.astype(np.float32), np.sin(ang).T.astype(np.float32)
    return m, np.concatenate([co, co, -si, si], 0)


def kernel(**inputs):
    import concourse.bacc as bacc
    from concourse.bass_utils import run_bass_kernel_spmd

    a = {k: np.asarray(v) for k, v in inputs.items()}
    half = ROPE // 2
    swap = np.r_[half:ROPE, 0:half]
    w = {"s5_in": a["s5_w_in"][0], "s5_glu": a["s5_w_glu"][0], "s5_out": a["s5_w_out"][0]}
    fox = a["fox_w_in"][0]
    w.update(fox_q=fox[:, 0:D], fox_k=fox[:, D:2 * D], fox_v=fox[:, 2 * D:3 * D], fox_out=a["fox_w_out"][0])
    F = FT * P
    for l in (0, 1):
        for hf, nf in enumerate(HALVES):
            f0 = sum(HALVES[:hf]) * P
            up = a["ffn_w_up"][l]
            both = np.stack([up[:, f0:f0 + nf * P].reshape(D, nf // 2, 256),
                             up[:, F + f0:F + f0 + nf * P].reshape(D, nf // 2, 256)], 2)
            w[f"up{l}{hf}"] = both.reshape(D, nf * 256)
            w[f"down{l}{hf}"] = a["ffn_w_down"][l][f0:f0 + nf * P]
    wi = a["w_in_2"][0]
    w.update(sb_q=wi[:, 0:512], sb_k=wi[:, 512:1024], sb_v=wi[:, 1024:1536], gate_sb=wi[:, 1536:2048])
    r0 = 2048 + QL + KVL
    rope_cols = wi[:, r0:r0 + ROPE]
    w["mla_c"] = np.concatenate([wi[:, 2048:r0], np.zeros((D, 64), wi.dtype), rope_cols, rope_cols[:, swap]], 1)
    w["gate_mla"] = wi[:, r0 + ROPE:r0 + ROPE + 512]
    gl = wi[:, r0 + ROPE + 512:]
    q = a["w_q_up_2"][0].reshape(QL, H2, QK)
    w["mla_q"] = np.concatenate([q, q[:, :, 64:][:, :, swap]], 2).reshape(QL, H2 * P)
    kv = a["w_kv_up_2"][0].reshape(KVL, H2, P)
    w["mla_k"], w["mla_v"] = kv[:, :, 0:64].reshape(KVL, 512), kv[:, :, 64:].reshape(KVL, 512)
    for m in range(4):
        c = slice(256 * m, 256 * (m + 1))
        w[f"g0_{m}"], w[f"g1_{m}"] = gl[:, c], gl[:, D:][:, c]
        w[f"osb_{m}"], w[f"omla_{m}"] = a["w_o_sb_2"][0][:, c], a["w_o_mla_2"][0][:, c]
    w["mix_out"] = a["w_out_2"][0]
    fox_b = np.zeros((P, 1), np.float32)
    fox_b[0:HEADS, 0] = a["fox_b_f"][0]
    masks, rope = _constants()
    cmat = [_pairs(a[n][0].transpose(0, 2, 1)) for n in ("s5_c_re", "s5_c_im")]
    s5d = np.zeros((2, CG, GP, CG), np.float32)
    for i in range(CG):
        s5d[:, i, :, i] = a["s5_d"].reshape(GP, 2, CG)[:, :, i].T
    s5d = s5d.reshape(2 * CG, GP, CG)
    arrays = {
        "weights": np.concatenate([_chunks(w[name], name) for name, *_ in LAYERS]),
        "ada_w": np.ascontiguousarray(a["ada_w"].reshape(4, D, 24, P).transpose(0, 2, 3, 1)).reshape(96, P, D),
        "xT": np.ascontiguousarray(a["x"][0].T),
        "c": a["c"],
        "params": np.concatenate([_tiles(a[n]) for n in ("norm_g", "ada_b", "final_g", "norm_in_g_2", "b_gate_2",
                                                        "q_norm_g_2", "kv_norm_g_2", "norm_f_g_2", "ffn_conv_w", "ffn_conv_b")] + [fox_b], 1),
        "consts": masks,
        "rope": rope,
        "s5p": np.stack([_pairs(a["s5_lam_re"][0]), _pairs(a["s5_lam_im"][0]),
                         _pairs(np.repeat(a["s5_log_dt"][0][:, None], ST, 1))], 1),
        "s5bc": np.stack([_pairs(a["s5_b_re"][0]), _pairs(a["s5_b_im"][0]), *cmat], 1),
        "s5d": s5d,
        "fox_f": np.ascontiguousarray(fox[:, 3 * D:].reshape(DT, P, HEADS).transpose(1, 0, 2)),
    }
    arrays = {f"in_{k}": np.ascontiguousarray(v) for k, v in arrays.items()}
    nc = bacc.Bacc("TRN2", target_bir_lowering=False, num_devices=1)
    args = [nc.dram_tensor(k, v.shape, mybir.dt.from_np(v.dtype), kind="ExternalInput").ap() for k, v in arrays.items()]
    out = nc.dram_tensor("out_T", (D, S), F32, kind="ExternalOutput").ap()
    build(nc, *args, out)
    r = run_bass_kernel_spmd(nc, [arrays], core_ids=[0])
    return np.ascontiguousarray(r.results[0]["out_T"].T)[None]
```
